# Optimizing a Trainium2 kernel written in Bass

```python
import math
import jax
import jax.numpy as jnp
from jax import lax
import numpy as np

D_MODEL = 2048
BATCH = 1
SEQ = 512
DEPTH = 1
DEC_BATCH = 1
DEC_SEQ = 64
PAST_LEN = 128

CHUNK = 64
SC_WIDTH = 1024
SC_CONV_W = 3
DN_HEADS = 8
DN_DK = 128
DN_DV = 128
DN_CONV_W = 4
DN_QKV = DN_HEADS * (2 * DN_DK + DN_DV)
DN_VW = DN_HEADS * DN_DV
IN_SPLITS = (SC_WIDTH, SC_WIDTH, SC_WIDTH, DN_QKV, DN_VW, DN_HEADS, DN_HEADS, D_MODEL, D_MODEL)
IN_WIDTH = 3 * SC_WIDTH + DN_QKV + DN_VW + 2 * DN_HEADS + 2 * D_MODEL
PEER_HEADS = 8
PEER_NKEYS = 128
PEER_EXPERTS = PEER_NKEYS * PEER_NKEYS
PEER_QDIM = 256
PEER_HALF = PEER_QDIM // 2
PEER_TOPK = 16
PEER_BLOCK = 128
EPS = 1e-6

kernel_name = "hybrid_shortconv_gdn_peer_stream_step"

def rms_norm(x, g):
    xf = x.astype(jnp.float32)
    y = xf * lax.rsqrt(jnp.mean(xf * xf, axis=-1, keepdims=True) + EPS)
    return (y * g.astype(jnp.float32)).astype(x.dtype)

def l2_norm(x):
    return x * lax.rsqrt(jnp.sum(x * x, axis=-1, keepdims=True) + EPS)

def split_cols(a, sizes):
    out, start = [], 0
    for s in sizes:
        out.append(a[..., start:start + s])
        start += s
    return out

def causal_dwconv(x, w, buf):
    width, t = w.shape[0], x.shape[1]
    xp = jnp.concatenate([buf.astype(x.dtype), x], axis=1)
    y = xp[:, 0:t] * w[0]
    for i in range(1, width):
        y = y + xp[:, i:i + t] * w[i]
    return y, xp[:, t:]

def gated_delta_chunked(q, k, v, beta, g, s0, chunk):
    b, t, h, _ = q.shape
    dv = v.shape[-1]
    n = t // chunk

    def blocks(a):
        a = a.reshape((b, n, chunk, h) + a.shape[3:])
        return jnp.moveaxis(a, 3, 1)

    q, k, v, beta, g = (blocks(a) for a in (q, k, v, beta, g))
    gc = jnp.cumsum(g, axis=-1)
    causal = jnp.tril(jnp.ones((chunk, chunk), dtype=bool))
    eye = jnp.eye(chunk, dtype=q.dtype)
    decay = jnp.exp(jnp.where(causal, gc[..., :, None] - gc[..., None, :], -jnp.inf))
    kb = k * beta[..., None]
    lower = jnp.einsum('bhnid,bhnjd->bhnij', kb, k) * decay * (1.0 - eye)
    tmat = lax.linalg.triangular_solve(lower + eye, jnp.broadcast_to(eye, lower.shape),
                                       left_side=True, lower=True, unit_diagonal=True)
    u = jnp.einsum('bhnij,bhnje->bhnie', tmat, v * beta[..., None])
    w = jnp.einsum('bhnij,bhnjd->bhnid', tmat, kb * jnp.exp(gc)[..., None])
    qk = jnp.einsum('bhnid,bhnjd->bhnij', q, k) * decay
    qg = q * jnp.exp(gc)[..., None]
    g_last = gc[..., -1]
    kd = k * jnp.exp(g_last[..., None] - gc)[..., None]

    def step(s, xs):
        qk_i, qg_i, kd_i, u_i, w_i, gl_i = xs
        v_new = u_i - jnp.einsum('bhcd,bhde->bhce', w_i, s)
        o_i = jnp.einsum('bhcd,bhde->bhce', qg_i, s) + jnp.einsum('bhij,bhje->bhie', qk_i, v_new)
        s = s * jnp.exp(gl_i)[..., None, None] + jnp.einsum('bhcd,bhce->bhde', kd_i, v_new)
        return s, o_i

    xs = tuple(jnp.moveaxis(a, 2, 0) for a in (qk, qg, kd, u, w, g_last))
    s_fin, o = lax.scan(step, s0, xs)
    o = jnp.transpose(o, (1, 0, 3, 2, 4)).reshape(b, t, h, dv)
    return o, s_fin

def token_mixers(xn, dn_state, dn_buf, sc_buf, w_in, sc_conv_w, dn_conv_w, a_log, dt_bias,
                 dn_norm_g, w_br_sc, w_br_dn, w_o, chunk):
    b, t, _ = xn.shape
    proj = xn @ w_in
    sc_b, sc_c, sc_h, dn_qkv, dn_z, dn_beta, dn_a, gate_sc, gate_dn = split_cols(proj, IN_SPLITS)
    sc_conv, sc_buf_new = causal_dwconv(sc_c * sc_h, sc_conv_w, sc_buf)
    y_sc = (sc_b * sc_conv) @ w_br_sc
    qkv, dn_buf_new = causal_dwconv(dn_qkv, dn_conv_w, dn_buf)
    qkv = jax.nn.silu(qkv).astype(jnp.float32)
    q, k, v = split_cols(qkv, (DN_HEADS * DN_DK, DN_HEADS * DN_DK, DN_VW))
    q = l2_norm(q.reshape(b, t, DN_HEADS, DN_DK)) * (DN_DK ** -0.5)
    k = l2_norm(k.reshape(b, t, DN_HEADS, DN_DK))
    v = v.reshape(b, t, DN_HEADS, DN_DV)
    beta = jax.nn.sigmoid(dn_beta.astype(jnp.float32))
    g = -jnp.exp(a_log.astype(jnp.float32)) * jax.nn.softplus(dn_a.astype(jnp.float32) + dt_bias.astype(jnp.float32))
    o, s_new = gated_delta_chunked(q, k, v, beta, g, dn_state.astype(jnp.float32), chunk)
    z = dn_z.astype(jnp.float32).reshape(b, t, DN_HEADS, DN_DV)
    o = rms_norm(o, dn_norm_g) * jax.nn.silu(z)
    y_dn = o.reshape(b, t, DN_VW).astype(xn.dtype) @ w_br_dn
    merged = jax.nn.sigmoid(gate_sc) * y_sc + jax.nn.sigmoid(gate_dn) * y_dn
    return merged @ w_o, s_new.astype(dn_state.dtype), dn_buf_new, sc_buf_new

def peer(x, w_q, sub_keys, u_tab, v_tab):
    n = x.shape[0]
    q = (x @ w_q).reshape(n, PEER_HEADS, 2, PEER_HALF)
    s = jnp.einsum('nhpd,hpkd->nhpk', q, sub_keys).astype(jnp.float32)
    top_s, top_i = lax.top_k(s, PEER_TOPK)
    cand_s = (top_s[:, :, 0, :, None] + top_s[:, :, 1, None, :]).reshape(n, PEER_HEADS, PEER_TOPK * PEER_TOPK)
    cand_i = (top_i[:, :, 0, :, None] * PEER_NKEYS + top_i[:, :, 1, None, :]).reshape(n, PEER_HEADS, PEER_TOPK * PEER_TOPK)
    best_s, pos = lax.top_k(cand_s, PEER_TOPK)
    idx = jnp.take_along_axis(cand_i, pos, axis=-1)
    gate = jax.nn.softmax(best_s, axis=-1).astype(x.dtype)
    pad = (-n) % PEER_BLOCK
    nb = (n + pad) // PEER_BLOCK
    xp = jnp.pad(x, ((0, pad), (0, 0))).reshape(nb, PEER_BLOCK, x.shape[1])
    ip = jnp.pad(idx, ((0, pad), (0, 0), (0, 0))).reshape(nb, PEER_BLOCK, PEER_HEADS, PEER_TOPK)
    gp = jnp.pad(gate, ((0, pad), (0, 0), (0, 0))).reshape(nb, PEER_BLOCK, PEER_HEADS, PEER_TOPK)

    def block_fn(args):
        xb, ib, gb = args
        hid = jax.nn.gelu(jnp.einsum('td,thkd->thk', xb, u_tab[ib]), approximate=False)
        return jnp.einsum('thk,thkd->td', hid * gb, v_tab[ib])

    out = lax.map(block_fn, (xp, ip, gp))
    return out.reshape(nb * PEER_BLOCK, x.shape[1])[:n]

def trunk_layer(h, dn_state, dn_buf, sc_buf, norm1_g, w_in, sc_conv_w, dn_conv_w, a_log, dt_bias,
                dn_norm_g, w_br_sc, w_br_dn, w_o, norm2_g, peer_wq, peer_keys, peer_u, peer_v, chunk):
    mix, s_new, dn_buf_new, sc_buf_new = token_mixers(
        rms_norm(h, norm1_g), dn_state, dn_buf, sc_buf, w_in, sc_conv_w, dn_conv_w, a_log, dt_bias,
        dn_norm_g, w_br_sc, w_br_dn, w_o, chunk)
    h = h + mix
    b, t, d = h.shape
    h = h + peer(rms_norm(h, norm2_g).reshape(b * t, d), peer_wq, peer_keys, peer_u, peer_v).reshape(b, t, d)
    return h, s_new, dn_buf_new, sc_buf_new

def setup_inputs(seed: int = 0) -> dict:
    key = jax.random.key(seed)
    ks = jax.random.split(key, 24)
    f32 = jnp.float32
    L = DEPTH

    def nrm(k, shape, scale):
        return jax.random.normal(k, shape, f32) * scale

    dt = jnp.exp(jax.random.uniform(ks[10], (L, DN_HEADS), f32, math.log(1e-3), math.log(1e-1)))
    return {
        "x_prompt": nrm(ks[0], (BATCH, SEQ, D_MODEL), 1.0),
        "x_sample": nrm(ks[1], (DEC_BATCH, DEC_SEQ, D_MODEL), 1.0),
        "state_dn": nrm(ks[2], (L, DEC_BATCH, DN_HEADS, DN_DK, DN_DV), 0.1),
        "state_dn_conv": nrm(ks[3], (L, DEC_BATCH, DN_CONV_W - 1, DN_QKV), 1.0),
        "state_sc_conv": nrm(ks[4], (L, DEC_BATCH, SC_CONV_W - 1, SC_WIDTH), 1.0),
        "norm1_g": 1.0 + nrm(ks[5], (L, D_MODEL), 0.01),
        "w_in": nrm(ks[6], (L, D_MODEL, IN_WIDTH), D_MODEL ** -0.5),
        "sc_conv_w": nrm(ks[7], (L, SC_CONV_W, SC_WIDTH), SC_CONV_W ** -0.5),
        "dn_conv_w": nrm(ks[8], (L, DN_CONV_W, DN_QKV), DN_CONV_W ** -0.5),
        "dn_a_log": jnp.log(jax.random.uniform(ks[9], (L, DN_HEADS), f32, 1.0, 16.0)),
        "dn_dt_bias": dt + jnp.log(-jnp.expm1(-dt)),
        "dn_norm_g": 1.0 + nrm(ks[11], (L, DN_DV), 0.01),
        "w_br_sc": nrm(ks[12], (L, SC_WIDTH, D_MODEL), SC_WIDTH ** -0.5),
        "w_br_dn": nrm(ks[13], (L, DN_VW, D_MODEL), DN_VW ** -0.5),
        "w_o": nrm(ks[14], (L, D_MODEL, D_MODEL), D_MODEL ** -0.5),
        "norm2_g": 1.0 + nrm(ks[15], (L, D_MODEL), 0.01),
        "peer_wq": nrm(ks[16], (L, D_MODEL, PEER_HEADS * PEER_QDIM), D_MODEL ** -0.5),
        "peer_keys": nrm(ks[17], (L, PEER_HEADS, 2, PEER_NKEYS, PEER_HALF), PEER_HALF ** -0.5),
        "peer_u": nrm(ks[18], (L, PEER_EXPERTS, D_MODEL), D_MODEL ** -0.5),
        "peer_v": nrm(ks[19], (L, PEER_EXPERTS, D_MODEL), PEER_HEADS ** -0.5),
        "final_norm_g": 1.0 + nrm(ks[20], (D_MODEL,), 0.01),
    }

def reference(x_prompt, x_sample, state_dn, state_dn_conv, state_sc_conv, norm1_g, w_in, sc_conv_w,
              dn_conv_w, dn_a_log, dn_dt_bias, dn_norm_g, w_br_sc, w_br_dn, w_o, norm2_g, peer_wq,
              peer_keys, peer_u, peer_v, final_norm_g):
    hp, hs = x_prompt, x_sample
    dn_p, dnc_p, scc_p, dn_s, dnc_s, scc_s = [], [], [], [], [], []
    for l in range(DEPTH):
        weights = (norm1_g[l], w_in[l], sc_conv_w[l], dn_conv_w[l], dn_a_log[l], dn_dt_bias[l],
                   dn_norm_g[l], w_br_sc[l], w_br_dn[l], w_o[l], norm2_g[l], peer_wq[l], peer_keys[l],
                   peer_u[l], peer_v[l])
        zero_dn = jnp.zeros((BATCH, DN_HEADS, DN_DK, DN_DV), state_dn.dtype)
        zero_dnc = jnp.zeros((BATCH, DN_CONV_W - 1, DN_QKV), hp.dtype)
        zero_scc = jnp.zeros((BATCH, SC_CONV_W - 1, SC_WIDTH), hp.dtype)
        hp, s1, c1, c2 = trunk_layer(hp, zero_dn, zero_dnc, zero_scc, *weights, CHUNK)
        hs, s3, c3, c4 = trunk_layer(hs, state_dn[l], state_dn_conv[l], state_sc_conv[l], *weights, x_sample.shape[1])
        dn_p.append(s1); dnc_p.append(c1); scc_p.append(c2)
        dn_s.append(s3); dnc_s.append(c3); scc_s.append(c4)
    y_prompt = rms_norm(hp, final_norm_g)
    y_sample = rms_norm(hs, final_norm_g)
    return (y_prompt, y_sample, jnp.stack(dn_p), jnp.stack(dnc_p), jnp.stack(scc_p),
            jnp.stack(dn_s), jnp.stack(dnc_s), jnp.stack(scc_s))


_drawn_inputs = setup_inputs


def setup_inputs(seed=0):
    import zlib

    import numpy as np

    out = dict(_drawn_inputs(seed))
    spreads = {}
    factors = {'norm1_g': 8.677,
     'dn_norm_g': 200.0,
     'norm2_g': 196.8,
     'final_norm_g': 187.546,
     'state_sc_conv': 31.488,
     'state_dn_conv': 2.995}
    for name, (base, spread) in spreads.items():
        noise = np.random.default_rng([zlib.crc32(name.encode()), seed]).standard_normal(out[name].shape)
        drawn = base * np.exp(spread * noise) if base else spread * noise
        out[name] = jnp.asarray(drawn.astype(out[name].dtype))
    for name, factor in factors.items():
        out[name] = (out[name] * factor).astype(out[name].dtype)
    return out
```

```python
import concourse.bass as bass
import numpy as np
from concourse import mybir

F32 = mybir.dt.float32
F32R = mybir.dt.float32r
U32 = mybir.dt.uint32
ALU = mybir.AluOpType
ACT = mybir.ActivationFunctionType
AX_X = mybir.AxisListType.X

D = 2048
TP, TS = 512, 64
T = TP + TS
HT = T // 2
KD = D // 128
C = 64
NCH = T // C
H = 8
HC = H * C
SCW, SC_TAPS = 1024, 3
QKV, DN_TAPS = 3072, 4
NSC, NQKV, NZ = SCW // 128, QKV // 128, 1024 // 128
DK = 128
NK = 128
TOPK = 16
HK = H * TOPK
G2 = 4
NG = NK // G2
TB = 48
NTB = T // TB
EPS = 1e-6
NEG = -1e30
LEVELS = 6
NPIECE = 8

P_A = 0
N_A = NQKV + NZ + 1
P_B = P_A + 2 * N_A
P_C = P_B + 6 * NSC
P_D = P_C + 3 * KD
P_E = P_D + 3 * KD
P_F = P_E + 2 * KD
P_G = P_F + 2 * KD
N_PIECES = P_G + 2 * 2 * G2 * NG

CONST = {}
_at = 0
for _name, _width in (("ones", 128), ("ident", 128), ("iota", 128), ("upper", C), ("negT", C), ("negL", C),
                      ("eye", C), ("levels", LEVELS * C), ("iota16", TOPK)):
    CONST[_name] = (_at, _width)
    _at += _width
N_CONST = _at
VEC = {}
_at = 0
for _name, _width in (("g1", KD), ("g2", KD), ("gf", KD), ("dnw", NQKV * DN_TAPS), ("scw", NSC * SC_TAPS),
                      ("dng", 1), ("alog", H), ("dtb", H), ("dnst", NQKV * (DN_TAPS - 1)),
                      ("scst", NSC * (SC_TAPS - 1))):
    VEC[_name] = (_at, _width)
    _at += _width
N_VEC = _at


def trunk_program(nc, x_in, w_in, vec_in, const_in, s0_in, keys_in, y_out, sp_out, ss_out, dnc_out, scc_out,
                  qkv_d, z_d, o_d, gates_d):
    base = -(-nc.sbuf_base // 64) * 64
    CH = T * 4
    at = {}
    pos = base
    for name, size in (("XH", KD * CH), ("XL", KD * CH), ("MG", KD * CH), ("W", 6 * 4096), ("CV", 4 * N_CONST),
                       ("VV", 4 * N_VEC), ("TAIL", 4 * (NQKV * 6 + NSC * 4)), ("Y", KD * CH)):
        at[name] = pos
        pos += -(-size // 64) * 64
    at["L"] = pos
    end = nc.sbuf_usable_end

    def sb(name, shape, dtype, offset):
        size = int(np.prod(shape[1:])) * 4
        assert offset + size <= end, (name, offset + size, end)
        return nc.alloc_sbuf_tensor_at(name, shape, dtype, offset=offset)

    class Region:
        def __init__(self, offset, limit):
            self.pos, self.limit = offset, limit

        def take(self, name, shape, dtype=F32):
            t = sb(name, shape, dtype, self.pos)
            self.pos += -(-int(np.prod(shape[1:])) * 4 // 32) * 32
            assert self.pos <= self.limit, (name, self.pos, self.limit)
            return t

    xh = sb("xh", [128, KD, T], F32R, at["XH"])
    xl = sb("xl", [128, KD, T], F32R, at["XL"])
    mg = sb("mg", [128, KD, T], F32, at["MG"])
    yh = sb("yh", [128, NSC, T], F32R, at["Y"])
    yl = sb("yl", [128, NSC, T], F32R, at["Y"] + NSC * CH)
    wr = [sb(f"wr{i}", [128, NPIECE, 128], F32, at["W"] + 4096 * i) for i in range(2)]
    wh = [sb(f"wh{i}", [128, NPIECE, 128], F32R, at["W"] + 4096 * (2 + i)) for i in range(2)]
    wl = [sb(f"wl{i}", [128, NPIECE, 128], F32R, at["W"] + 4096 * (4 + i)) for i in range(2)]
    cst = sb("cst", [128, N_CONST], F32, at["CV"])
    vec = sb("vec", [128, N_VEC], F32, at["VV"])
    tail = sb("tail", [128, NQKV, 2, DN_TAPS - 1], F32, at["TAIL"])
    sctail = sb("sctail", [128, NSC, 2, SC_TAPS - 1], F32, at["TAIL"] + 4 * NQKV * 6)

    def const(name, rows=128):
        a, n = CONST[name]
        return cst[0:rows, a:a + n]

    def vector(name, j=None, n=1):
        a, m = VEC[name]
        return vec[:, a:a + m] if j is None else vec[:, bass.ds(a + j, n)]

    r = Region(at["L"], end)
    sq = [r.take(f"sq{i}", [128, T]) for i in range(2)]
    nt = [r.take(f"nt{i}", [128, T]) for i in range(2)]
    ms, rst = r.take("ms", [128, T]), r.take("rst", [128, T])
    r = Region(at["L"], end)
    AW = T + 2 * (DN_TAPS - 1)
    bar = r.take("bar", [128, T])
    cbuf = [r.take(f"cbuf{i}", [128, AW]) for i in range(2)]
    cv = [r.take(f"cv{i}", [128, AW]) for i in range(2)]
    sv = [r.take(f"sv{i}", [128, T]) for i in range(2)]
    r = Region(at["L"] + CH, end)
    lq = [r.take(f"lq{i}", [128, T]) for i in range(2)]
    ln = [r.take(f"ln{i}", [128, T]) for i in range(2)]
    lo_ = [r.take(f"lo{i}", [128, T]) for i in range(2)]
    r = Region(at["L"] + CH, end)
    SW = T + 2 * (SC_TAPS - 1)
    ctmp = r.take("ctmp", [128, T])
    scb = r.take("scb", [128, SW])
    scv = r.take("scv", [128, SW])
    yt = r.take("yt", [128, T])
    small = {n: r.take(n, [64, NCH * H]) for n in ("beta", "gtok", "gcum", "eg", "nbeg", "kdec", "sp1", "sp2")}
    egl = r.take("egl", [128, NCH * H])
    decay = r.take("decay", [64, H])
    xx = r.take("xx", [64, HC])
    yy = r.take("yy", [64, HC])
    lm = r.take("lm", [64, HC])
    pp = r.take("pp", [64, HC])
    oo = r.take("oo", [128, HC])
    m = Region(at["MG"], at["MG"] + KD * CH)
    qkv = m.take("qkv", [128, NQKV, C])
    state = m.take("state", [128, H, 128])
    sdec = m.take("sdec", [128, H, 128])
    vb = m.take("vb", [64, H, 128])
    kd = m.take("kd", [64, H, 128])
    rr = m.take("rr", [64, H, 128])
    el = m.take("el", [64, HC])
    ll = m.take("ll", [64, HC])
    att = m.take("att", [64, HC])
    m = Region(r.pos, end)
    egb = m.take("egb", [128, HC])
    qg = m.take("qg", [128, HC])
    r = Region(at["L"], end)
    sg = [r.take(f"sg{i}", [128, T]) for i in range(2)]
    dt = [r.take(f"dt{i}", [128, T]) for i in range(2)]
    xr = [r.take(f"xr{i}", [128, T]) for i in range(2)]
    mt_ = [r.take(f"mt_{i}", [128, T]) for i in range(2)]
    r = Region(at["L"], end)
    go = [r.take(f"go{i}", [128, T]) for i in range(2)]
    gz = [r.take(f"gz{i}", [128, T]) for i in range(2)]
    gq = [r.take(f"gq{i}", [128, T]) for i in range(2)]
    gr = [r.take(f"gr{i}", [128, T]) for i in range(2)]
    gt_ = [r.take(f"gt_{i}", [128, T]) for i in range(2)]
    qf = sb("qf", [128, KD, T], F32, at["Y"])
    idx_at = (end - 3 * CH) // 64 * 64
    r = Region(idx_at, end)
    idxT = [r.take(n, [128, T]) for n in ("i1T", "i2T", "gateT")]
    r = Region(at["L"], idx_at)
    keys = r.take("keys", [128, KD, NK])
    mrall = sb("mrall", [128, KD, NK], F32, r.pos)
    cand = r.take("cand", [128, 4, TOPK, TOPK])
    sel = r.take("sel", [128, 4, TOPK, TOPK])
    tv = r.take("tv", [128, KD, TOPK])
    ti = r.take("ti", [128, KD, TOPK], U32)
    tif = r.take("tif", [128, KD, TOPK])
    best = r.take("best", [128, H, TOPK])
    posu = r.take("posu", [128, H, TOPK], U32)
    posi = [r.take(f"posi{i}", [128, H, TOPK], U32) for i in range(2)]
    posf = [r.take(f"posf{i}", [128, H, TOPK]) for i in range(2)]
    pick = [r.take(f"pick{i}", [128, H, TOPK]) for i in range(2)]
    gate = r.take("gate", [128, H, TOPK])
    gsum = r.take("gsum", [128, H])
    GB = NK * TB * 4
    r = Region(at["Y"] + 2 * GB, idx_at)
    oa = [r.take(f"oa{i}", [128, 4, NK]) for i in range(2)]
    ob = [r.take(f"ob{i}", [128, 4, NK]) for i in range(2)]
    gbuf = [sb(f"gbuf{i}", [128, NK, TB], F32, at["Y"] + i * GB) for i in range(2)]
    r = Region(at["L"], end)
    gtile = [r.take(f"gtile{i}", [128, NTB, G2, TB]) for i in range(2)]
    gl = [r.take(f"gl{i}", [128, T]) for i in range(2)]
    mm = [r.take(f"mm{i}", [128, T]) for i in range(2)]

    ps = [nc.alloc_psum_tensor(f"ps{i}", [128, 2, 512], F32) for i in range(2)]
    aux = nc.alloc_psum_tensor("aux", [128, 4, 512], F32)
    raw_flat = aux[0:64, 2:4, :].rearrange("p a b -> p (a b)")[:, 0:T]
    raw_tok = raw_flat.rearrange("p (n c) -> p n c", c=C)

    names = """raw_full0 raw_full1 hi_done lo_done piece_used group_done evacuated0 evacuated1
        const_in x_loaded norm_sq norm_sum norm_ms norm_root norm_inv norm_scaled norm_hi norm_lo
        conv_step conv_done silu_done pads_set kept_sv0 kept_sv1
        l2_sq l2_sum l2_ss l2_root l2_inv l2_out kept_qk0 kept_qk1
        tok_ps beta_done sp_in sp_exp sp_one sp_ln sp_max decay_exp g_ready gc_ps gcum_done kdec_in kdec_done eg_done
        nbeg_done chunk_in s_init gu_done gcb_ps kq_ps masked_raw masked exp_done
        att_done l_raw l_done x1_in x1_done xt_ps y1_done qg_done lm_done p_ps p_copied z_ps y_upd x_upd
        v_ps vb_done k_ps kd_done sdec_done ks_ps r_raw r_done vn_ps vn_done o_ps o_copied o_kept
        sup_ps s_done s_kept sc_step sc_hi sc_lo
        half_merged merged go_in0 go_in1 go_sq go_sum go_ss go_root go_inv go_raw go_scaled go_hi go_lo
        mg_hi mg_lo xr_in0 xr_in1 keys_in score_ps topk_step scores_read shifted gate_exp pick_done pickT_ps
        pickT_done onehots gmat_ps gmat_out gates_kept0 gates_kept1
        gt_in0 gt_in1 gelu_read m_done m_hi m_lo tails_kept y_kept0 y_kept1 dve_waited pe_waited""".split()
    S = {n: nc.alloc_semaphore(n) for n in names}

    def halves(t):
        return t.rearrange("p (a b) -> p a b", a=2)

    def both(slot):
        return ps[slot][:, :, 0:HT]

    def heads(t, n=C):
        return t.rearrange("p (h n) -> p h n", n=n)

    def pair(b):
        return aux[0:64, b:b + 2, :].rearrange("p a (h n) -> p (a h) n", n=128)

    def peel(eng, n, body):
        body(0)
        with eng.Fori(1, n) as i:
            body(i)

    EV_B = (N_A // 2 + 1, N_A // 2)
    EV_C = (EV_B[0] + 2 * NSC, EV_B[1] + NSC)
    EV_D = (EV_C[0] + KD, EV_C[1] + KD)
    EV_E = (EV_D[0] + KD, EV_D[1] + KD)
    EV_F = (EV_E[0] + KD // 2, EV_E[1] + KD // 2)
    EV_G = (EV_F[0] + KD // 2, EV_F[1] + KD // 2)
    PER_G = (G2 + KD) // 2
    EV_END = (EV_G[0] + NG * PER_G, EV_G[1] + NG * PER_G)
    HPA, HPB, HPC, HPD, HPE, HPF, HPG = (p // 2 for p in (P_A, P_B, P_C, P_D, P_E, P_F, P_G))
    NP1 = NCH - 1

    block_context = nc.Block()
    block = block_context.__enter__()

    @block.sync
    def _(sp):
        def load(hp, slot):
            if not (isinstance(hp, int) and hp == 0):
                sp.wait_ge(S["lo_done"], 2 * hp + slot - 1)
            sp.dma_start(wr[slot][:, :, :].rearrange("p a n -> p (a n)"), w_in[2 * hp + slot, :, :]
                         ).then_inc(S[f"raw_full{slot}"], 16)

        def loads(hp, n, c0=0):
            for c in range(c0, c0 + n):
                load(hp + 2 + c // 2, c % 2)

        sp.dma_start(cst[:, :], const_in).then_inc(S["const_in"], 16)
        sp.dma_start(vec[:, :], vec_in).then_inc(S["const_in"], 16)
        sp.dma_start(mg[:, :, :], x_in).then_inc(S["x_loaded"], 16)
        for p in range(4):
            load(p // 2, p % 2)

        with sp.Fori(0, H) as i:
            loads(HPA + 2 * i, 4)
        with sp.Fori(0, H // 2) as i:
            for u in range(2):
                loads(HPA + 16 + 2 * i + u, 2)
                sp.wait_ge(S["silu_done"], 17 + 2 * i + u)
                sp.dma_start(qkv_d[:, :, 16 + 2 * i + u, :].rearrange("n p c -> p n c"),
                             sv[u][:, :].rearrange("p (n c) -> p n c", c=C)).then_inc(S[f"kept_sv{u}"], 16)
        with sp.Fori(0, NZ // 2) as i:
            for u in range(2):
                loads(HPA + 24 + 2 * i + u, 2)
                sp.wait_ge(S[f"evacuated{u}"], NQKV // 2 + i + 1)
                sp.dma_start(z_d[2 * i + u, :, :], sv[u][:, :]).then_inc(S[f"kept_sv{u}"], 16)
        loads(HPA + 32, 2)
        sp.dma_start(dnc_out, tail[:, :, :, :]).then_inc(S["tails_kept"], 16)
        with sp.Fori(0, H) as i:
            for u in range(2):
                sp.wait_ge(S["l2_out"], 2 * i + u + 1)
                sp.dma_start(qkv_d[:, :, 2 * i + u, :].rearrange("n p c -> p n c"),
                             lo_[u][:, :].rearrange("p (n c) -> p n c", c=C)).then_inc(S[f"kept_qk{u}"], 16)
        for u in range(2):
            sp.wait_ge(S[f"kept_sv{u}"], 16 * (H + NZ) // 2)
            sp.wait_ge(S[f"kept_qk{u}"], 16 * H)

        def chunk_load(n):
            sp.dma_start(qkv[:, :, :], qkv_d[n, :, :, :]).then_inc(S["chunk_in"], 16)

        def chunk_store(n):
            sp.wait_ge(S["o_copied"], n + 1)
            sp.dma_start(o_d[n, :, :], oo[:, :]).then_inc(S["o_kept"], 16)

        chunk_load(0)
        with sp.Fori(0, NSC) as n:
            sp.wait_ge(S["ks_ps"], n + 1)
            sp.wait_ge(S["qg_done"], n + 1)
            chunk_load(n + 1)
            chunk_store(n)
            loads(HPB + 3 * n, 6)
        sp.wait_ge(S["s_done"], NP1)
        sp.dma_start(sp_out, state[:, :, :]).then_inc(S["s_kept"], 16)
        sp.wait_ge(S["s_kept"], 16)
        sp.dma_start(state[:, :, :], s0_in).then_inc(S["s_init"], 16)
        chunk_store(NCH - 1)
        sp.wait_ge(S["s_done"], NCH)
        sp.dma_start(ss_out, state[:, :, :]).then_inc(S["s_kept"], 16)
        sp.wait_ge(S["sc_lo"], NSC)
        sp.dma_start(scc_out, sctail[:, :, :, :]).then_inc(S["tails_kept"], 16)
        with sp.Fori(0, KD // 2) as i:
            loads(HPC + 3 * i, 6)
        sp.wait_ge(S["half_merged"], KD)
        sp.wait_ge(S["o_kept"], 16 * NCH)

        def head_load(i):
            for u in range(2):
                if not isinstance(i, int):
                    sp.wait_ge(S["go_scaled"], 2 * i + u - 1)
                sp.dma_start(go[u][:, :].rearrange("p (n c) -> p n c", c=C),
                             o_d[:, :, bass.ds((2 * i + u) * C, C)].rearrange("n p c -> p n c")
                             ).then_inc(S[f"go_in{u}"], 16)
                sp.dma_start(gz[u][:, :], z_d[2 * i + u, :, :]).then_inc(S[f"go_in{u}"], 16)

        peel(sp, H // 2, head_load)
        with sp.Fori(0, KD // 2) as i:
            loads(HPD + 3 * i, 6)

        def x_again(i):
            for u in range(2):
                loads(HPE + 2 * i + u, 2)
                if isinstance(i, int):
                    sp.wait_ge(S["mg_lo"], KD)
                else:
                    sp.wait_ge(S[f"evacuated{u}"], EV_E[u] + i)
                sp.dma_start(xr[u][:, :], x_in[:, 2 * i + u, :]).then_inc(S[f"xr_in{u}"], 16)

        peel(sp, KD // 2, x_again)
        with sp.Fori(0, KD // 2) as i:
            loads(HPF + 2 * i, 4)
        sp.wait_ge(S["norm_lo"], 2 * KD)
        sp.dma_start(keys[:, :, :], keys_in).then_inc(S["keys_in"], 16)

        def gates_store(i):
            for u in range(2):
                sp.wait_ge(S["gmat_out"], (TB // 4) * (2 * i + u + 1))
                sp.dma_start(gates_d[:, :, 2 * i + u, :].rearrange("g p n -> p g n"),
                             gbuf[u][:, :, :].rearrange("p (g i) t -> p g (i t)", i=G2)
                             ).then_inc(S[f"gates_kept{u}"], 16)

        with sp.Fori(0, NTB // 2) as i:
            gates_store(i)
        for u in range(2):
            sp.wait_ge(S[f"gates_kept{u}"], 16 * NTB // 2)

        def gate_load(g, u):
            if not (isinstance(g, int) and g < 2):
                sp.wait_ge(S["m_done"], G2 * (g - 1))
            sp.dma_start(gtile[u][:, :, :, :].rearrange("p a i t -> p a (i t)"), gates_d[g, :, :, :]
                         ).then_inc(S[f"gt_in{u}"], 16)

        gate_load(0, 0)
        gate_load(1, 1)
        loads(HPG, 2 * G2)
        with sp.Fori(0, NG // 2 - 1) as i:
            for u in range(2):
                hp = HPG + G2 + 8 * (2 * i + u)
                loads(hp, 2 * G2)
                gate_load(2 * i + u + 2, u)
                loads(hp + G2, 2 * G2)
        loads(HPG + G2 + 8 * (NG - 2), 16)
        loads(HPG + G2 + 8 * (NG - 1), 4)

        def y_store(i):
            for u in range(2):
                sp.wait_ge(S["norm_scaled"], 2 * KD + 2 * i + u + 1)
                sp.dma_start(y_out[:, 2 * i + u, :], nt[u][:, :]).then_inc(S[f"y_kept{u}"], 16)

        with sp.Fori(0, KD // 2) as i:
            y_store(i)
        for u in range(2):
            sp.wait_ge(S[f"y_kept{u}"], 16 * KD // 2)
        sp.wait_ge(S["s_kept"], 32)
        sp.wait_ge(S["tails_kept"], 32)

    @block.gpsimd
    def _(pool):
        with pool.Fori(0, N_PIECES // 2) as i:
            for u in range(2):
                pool.wait_ge(S["hi_done"], 2 * i + u + 1)
                pool.tensor_tensor(wl[u][:, :, :], wr[u][:, :, :], wh[u][:, :, :].bitcast(F32),
                                   ALU.subtract).then_inc(S["lo_done"], 1)

    @block.scalar
    def _(act):
        def hi(hp, slot):
            act.wait_ge(S[f"raw_full{slot}"], 16 * hp + 16)
            if not (isinstance(hp, int) and hp == 0):
                act.wait_ge(S["piece_used"], 2 * hp + slot - 1)
            act.activation(wh[slot][:, :, :], wr[slot][:, :, :], ACT.Copy).then_inc(S["hi_done"], 1)

        def his(hp, n, c0=0):
            for c in range(c0, c0 + n):
                hi(hp + 1 + c // 2, c % 2)

        def norm(c, ready):
            ready()
            for k in range(KD):
                if k >= 2:
                    act.wait_ge(S["norm_sum"], KD * c + k - 1)
                act.activation(sq[k % 2][:, :], mg[:, k, :], ACT.Square).then_inc(S["norm_sq"], 1)
            act.wait_ge(S["norm_ms"], c + 1)
            act.activation(rst[:, :], ms[:, :], ACT.Sqrt).then_inc(S["norm_root"], 1)
            if c < 2:
                for k in range(KD):
                    act.wait_ge(S["norm_scaled"], KD * c + k + 1)
                    act.activation(xh[:, k, :], nt[k % 2][:, :], ACT.Copy).then_inc(S["norm_hi"], 1)

        for u in range(2):
            hi(0, u)
        norm(0, lambda: (act.wait_ge(S["x_loaded"], 16), act.wait_ge(S["const_in"], 32)))

        def qkv_in(m, i, u, piece, ev, first):
            his(piece, 2)
            act.wait_ge(S["piece_used"], 2 * piece + 2)
            if first:
                act.wait_ge(S["pads_set"], 2)
            else:
                act.wait_ge(S["conv_done"], m - 1)
            a, n = VEC["dnst"]
            w = DN_TAPS - 1
            act.activation(cbuf[u][:, w:w + HT], ps[u][:, 0, 0:HT], ACT.Copy)
            act.activation(cbuf[u][:, w + HT:w + TP], ps[u][:, 1, 0:TP - HT], ACT.Copy)
            act.activation(cbuf[u][:, w + TP:2 * w + TP], vec[:, bass.ds(a + m * w, w)], ACT.Copy)
            act.activation(cbuf[u][:, 2 * w + TP:AW], ps[u][:, 1, TP - HT:HT], ACT.Copy)
            act.activation(tail[:, m, :, :], ps[u][:, 1, HT - 2 * TS:HT].rearrange(
                "p (a b) -> p a b", a=2)[:, :, TS - w:TS], ACT.Copy).then_inc(S[f"evacuated{u}"], 1)

        def silu_out(m, u, out):
            act.wait_ge(S["conv_done"], m + 1)
            w = DN_TAPS - 1
            act.activation(out[:, 0:TP], cv[u][:, 0:TP], ACT.Silu)
            act.activation(out[:, TP:T], cv[u][:, TP + w:T + w], ACT.Silu).then_inc(S["silu_done"], 1)

        def qk_unit(i):
            for u in range(2):
                m = 2 * i + u
                qkv_in(m, i, u, HPA + m, i, isinstance(i, int))
                if isinstance(i, int) and u == 0:
                    act.wait_ge(S["norm_lo"], KD)
                silu_out(m, u, mg[:, m, :])

        peel(act, H, qk_unit)

        def v_unit(i):
            for u in range(2):
                m = 16 + 2 * i + u
                qkv_in(m, i, u, HPA + m, i, False)
                if not isinstance(i, int):
                    act.wait_ge(S[f"kept_sv{u}"], 16 * i)
                silu_out(m, u, sv[u])

        peel(act, H // 2, v_unit)
        with act.Fori(0, NZ // 2) as i:
            for u in range(2):
                m = 24 + 2 * i + u
                his(HPA + m, 2)
                act.wait_ge(S[f"kept_sv{u}"], 16 * i + 16 * H // 2)
                act.wait_ge(S["piece_used"], 2 * m + 2)
                act.activation(halves(sv[u][:, :]), both(u), ACT.Silu).then_inc(S[f"evacuated{u}"], 1)
        his(HPA + 32, 2)
        act.wait_ge(S["piece_used"], P_B)
        act.activation(halves(bar[:, :]), both(0), ACT.Copy).then_inc(S["evacuated0"], 1)

        for u in range(2):
            act.wait_ge(S[f"kept_sv{u}"], 16 * (H + NZ) // 2)

        def l2_unit(i):
            for u in range(2):
                m = 2 * i + u
                if not isinstance(i, int):
                    act.wait_ge(S["l2_sum"], m - 1)
                    act.wait_ge(S[f"kept_qk{u}"], 16 * i)
                act.activation(lq[u][:, :], mg[:, m, :], ACT.Square).then_inc(S["l2_sq"], 1)
            for u in range(2):
                m = 2 * i + u
                act.wait_ge(S["l2_ss"], m + 1)
                act.activation(ln[u][:, :], ln[u][:, :], ACT.Sqrt).then_inc(S["l2_root"], 1)

        act.wait_ge(S["silu_done"], 16)
        peel(act, H, l2_unit)

        act.wait_ge(S["tok_ps"], 1)
        for u in range(2):
            act.wait_ge(S[f"kept_qk{u}"], 16 * H)
        act.activation(heads(small["beta"][:, :], H), raw_tok[:, :, 0:H], ACT.Sigmoid).then_inc(S["beta_done"], 1)
        act.activation(decay[:, :], vector("alog")[0:64, :], ACT.Exp).then_inc(S["decay_exp"], 1)
        act.wait_ge(S["sp_in"], 1)
        act.activation(small["sp2"][:, :], small["sp2"][:, :], ACT.Exp, scale=-1.0).then_inc(S["sp_exp"], 1)
        act.wait_ge(S["sp_one"], 1)
        act.activation(small["sp2"][:, :], small["sp2"][:, :], ACT.Ln).then_inc(S["sp_ln"], 1)
        act.wait_ge(S["gc_ps"], 1)
        act.activation(small["eg"][:, :], aux[0:64, 0, 0:NCH * H], ACT.Exp)
        act.activation(egl[:, :], aux[:, 1, 0:NCH * H], ACT.Exp).then_inc(S["eg_done"], 1)
        act.wait_ge(S["kdec_in"], 1)
        act.activation(small["kdec"][:, :], small["kdec"][:, :], ACT.Exp).then_inc(S["kdec_done"], 1)

        def delta(n):
            act.wait_ge(S["masked"], 2 * n + 1)
            act.activation(pp[:, :], pp[:, :], ACT.Exp).then_inc(S["exp_done"], 1)
            act.wait_ge(S["masked"], 2 * n + 2)
            act.activation(el[:, :], el[:, :], ACT.Exp).then_inc(S["exp_done"], 1)
            act.activation(egb[:, :], aux[:, 1, :], ACT.Exp).then_inc(S["exp_done"], 1)
            act.wait_ge(S["xt_ps"], n + 1)
            act.activation(yy[:, :], aux[0:64, 3, :], ACT.Copy).then_inc(S["y1_done"], 1)
            for l in range(1, LEVELS):
                act.wait_ge(S["p_ps"], 5 * n + l)
                act.activation(pp[:, :], aux[0:64, 2, :], ACT.Copy).then_inc(S["p_copied"], 1)
            act.wait_ge(S["vn_ps"], n + 1)
            act.activation(vb[:, :, :], pair(2), ACT.Copy).then_inc(S["vn_done"], 1)
            if not (isinstance(n, int) and n == 0):
                act.wait_ge(S["o_kept"], 16 * n)
            act.wait_ge(S["o_ps"], n + 1)
            act.activation(oo[:, :], aux[:, 0, :], ACT.Copy).then_inc(S["o_copied"], 1)

        def short(j):
            hp = HPB + 3 * j
            his(hp, 2)
            act.wait_ge(S["evacuated1"], EV_B[1] + j)
            act.wait_ge(S["piece_used"], 2 * hp + 2)
            act.activation(halves(ctmp[:, :]), both(0), ACT.Copy).then_inc(S["evacuated0"], 1)
            his(hp, 4, 2)
            act.wait_ge(S["evacuated0"], EV_B[0] + 2 * j + 2)
            act.activation(yh[:, j, :], yt[:, :], ACT.Copy).then_inc(S["sc_hi"], 1)

        def delta_short(n):
            delta(n)
            short(n)

        peel(act, NSC, delta_short)
        delta(NCH - 1)

        def gates(hp, i, ev, nw):
            for u in range(2):
                his(hp, 2, 3 * u)
                act.wait_ge(S["evacuated1"], ev[1] + 2 * i + u - 1)
                act.wait_ge(S["piece_used"], 2 * hp + 3 * u + 2)
                act.activation(halves(sg[u][:, :]), both(0), ACT.Sigmoid).then_inc(S["evacuated0"], 1)
                his(hp, 1, 3 * u + 2)

        act.wait_ge(S["o_kept"], 16 * NCH)
        act.wait_ge(S["sc_lo"], NSC)
        act.wait_ge(S["s_done"], NCH)
        with act.Fori(0, KD // 2) as i:
            gates(HPC + 3 * i, i, EV_C, 0)

        act.wait_ge(S["half_merged"], KD)
        act.wait_ge(S["piece_used"], P_D)

        def gated(i):
            for u in range(2):
                h = 2 * i + u
                act.wait_ge(S[f"go_in{u}"], 32 * i + 32)
                if not isinstance(i, int):
                    act.wait_ge(S["go_sum"], h - 1)
                act.activation(gq[u][:, :], go[u][:, :], ACT.Square).then_inc(S["go_sq"], 1)
            for u in range(2):
                act.wait_ge(S["go_ss"], 2 * i + u + 1)
                act.activation(gr[u][:, :], gr[u][:, :], ACT.Sqrt).then_inc(S["go_root"], 1)
            for u in range(2):
                act.wait_ge(S["go_scaled"], 2 * i + u + 1)
                act.activation(yh[:, 2 * i + u, :], gt_[u][:, :], ACT.Copy).then_inc(S["go_hi"], 1)

        peel(act, H // 2, gated)
        act.wait_ge(S["go_lo"], H)
        with act.Fori(0, KD // 2) as i:
            gates(HPD + 3 * i, i, EV_D, 0)
        act.wait_ge(S["piece_used"], P_E)
        act.wait_ge(S["merged"], KD)
        for k in range(KD):
            act.activation(xh[:, k, :], mg[:, k, :], ACT.Copy).then_inc(S["mg_hi"], 1)
        with act.Fori(0, KD // 2) as i:
            his(HPE + 2 * i, 4)
        norm(1, lambda: (act.wait_ge(S["evacuated0"], EV_F[0]), act.wait_ge(S["evacuated1"], EV_F[1])))
        with act.Fori(0, KD // 2) as i:
            his(HPF + 2 * i, 4)

        def soft(tb, rows):
            act.wait_ge(S["shifted"], tb + 1)
            act.activation(gate[0:rows, :, :], gate[0:rows, :, :], ACT.Exp).then_inc(S["gate_exp"], 1)
            act.wait_ge(S["pickT_ps"], tb + 1)
            for x in range(3):
                done = act.activation(idxT[x][:, bass.ds(tb * 128, rows)], ps[1][:, 0, 128 * x:128 * x + rows],
                                      ACT.Copy)
            done.then_inc(S["pickT_done"], 1)

        with act.Fori(0, TP // 128) as tb:
            soft(tb, 128)
        soft(TP // 128, TS)

        def gmats(i):
            for blk in range(2):
                if not isinstance(i, int):
                    act.wait_ge(S[f"gates_kept{blk}"], 16 * i)
                with act.Fori(0, TB // 8) as l:
                    for u in range(2):
                        act.wait_ge(S["gmat_ps"], (TB // 4) * (2 * i + blk) + 2 * l + u + 1)
                        act.activation(gbuf[blk][:, :, bass.ds(8 * l + 4 * u, 4)],
                                       aux[:, u, :].rearrange("p (t i) -> p i t", t=4),
                                       ACT.Copy).then_inc(S["gmat_out"], 1)

        peel(act, NTB // 2, gmats)
        for u in range(2):
            act.wait_ge(S[f"gates_kept{u}"], 16 * NTB // 2)

        def hidden(hp, g, par, last=False):
            for k in range(G2):
                q = k % 2
                his(hp + k, 2)
                act.wait_ge(S["piece_used"], 2 * (hp + k) + 2)
                if not (isinstance(g, int) and g == 0 and k < 2):
                    act.wait_ge(S["m_done"], G2 * g + k - 1)
                act.activation(halves(gl[q][:, :]), both(q), ACT.Gelu).then_inc(S[f"evacuated{q}"], 1)
                act.wait_ge(S["m_done"], G2 * g + k + 1)
                act.activation(yh[:, G2 * par + k, :], mm[q][:, :], ACT.Copy).then_inc(S["m_hi"], 1)

        hidden(HPG, 0, 0)
        with act.Fori(0, NG // 2 - 1) as i:
            for u in range(2):
                hp = HPG + G2 + 8 * (2 * i + u)
                hidden(hp, 2 * i + u + 1, 1 - u)
                his(hp + G2, 8)
        hp = HPG + G2 + 8 * (NG - 2)
        hidden(hp, NG - 1, 1)
        his(hp + G2, 8)
        his(hp + 8, 6)
        norm(2, lambda: (act.wait_ge(S["evacuated0"], EV_END[0]), act.wait_ge(S["evacuated1"], EV_END[1])))

    @block.vector
    def _(dve):
        def wait(name, value):
            dve.wait_ge(S[name], value)

        def norm(c, ready):
            ready()
            wait("norm_sum", KD * (c + 1))
            dve.tensor_scalar(halves(ms[:, :]), aux[:, 0:2, 0:HT], 1.0 / D, EPS, ALU.mult, ALU.add
                              ).then_inc(S["norm_ms"], 1)
            wait("norm_root", c + 1)
            dve.reciprocal(ms[:, :], rst[:, :]).then_inc(S["norm_inv"], 1)
            wait("norm_inv", c + 1)
            for k in range(0, KD, 2):
                for u in range(2):
                    if k:
                        if c < 2:
                            wait("norm_lo", KD * c + k + u - 1)
                        else:
                            wait(f"y_kept{u}", 16 * k // 2)
                    dve.scalar_tensor_tensor(nt[u][:, :], mg[:, k + u, :], vector(("g1", "g2", "gf")[c], k + u),
                                             ms[:, :], ALU.mult, ALU.mult).then_inc(S["norm_scaled"], 1)
                if c < 2:
                    for u in range(2):
                        wait("norm_hi", KD * c + k + u + 1)
                        dve.tensor_tensor(xl[:, k + u, :], nt[u][:, :], xh[:, k + u, :].bitcast(F32),
                                          ALU.subtract).then_inc(S["norm_lo"], 1)

        norm(0, lambda: wait("const_in", 32))
        wait("norm_lo", KD)
        for u in range(2):
            dve.memset(cbuf[u][:, 0:DN_TAPS - 1], 0.0).then_inc(S["pads_set"], 1)

        def conv(m, i, u):
            wait(f"evacuated{u}", i + 1)
            if u < 2 and not (isinstance(m, int) and m < 2):
                wait("silu_done", m - 1)
            w = DN_TAPS - 1
            n = AW - w
            a, _n = VEC["dnw"]
            dve.tensor_scalar(cv[u][:, 0:n], cbuf[u][:, 0:n], vec[:, bass.ds(a + DN_TAPS * m, 1)], None,
                              ALU.mult).then_inc(S["conv_step"], 1)
            for k in range(1, DN_TAPS):
                wait("conv_step", w * m + k)
                dve.scalar_tensor_tensor(cv[u][:, 0:n], cbuf[u][:, k:k + n],
                                         vec[:, bass.ds(a + DN_TAPS * m + k, 1)], cv[u][:, 0:n],
                                         ALU.mult, ALU.add
                                         ).then_inc(S["conv_step"] if k < w else S["conv_done"], 1)

        def conv_pair(i):
            for u in range(2):
                conv(2 * i + u, i, u)

        peel(dve, NQKV // 2, conv_pair)

        for u in range(2):
            wait(f"kept_sv{u}", 16 * (H + NZ) // 2)

        def l2(i, scale):
            first = isinstance(i, int)
            for u in range(2):
                m = 2 * i + u
                wait("l2_sum", m + 1)
                if not first:
                    wait("l2_out", m - 1)
                dve.tensor_scalar(halves(ln[u][:, :]), aux[:, 2 * u:2 * u + 2, 0:HT], scale, scale * EPS,
                                  ALU.mult, ALU.add).then_inc(S["l2_ss"], 1)
            for u in range(2):
                m = 2 * i + u
                wait("l2_root", m + 1)
                dve.reciprocal(ln[u][:, :], ln[u][:, :]).then_inc(S["l2_inv"], 1)
            for u in range(2):
                m = 2 * i + u
                wait("l2_inv", m + 1)
                if not first:
                    wait(f"kept_qk{u}", 16 * i)
                dve.tensor_tensor(lo_[u][:, :], mg[:, m, :], ln[u][:, :], ALU.mult).then_inc(S["l2_out"], 1)

        l2(0, float(DK))
        with dve.Fori(1, H // 2) as i:
            l2(i, float(DK))
        with dve.Fori(H // 2, H) as i:
            l2(i, 1.0)

        sp1, sp2 = small["sp1"][:, :], small["sp2"][:, :]
        for u in range(2):
            wait(f"kept_qk{u}", 16 * H)
        wait("tok_ps", 1)
        wait("beta_done", 1)
        dve.tensor_tensor(heads(sp1, H), raw_tok[:, :, 32:32 + H],
                          vector("dtb")[0:64, :].unsqueeze(1).to_broadcast([64, NCH, H]), ALU.add
                          ).then_inc(S["sp_max"], 1)
        wait("sp_max", 1)
        dve.tensor_scalar(sp2, sp1, -1.0, None, ALU.mult).then_inc(S["sp_max"], 1)
        wait("sp_max", 2)
        dve.tensor_tensor(sp2, sp2, sp1, ALU.max).then_inc(S["sp_in"], 1)
        wait("sp_exp", 1)
        dve.tensor_scalar(sp2, sp2, 1.0, None, ALU.add).then_inc(S["sp_one"], 1)
        wait("sp_ln", 1)
        dve.scalar_tensor_tensor(sp1, sp1, 0.0, sp2, ALU.max, ALU.add).then_inc(S["sp_max"], 1)
        wait("sp_max", 3)
        wait("decay_exp", 1)
        dve.scalar_tensor_tensor(heads(small["gtok"][:, :], H), heads(sp1, H), -1.0,
                                 decay[:, :].unsqueeze(1).to_broadcast([64, NCH, H]), ALU.mult, ALU.mult
                                 ).then_inc(S["g_ready"], 1)
        wait("gc_ps", 1)
        wait("eg_done", 1)
        dve.tensor_copy(small["gcum"][:, :], aux[0:64, 0, 0:NCH * H]).then_inc(S["gcum_done"], 1)
        wait("gcum_done", 1)
        dve.tensor_tensor(small["kdec"][:, :], aux[0:64, 1, 0:NCH * H], small["gcum"][:, :], ALU.subtract
                          ).then_inc(S["kdec_in"], 1)
        dve.tensor_tensor(small["nbeg"][:, :], small["beta"][:, :], small["eg"][:, :], ALU.mult
                          ).then_inc(S["nbeg_done"], 1)
        wait("nbeg_done", 1)
        wait("kdec_done", 1)
        dve.memset(scb[:, 0:SC_TAPS - 1], 0.0).then_inc(S["pads_set"], 1)
        dve.memset(state[:, :, :], 0.0).then_inc(S["pads_set"], 1)
        wait("pads_set", 4)

        def per_token(name, n, width=C):
            return small[name][:, bass.ds(n * H, H)].unsqueeze(2).to_broadcast([64, H, width])

        def per_mask(t):
            return t.unsqueeze(1).to_broadcast([64, H, C])

        def level(l):
            a, _n = CONST["levels"]
            return cst[0:64, a + C * l:a + C * l + C]

        def delta(n):
            first = isinstance(n, int) and n == 0
            dve.tensor_tensor(heads(lm[:, :]), per_token("gtok", n), per_mask(const("upper", 64)), ALU.mult
                              ).then_inc(S["gu_done"], 1)
            wait("gcb_ps", n + 1)
            dve.tensor_tensor(heads(pp[:, :]), heads(aux[0:64, 1, :]), per_token("gcum", n), ALU.subtract
                              ).then_inc(S["masked_raw"], 1)
            dve.tensor_tensor(heads(el[:, :]), per_token("gcum", n), heads(aux[0:64, 1, :]), ALU.subtract
                              ).then_inc(S["masked_raw"], 1)
            wait("masked_raw", 2 * n + 2)
            dve.tensor_tensor(heads(pp[:, :]), heads(pp[:, :]), per_mask(const("negT", 64)), ALU.add
                              ).then_inc(S["masked"], 1)
            dve.tensor_tensor(heads(el[:, :]), heads(el[:, :]), per_mask(const("negL", 64)), ALU.add
                              ).then_inc(S["masked"], 1)
            wait("kq_ps", n + 1)
            wait("exp_done", 3 * n + 1)
            dve.tensor_tensor(att[:, :], pp[:, :], aux[0:64, 2, :], ALU.mult).then_inc(S["att_done"], 1)
            wait("exp_done", 3 * n + 2)
            dve.tensor_tensor(ll[:, :], el[:, :], aux[0:64, 0, :], ALU.mult).then_inc(S["l_raw"], 1)
            wait("l_raw", n + 1)
            dve.tensor_tensor(heads(ll[:, :]), heads(ll[:, :]), per_token("beta", n), ALU.mult
                              ).then_inc(S["l_done"], 1)
            wait("l_done", n + 1)
            dve.tensor_tensor(heads(xx[:, :]), heads(ll[:, :]), per_mask(level(0)), ALU.mult
                              ).then_inc(S["x1_in"], 1)
            wait("x1_in", n + 1)
            dve.tensor_tensor(heads(xx[:, :]), per_mask(const("eye", 64)), heads(xx[:, :]), ALU.subtract
                              ).then_inc(S["x1_done"], 1)
            dve.tensor_tensor(heads(lm[:, :]), heads(ll[:, :]), per_mask(level(1)), ALU.mult
                              ).then_inc(S["lm_done"], 1)
            wait("exp_done", 3 * n + 3)
            dve.tensor_tensor(qg[:, :], qkv[:, 0:H, :].rearrange("p h c -> p (h c)"), egb[:, :], ALU.mult
                              ).then_inc(S["qg_done"], 1)
            wait("v_ps", n + 1)
            dve.tensor_tensor(vb[:, :, :], pair(0), per_token("beta", n, 128), ALU.mult
                              ).then_inc(S["vb_done"], 1)
            wait("y1_done", n + 1)
            for l in range(1, LEVELS):
                if l < LEVELS - 1:
                    wait("p_ps", 5 * n + l)
                    dve.tensor_tensor(heads(lm[:, :]), heads(ll[:, :]), per_mask(level(l + 1)), ALU.mult
                                      ).then_inc(S["lm_done"], 1)
                if l == 2:
                    wait("k_ps", n + 1)
                    dve.tensor_tensor(kd[:, :, :], pair(0), per_token("kdec", n, 128), ALU.mult
                                      ).then_inc(S["kd_done"], 1)
                if l == 3:
                    if not first:
                        wait("s_done", n)
                    if isinstance(n, int) and n == NP1:
                        wait("s_init", 16)
                    dve.tensor_tensor(sdec[:, :, :], state[:, :, :],
                                      egl[:, bass.ds(n * H, H)].unsqueeze(2).to_broadcast([128, H, 128]),
                                      ALU.mult).then_inc(S["sdec_done"], 1)
                wait("z_ps", 5 * n + l)
                dve.tensor_tensor(yy[:, :], yy[:, :], aux[0:64, 3, :], ALU.subtract).then_inc(S["y_upd"], 1)
                if l < LEVELS - 1:
                    dve.tensor_tensor(xx[:, :], xx[:, :], aux[0:64, 2, :], ALU.subtract).then_inc(S["x_upd"], 1)
                    wait("y_upd", 5 * n + l)
                    wait("x_upd", 4 * n + l)
            wait("ks_ps", n + 1)
            dve.tensor_tensor(rr[:, :, :], pair(0), per_token("nbeg", n, 128), ALU.mult).then_inc(S["r_raw"], 1)
            wait("r_raw", n + 1)
            dve.tensor_tensor(rr[:, :, :], vb[:, :, :], rr[:, :, :], ALU.subtract).then_inc(S["r_done"], 1)
            wait("sup_ps", n + 1)
            wait("sdec_done", n + 1)
            dve.tensor_tensor(state[:, :, :], sdec[:, :, :],
                              aux[:, 2:4, :].rearrange("p a (h n) -> p (a h) n", n=128), ALU.add
                              ).then_inc(S["s_done"], 1)

        def short(j):
            w = SC_TAPS - 1
            a, _n = VEC["scst"]
            b, _n = VEC["scw"]
            n = SW - w
            first = isinstance(j, int)
            wait("evacuated0", EV_B[0] + 2 * j + 1)
            hp = HPB + 3 * j
            wait("piece_used", 2 * hp + 4)
            dve.tensor_copy(scb[:, w + TP:2 * w + TP], vec[:, bass.ds(a + w * j, w)])
            dve.tensor_tensor(scb[:, w:w + HT], ctmp[:, 0:HT], ps[1][:, 0, 0:HT], ALU.mult)
            dve.tensor_tensor(scb[:, w + HT:w + TP], ctmp[:, HT:TP], ps[1][:, 1, 0:TP - HT], ALU.mult)
            dve.tensor_tensor(scb[:, 2 * w + TP:SW], ctmp[:, TP:T], ps[1][:, 1, TP - HT:HT], ALU.mult
                              ).then_inc(S["evacuated1"], 1)
            wait("evacuated1", EV_B[1] + j + 1)
            dve.tensor_copy(sctail[:, j, 0, :], scb[:, TP:TP + w])
            dve.tensor_copy(sctail[:, j, 1, :], scb[:, SW - w:SW])
            dve.tensor_scalar(scv[:, 0:n], scb[:, 0:n], vec[:, bass.ds(b + SC_TAPS * j, 1)], None, ALU.mult
                              ).then_inc(S["sc_step"], 1)
            for k in range(1, SC_TAPS):
                wait("sc_step", SC_TAPS * j + k)
                dve.scalar_tensor_tensor(scv[:, 0:n], scb[:, k:k + n], vec[:, bass.ds(b + SC_TAPS * j + k, 1)],
                                         scv[:, 0:n], ALU.mult, ALU.add).then_inc(S["sc_step"], 1)
            wait("sc_step", SC_TAPS * j + SC_TAPS)
            wait("piece_used", 2 * hp + 6)
            dve.tensor_tensor(yt[:, 0:HT], scv[:, 0:HT], ps[0][:, 0, 0:HT], ALU.mult)
            dve.tensor_tensor(yt[:, HT:TP], scv[:, HT:TP], ps[0][:, 1, 0:TP - HT], ALU.mult)
            dve.tensor_tensor(yt[:, TP:T], scv[:, TP + w:T + w], ps[0][:, 1, TP - HT:HT], ALU.mult
                              ).then_inc(S["evacuated0"], 1)
            wait("sc_hi", j + 1)
            dve.tensor_tensor(yl[:, j, :], yt[:, :], yh[:, j, :].bitcast(F32), ALU.subtract
                              ).then_inc(S["sc_lo"], 1)
            wait("sc_lo", j + 1)

        def delta_short(n):
            delta(n)
            short(n)

        peel(dve, NSC, delta_short)
        delta(NCH - 1)

        wait("s_kept", 32)
        wait("o_kept", 16 * NCH)
        with dve.Fori(0, KD // 2) as i:
            for u in range(2):
                wait("evacuated0", EV_C[0] + 2 * i + u + 1)
                wait("piece_used", P_C + 6 * i + 3 * u + 3)
                dve.tensor_tensor(halves(mg[:, 2 * i + u, :]), halves(sg[u][:, :]), both(1), ALU.mult
                                  ).then_inc(S["evacuated1"], 1)
        wait("evacuated1", EV_D[1])
        dve.engine_nop().then_inc(S["half_merged"], KD)

        def gated(i):
            first = isinstance(i, int)
            for u in range(2):
                wait("go_sum", 2 * i + u + 1)
                dve.tensor_scalar(halves(gr[u][:, :]), aux[:, 2 * u:2 * u + 2, 0:HT], 1.0 / 128, EPS,
                                  ALU.mult, ALU.add).then_inc(S["go_ss"], 1)
            for u in range(2):
                wait("go_root", 2 * i + u + 1)
                dve.reciprocal(gr[u][:, :], gr[u][:, :]).then_inc(S["go_inv"], 1)
            for u in range(2):
                h = 2 * i + u
                wait("go_inv", h + 1)
                if not first:
                    wait("go_lo", h - 1)
                dve.tensor_tensor(gt_[u][:, :], go[u][:, :], gr[u][:, :], ALU.mult).then_inc(S["go_raw"], 1)
            for u in range(2):
                wait("go_raw", 2 * i + u + 1)
                dve.scalar_tensor_tensor(gt_[u][:, :], gt_[u][:, :], vector("dng", 0), gz[u][:, :],
                                         ALU.mult, ALU.mult).then_inc(S["go_scaled"], 1)
            for u in range(2):
                h = 2 * i + u
                wait("go_hi", h + 1)
                dve.tensor_tensor(yl[:, h, :], gt_[u][:, :], yh[:, h, :].bitcast(F32), ALU.subtract
                                  ).then_inc(S["go_lo"], 1)

        peel(dve, H // 2, gated)
        wait("go_lo", H)
        with dve.Fori(0, KD // 2) as i:
            for u in range(2):
                m = 2 * i + u
                wait("evacuated0", EV_D[0] + m + 1)
                wait("piece_used", P_D + 6 * i + 3 * u + 3)
                dve.tensor_tensor(halves(dt[u][:, :]), halves(sg[u][:, :]), both(1), ALU.mult
                                  ).then_inc(S["evacuated1"], 1)
                wait("evacuated1", EV_D[1] + m + 1)
                dve.tensor_tensor(mg[:, m, :], mg[:, m, :], dt[u][:, :], ALU.add).then_inc(S["merged"], 1)
        for k in range(KD):
            wait("mg_hi", k + 1)
            dve.tensor_tensor(xl[:, k, :], mg[:, k, :], xh[:, k, :].bitcast(F32), ALU.subtract
                              ).then_inc(S["mg_lo"], 1)
        wait("mg_lo", KD)
        with dve.Fori(0, KD // 2) as i:
            for u in range(2):
                wait(f"xr_in{u}", 16 * i + 16)
                wait("piece_used", P_E + 4 * i + 2 * u + 2)
                dve.tensor_tensor(halves(mg[:, 2 * i + u, :]), halves(xr[u][:, :]), both(u), ALU.add
                                  ).then_inc(S[f"evacuated{u}"], 1)
        for u in range(2):
            wait(f"evacuated{u}", EV_F[u])
        norm(1, lambda: None)
        with dve.Fori(0, KD // 2) as i:
            for u in range(2):
                wait("piece_used", P_F + 4 * i + 2 * u + 2)
                dve.tensor_copy(halves(qf[:, 2 * i + u, :]), both(u)).then_inc(S[f"evacuated{u}"], 1)
        wait("norm_lo", 2 * KD)

        tvv = tv[:, :, :].rearrange("p (h s) k -> p h s k", s=2)
        tifv = tif[:, :, :].rearrange("p (h s) k -> p h s k", s=2)
        NEGMAX = -3.0e38
        STEPS = 23

        def plain_wait(name, value):
            wait(name, value)
            if not isinstance(value, int):
                dve.sem_inc(S["dve_waited"])

        def topk(tb, rows):
            count = [0]

            def step(ins):
                count[0] += 1
                ins.then_inc(S["topk_step"], 1)
                plain_wait("topk_step", STEPS * tb + count[0])

            def score(hp):
                return aux[0:rows, hp // 4, (hp % 4) * NK:(hp % 4 + 1) * NK]

            R = slice(0, rows)
            plain_wait("score_ps", tb + 1)
            for hp in range(KD):
                last = dve.max(tv[R, hp, 0:8], score(hp))
            step(last)
            for hp in range(KD):
                dve.max_index(ti[R, hp, 0:8], tv[R, hp, 0:8], score(hp))
                last = dve.match_replace(mrall[R, hp, :], tv[R, hp, 0:8], score(hp), NEGMAX)
            last.then_inc(S["scores_read"], 1)
            plain_wait("scores_read", tb + 1)
            for hp in range(KD):
                last = dve.max(tv[R, hp, 8:16], mrall[R, hp, :])
            step(last)
            for hp in range(KD):
                last = dve.max_index(ti[R, hp, 8:16], tv[R, hp, 8:16], mrall[R, hp, :])
            step(last)
            step(dve.tensor_copy(tif[R, :, :], ti[R, :, :]))
            for hh in range(2):
                hs = slice(4 * hh, 4 * hh + 4)
                step(dve.tensor_tensor(cand[R, :, :, :],
                                       tvv[R, hs, 0, :].unsqueeze(3).to_broadcast([rows, 4, TOPK, TOPK]),
                                       tvv[R, hs, 1, :].unsqueeze(2).to_broadcast([rows, 4, TOPK, TOPK]), ALU.add))
                for h in range(4):
                    last = dve.max(best[R, 4 * hh + h, 0:8], cand[R, h, :, :].rearrange("p a b -> p (a b)"))
                step(last)
                for h in range(4):
                    c = cand[R, h, :, :].rearrange("p a b -> p (a b)")
                    dve.max_index(posu[R, 4 * hh + h, 0:8], best[R, 4 * hh + h, 0:8], c)
                    last = dve.match_replace(sel[R, h, :, :].rearrange("p a b -> p (a b)"),
                                             best[R, 4 * hh + h, 0:8], c, NEGMAX)
                step(last)
                for h in range(4):
                    last = dve.max(best[R, 4 * hh + h, 8:16], sel[R, h, :, :].rearrange("p a b -> p (a b)"))
                step(last)
                for h in range(4):
                    last = dve.max_index(posu[R, 4 * hh + h, 8:16], best[R, 4 * hh + h, 8:16],
                                         sel[R, h, :, :].rearrange("p a b -> p (a b)"))
                step(last)
            dve.tensor_tensor(gate[R, :, :], best[R, :, :], best[R, :, 0:1].to_broadcast([rows, H, TOPK]),
                              ALU.subtract).then_inc(S["shifted"], 1)
            dve.tensor_scalar(posi[0][R, :, :], posu[R, :, :], 4, None, ALU.logical_shift_right)
            step(dve.tensor_scalar(posi[1][R, :, :], posu[R, :, :], TOPK - 1, None, ALU.bitwise_and))
            for s in range(2):
                last = dve.tensor_copy(posf[s][R, :, :], posi[s][R, :, :])
            step(last)
            i16 = const("iota16")[R, :].unsqueeze(1).to_broadcast([rows, 4 * TOPK, TOPK])
            for hh in range(2):
                hs = slice(4 * hh, 4 * hh + 4)
                bufs = (sel, cand)
                for s in range(2):
                    last = dve.tensor_tensor(bufs[s][R, :, :, :].rearrange("p h k j -> p (h k) j"), i16,
                                             posf[s][R, hs, :].rearrange("p h k -> p (h k)").unsqueeze(2)
                                             .to_broadcast([rows, 4 * TOPK, TOPK]), ALU.is_equal)
                step(last)
                for s in range(2):
                    last = dve.tensor_tensor(bufs[s][R, :, :, :], bufs[s][R, :, :, :],
                                             tifv[R, hs, s, :].unsqueeze(2).to_broadcast([rows, 4, TOPK, TOPK]),
                                             ALU.mult)
                step(last)
                for s in range(2):
                    last = dve.reduce_sum(pick[s][R, hs, :], bufs[s][R, :, :, :], AX_X)
                if hh == 0:
                    step(last)
            wait("gate_exp", tb + 1)
            step(dve.reduce_sum(gsum[R, :], gate[R, :, :], AX_X))
            step(dve.reciprocal(gsum[R, :], gsum[R, :]))
            dve.tensor_tensor(gate[R, :, :], gate[R, :, :],
                              gsum[R, :].unsqueeze(2).to_broadcast([rows, H, TOPK]), ALU.mult
                              ).then_inc(S["pick_done"], 1)
            wait("pickT_ps", tb + 1)
            assert count[0] == STEPS, count[0]

        with dve.Fori(0, TP // 128) as tb:
            topk(tb, 128)
        topk(TP // 128, TS)

        wait("pickT_done", TP // 128 + 1)

        def onehots(i):
            for u in range(2):
                if not isinstance(i, int):
                    wait("gmat_ps", 2 * i + u - 1)
                for c in range(4):
                    t = bass.ds(8 * i + 4 * u + c, 1)
                    dve.tensor_scalar(oa[u][:, c, :], const("iota"), idxT[0][:, t], idxT[2][:, t],
                                      ALU.is_equal, ALU.mult)
                    last = dve.tensor_scalar(ob[u][:, c, :], const("iota"), idxT[1][:, t], None, ALU.is_equal)
                last.then_inc(S["onehots"], 1)

        peel(dve, T // 8, onehots)
        for u in range(2):
            wait(f"gates_kept{u}", 16 * NTB // 2)

        def hidden(hp, g, gi, par):
            gp = par
            wait(f"gt_in{par}", 16 * gi + 16)
            for k in range(G2):
                q = k % 2
                wait(f"evacuated{q}", EV_G[q] + PER_G * g + k // 2 + 1 - (0 if isinstance(g, int) and g == 0
                                                                          else KD // 2))
                if not (isinstance(g, int) and g == 0 and k < 2):
                    wait("m_lo", G2 * g + k - 1)
                dve.tensor_tensor(mm[q][:, :].rearrange("p (a t) -> p a t", t=TB),
                                  gl[q][:, :].rearrange("p (a t) -> p a t", t=TB),
                                  gtile[par][:, :, k, :], ALU.mult).then_inc(S["m_done"], 1)
                wait("m_hi", G2 * g + k + 1)
                dve.tensor_tensor(yl[:, G2 * par + k, :], mm[q][:, :], yh[:, G2 * par + k, :].bitcast(F32),
                                  ALU.subtract).then_inc(S["m_lo"], 1)

        def collect(hp, g):
            for d in range(KD // 2):
                wait("group_done", (KD // 2) * g + d + 1)
                dve.tensor_tensor(halves(mg[:, 2 * d, :]), halves(mg[:, 2 * d, :]), both(0), ALU.add
                                  ).then_inc(S["evacuated0"], 1)
                wait("piece_used", 2 * hp + d + 1)
                dve.tensor_tensor(halves(mg[:, 2 * d + 1, :]), halves(mg[:, 2 * d + 1, :]), both(1), ALU.add
                                  ).then_inc(S["evacuated1"], 1)

        hidden(HPG, 0, 0, 0)
        with dve.Fori(0, NG // 2 - 1) as i:
            for u in range(2):
                hp = HPG + G2 + 8 * (2 * i + u)
                hidden(hp, 2 * i + u + 1, i + u, 1 - u)
                collect(hp + G2, 2 * i + u)
        hp = HPG + G2 + 8 * (NG - 2)
        hidden(hp, NG - 1, NG // 2 - 1, 1)
        collect(hp + G2, NG - 2)
        collect(hp + 8, NG - 1)
        for u in range(2):
            wait(f"evacuated{u}", EV_END[u])
        norm(2, lambda: None)

    @block.tensor
    def _(pe):
        def piece(hp, c, slot, high, low, k0, first, last, tiles_=range(NPIECE), done=("piece_used",)):
            w = c % 2
            for t in tiles_:
                for half in range(2):
                    cols = slice(half * HT, (half + 1) * HT)
                    k = k0 + t - tiles_[0]
                    for x, (a, b) in enumerate(((wh, high), (wh, low), (wl, high))):
                        mm_ = pe.matmul(ps[slot][:, half, 0:HT], a[w][:, t, :], b[:, k, cols],
                                        start=first and t == tiles_[0] and x == 0,
                                        stop=last and t == tiles_[-1] and x == 2)
            mm_.then_inc(S[done[0]], 1)

        def product(hp, c0, slot, ev, high, low, n):
            if not (isinstance(ev, int) and ev == 0):
                pe.wait_ge(S[f"evacuated{slot}"], ev)
            for c in range(n):
                pe.wait_ge(S["lo_done"], 2 * hp + c0 + c + 1)
                piece(hp, c0 + c, slot, high, low, NPIECE * c, c == 0, c == n - 1)

        def norm(c):
            for k in range(KD):
                pe.wait_ge(S["norm_sq"], KD * c + k + 1)
                for half in range(2):
                    last = pe.matmul(aux[:, half, 0:HT], const("ones"), sq[k % 2][:, half * HT:(half + 1) * HT],
                                     start=k == 0, stop=k == KD - 1)
                last.then_inc(S["norm_sum"], 1)

        pe.wait_ge(S["const_in"], 32)
        norm(0)
        pe.wait_ge(S["norm_lo"], KD)

        def a_pair(i):
            for u in range(2):
                product(HPA + 2 * i + u, 0, u, i, xh, xl, 2)

        peel(pe, N_A // 2, a_pair)
        product(HPA + N_A - 1, 0, 0, N_A // 2, xh, xl, 2)

        def l2(i):
            for u in range(2):
                m = 2 * i + u
                pe.wait_ge(S["l2_sq"], m + 1)
                if not isinstance(i, int):
                    pe.wait_ge(S["l2_ss"], m - 1)
                for half in range(2):
                    last = pe.matmul(aux[:, 2 * u + half, 0:HT], const("ones"),
                                     lq[u][:, half * HT:(half + 1) * HT], start=True, stop=True)
                last.then_inc(S["l2_sum"], 1)

        peel(pe, H, l2)
        pe.wait_ge(S["evacuated0"], EV_B[0])
        pe.wait_ge(S["l2_ss"], 2 * H)
        for n in range(NCH):
            last = pe.transpose(raw_flat[:, n * C:(n + 1) * C], bar[0:64, n * C:(n + 1) * C],
                                const("ident", 64)[:, 0:64])
        last.then_inc(S["tok_ps"], 1)
        pe.wait_ge(S["g_ready"], 1)
        pe.matmul(aux[0:64, 0, 0:NCH * H], const("upper", 64), small["gtok"][:, :], start=True, stop=True)
        pe.matmul(aux[:, 1, 0:NCH * H], const("ones", 64), small["gtok"][:, :], start=True, stop=True
                  ).then_inc(S["gc_ps"], 1)
        pe.wait_ge(S["kdec_in"], 1)
        pe.wait_ge(S["eg_done"], 1)

        def pe_wait(sem, value):
            pe.wait_ge(sem, value)
            if not isinstance(value, int):
                pe.sem_inc(S["pe_waited"])

        def delta(n):
            first = isinstance(n, int) and n == 0

            def per_head(out, left, right, start=True, stop=True):
                for h in range(H):
                    last = pe.matmul(out(h), left(h), right(h), start=start, stop=stop)
                return last

            q_h = lambda h: qkv[:, h, :]
            k_h = lambda h: qkv[:, H + h, :]
            v_h = lambda h: qkv[:, 2 * H + h, :]
            sq_h = lambda t: (lambda h: t[:, h * C:(h + 1) * C])
            bank = lambda b, rows=64: (lambda h: aux[0:rows, b, h * C:(h + 1) * C])
            wide = lambda b, rows=64: (lambda h: aux[0:rows, b + h // 4, (h % 4) * 128:(h % 4 + 1) * 128])
            pe_wait(S["gu_done"], n + 1)
            if not first:
                pe_wait(S["r_done"], n)
            pe.matmul(aux[:, 1, :], const("ones", 64), lm[:, :], start=True, stop=True).then_inc(S["gcb_ps"], 1)
            pe_wait(S["chunk_in"], 16 * n + 16)
            if not first:
                pe_wait(S["s_done"], n)
                pe_wait(S["o_copied"], n)
            per_head(bank(2), k_h, q_h)
            per_head(bank(0), k_h, k_h).then_inc(S["kq_ps"], 1)
            pe_wait(S["x1_done"], n + 1)
            for h in range(H):
                last = pe.transpose(aux[0:64, 3, h * C:(h + 1) * C], xx[:, h * C:(h + 1) * C],
                                    const("ident", 64)[:, 0:64])
            last.then_inc(S["xt_ps"], 1)
            pe_wait(S["exp_done"], 3 * n + 3)
            for h in range(H):
                last = pe.transpose(wide(0)(h), v_h(h), const("ident"))
            last.then_inc(S["v_ps"], 1)
            pe_wait(S["att_done"], n + 1)
            for l in range(1, LEVELS):
                if l == 1:
                    pe_wait(S["y1_done"], n + 1)
                else:
                    pe_wait(S["y_upd"], 5 * n + l - 1)
                    pe_wait(S["x_upd"], 4 * n + l - 1)
                pe_wait(S["lm_done"], 5 * n + l)
                per_head(bank(2), sq_h(lm), sq_h(yy)).then_inc(S["p_ps"], 1)
                if l == 1:
                    pe_wait(S["vb_done"], n + 1)
                    for h in range(H):
                        last = pe.transpose(wide(0)(h), k_h(h), const("ident"))
                    last.then_inc(S["k_ps"], 1)
                pe_wait(S["p_copied"], 5 * n + l)
                last = per_head(bank(3), sq_h(xx), sq_h(pp))
                if l < LEVELS - 1:
                    last = per_head(bank(2), sq_h(pp), sq_h(xx))
                last.then_inc(S["z_ps"], 1)
            if isinstance(n, int) and n == NP1:
                pe_wait(S["s_init"], 16)
            if first:
                pe_wait(S["pads_set"], 4)
            pe_wait(S["kd_done"], n + 1)
            per_head(wide(0), k_h, lambda h: state[:, h, :]).then_inc(S["ks_ps"], 1)
            pe_wait(S["r_done"], n + 1)
            pe_wait(S["y_upd"], 5 * n + 5)
            per_head(wide(2), sq_h(yy), lambda h: rr[:, h, :]).then_inc(S["vn_ps"], 1)
            pe_wait(S["vn_done"], n + 1)
            pe_wait(S["qg_done"], n + 1)
            for h in range(H):
                pe.matmul(bank(0, 128)(h), state[:, h, :], qg[:, h * C:(h + 1) * C], start=True, stop=False)
                last = pe.matmul(bank(0, 128)(h), vb[:, h, :], att[:, h * C:(h + 1) * C], start=False, stop=True)
            last.then_inc(S["o_ps"], 1)
            per_head(wide(2, 128), lambda h: kd[:, h, :], lambda h: vb[:, h, :]).then_inc(S["sup_ps"], 1)

        def short(j):
            hp = HPB + 3 * j
            product(hp, 0, 0, EV_B[0] + 2 * j, xh, xl, 2)
            product(hp, 2, 1, EV_B[1] + j, xh, xl, 2)
            product(hp, 4, 0, EV_B[0] + 2 * j + 1, xh, xl, 2)

        def delta_short(n):
            delta(n)
            short(n)

        peel(pe, NSC, delta_short)
        delta(NCH - 1)

        def branch(hp0, ev):
            with pe.Fori(0, KD // 2) as i:
                for u in range(2):
                    product(hp0 + 3 * i, 3 * u, 0, ev[0] + 2 * i + u, xh, xl, 2)
                    product(hp0 + 3 * i, 3 * u + 2, 1, ev[1] + 2 * i + u, yh, yl, 1)

        pe.wait_ge(S["sc_lo"], NSC)
        pe.wait_ge(S["s_done"], NCH)
        pe.wait_ge(S["o_copied"], NCH)
        branch(HPC, EV_C)

        def gated(i):
            for u in range(2):
                h = 2 * i + u
                pe.wait_ge(S["go_sq"], h + 1)
                if not isinstance(i, int):
                    pe.wait_ge(S["go_ss"], h - 1)
                for half in range(2):
                    last = pe.matmul(aux[:, 2 * u + half, 0:HT], const("ones"),
                                     gq[u][:, half * HT:(half + 1) * HT], start=True, stop=True)
                last.then_inc(S["go_sum"], 1)

        peel(pe, H // 2, gated)
        pe.wait_ge(S["go_lo"], H)
        branch(HPD, EV_D)
        pe.wait_ge(S["mg_lo"], KD)
        with pe.Fori(0, KD // 2) as i:
            for u in range(2):
                product(HPE + 2 * i + u, 0, u, EV_E[u] + i, xh, xl, 2)
        norm(1)
        pe.wait_ge(S["norm_lo"], 2 * KD)
        with pe.Fori(0, KD // 2) as i:
            for u in range(2):
                product(HPF + 2 * i + u, 0, u, EV_F[u] + i, xh, xl, 2)
        for u in range(2):
            pe.wait_ge(S[f"evacuated{u}"], EV_G[u])
        pe.wait_ge(S["keys_in"], 16)

        def scores(tb, rows):
            if tb:
                pe.wait_ge(S["scores_read"], tb)
            for hp in range(KD):
                last = pe.matmul(aux[0:rows, hp // 4, (hp % 4) * NK:(hp % 4 + 1) * NK],
                                 qf[:, hp, tb * 128:tb * 128 + rows], keys[:, hp, :], start=True, stop=True)
            last.then_inc(S["score_ps"], 1)

        def turn(tb, rows):
            pe.wait_ge(S["pick_done"], tb + 1)
            if tb:
                pe.wait_ge(S["pickT_done"], tb)
            for x, t in enumerate((pick[0], pick[1], gate)):
                last = pe.transpose(ps[1][:, 0, 128 * x:128 * x + rows],
                                    t[0:rows, :, :].rearrange("p h k -> p (h k)"), const("ident", rows)[:, 0:rows])
            last.then_inc(S["pickT_ps"], 1)

        for tb in range(TP // 128 + 1):
            scores(tb, 128 if tb < TP // 128 else TS)
            if tb:
                turn(tb - 1, 128)
        turn(TP // 128, TS)

        def gmats(i):
            for u in range(2):
                pe.wait_ge(S["onehots"], 2 * i + u + 1)
                if not isinstance(i, int):
                    pe.wait_ge(S["gmat_out"], 2 * i + u - 1)
                for c in range(4):
                    last = pe.matmul(aux[:, u, c * NK:(c + 1) * NK], oa[u][:, c, :], ob[u][:, c, :],
                                     start=True, stop=True)
                last.then_inc(S["gmat_ps"], 1)

        pe.wait_ge(S["pickT_done"], TP // 128 + 1)
        peel(pe, T // 8, gmats)

        def hidden(hp, ev0, ev1):
            for k in range(G2):
                product(hp + k, 0, k % 2, (ev0, ev1)[k % 2] + k // 2, xh, xl, 2)

        def values(hp, g, par, ev0, ev1):
            pe.wait_ge(S["m_lo"], G2 * g + G2)
            for d in range(KD // 2):
                pe.wait_ge(S["lo_done"], 2 * hp + d + 1)
                for x in range(2):
                    pe.wait_ge(S[f"evacuated{x}"], (ev0, ev1)[x] + d)
                    piece(hp, d, x, yh, yl, G2 * par, True, True, range(G2 * x, G2 * x + G2),
                          ("group_done", "piece_used")[x:])

        hidden(HPG, EV_G[0], EV_G[1])

        def step(g, hp, par):
            base = [EV_G[x] + G2 // 2 + PER_G * g for x in range(2)]
            hidden(hp, base[0], base[1])
            values(hp + G2, g, par, base[0] + G2 // 2, base[1] + G2 // 2)

        with pe.Fori(0, NG // 2 - 1) as i:
            for u in range(2):
                step(2 * i + u, HPG + G2 + 8 * (2 * i + u), u)
        hp = HPG + G2 + 8 * (NG - 2)
        step(NG - 2, hp, 0)
        values(hp + 8, NG - 1, 1, EV_END[0] - KD // 2, EV_END[1] - KD // 2)
        norm(2)

    block_context.__exit__(None, None, None)


def constants():
    t = np.zeros((128, N_CONST), np.float32)

    def put(name, value):
        a, n = CONST[name]
        t[0:value.shape[0], a:a + n] = value

    i, j = np.arange(C)[:, None], np.arange(C)[None, :]
    put("ones", np.ones((128, 128), np.float32))
    put("ident", np.eye(128, dtype=np.float32))
    put("iota", np.broadcast_to(np.arange(128, dtype=np.float32), (128, 128)))
    put("upper", (i <= j).astype(np.float32))
    put("negT", np.where(j >= i, 0.0, NEG).astype(np.float32))
    put("negL", np.where(j < i, 0.0, NEG).astype(np.float32))
    put("eye", np.eye(C, dtype=np.float32))
    put("levels", np.concatenate([((i >> (l + 1)) == (j >> (l + 1))) & ((i >> l) % 2 == 1) & ((j >> l) % 2 == 0)
                                  for l in range(LEVELS)], axis=1).astype(np.float32))
    put("iota16", np.broadcast_to(np.arange(TOPK, dtype=np.float32), (128, TOPK)))
    return t


def pieces(w):
    k, m = w.shape
    return w.reshape(k // 1024, NPIECE, 128, m // 128, 128).transpose(3, 0, 2, 1, 4).reshape(-1, 128, 1024)


def kernel(x_prompt, x_sample, state_dn, state_dn_conv, state_sc_conv, norm1_g, w_in, sc_conv_w, dn_conv_w,
           dn_a_log, dn_dt_bias, dn_norm_g, w_br_sc, w_br_dn, w_o, norm2_g, peer_wq, peer_keys, peer_u,
           peer_v, final_norm_g):
    import concourse.bacc as bacc
    from concourse.bass_utils import run_bass_kernel_spmd

    f = {n: np.asarray(a) for n, a in dict(
        x_prompt=x_prompt, x_sample=x_sample, state_dn=state_dn, state_dn_conv=state_dn_conv,
        state_sc_conv=state_sc_conv, norm1_g=norm1_g, w_in=w_in, sc_conv_w=sc_conv_w, dn_conv_w=dn_conv_w,
        dn_a_log=dn_a_log, dn_dt_bias=dn_dt_bias, dn_norm_g=dn_norm_g, w_br_sc=w_br_sc, w_br_dn=w_br_dn,
        w_o=w_o, norm2_g=norm2_g, peer_wq=peer_wq, peer_keys=peer_keys, peer_u=peer_u, peer_v=peer_v,
        final_norm_g=final_norm_g).items()}
    x = np.concatenate([f["x_prompt"][0], f["x_sample"][0]], axis=0)
    x = np.ascontiguousarray(x.T.reshape(KD, 128, T).transpose(1, 0, 2))

    w = f["w_in"][0]
    edges = np.cumsum((0, SCW, SCW, SCW, QKV, 1024, H, H, D, D))
    sc_b, sc_c, sc_h, qkv_w, z_w, beta_w, a_w, gsc_w, gdn_w = (w[:, a:b] for a, b in zip(edges, edges[1:]))
    ba = np.zeros((D, 128), np.float32)
    ba[:, 0:H] = beta_w
    ba[:, 32:32 + H] = a_w
    stream = [pieces(qkv_w), pieces(z_w), pieces(ba)]
    stream.append(np.stack([pieces(m).reshape(NSC, 2, 128, 1024) for m in (sc_c, sc_h, sc_b)], axis=1
                           ).reshape(-1, 128, 1024))
    for gate_w, branch_w in ((gsc_w, f["w_br_sc"][0]), (gdn_w, f["w_br_dn"][0])):
        stream.append(np.concatenate([pieces(gate_w).reshape(KD, 2, 128, 1024),
                                      pieces(branch_w).reshape(KD, 1, 128, 1024)], axis=1).reshape(-1, 128, 1024))
    stream += [pieces(f["w_o"][0]), pieces(f["peer_wq"][0])]
    u = f["peer_u"][0].reshape(NK, NG, G2, 2, NPIECE, 128).transpose(1, 2, 3, 5, 4, 0).reshape(NG, 2 * G2, 128, 1024)
    v = f["peer_v"][0].reshape(NK, NG, G2, KD // 2, 2, 128).transpose(1, 3, 0, 4, 2, 5).reshape(
        NG, KD // 2, 128, 1024)
    stream.append(u[0])
    for g in range(NG - 1):
        stream += [u[g + 1], v[g]]
    stream.append(v[NG - 1])
    stream = np.concatenate(stream, axis=0)
    assert stream.shape == (N_PIECES, 128, 1024)

    vec = np.zeros((128, N_VEC), np.float32)

    def put(name, value):
        a, n = VEC[name]
        vec[:, a:a + n] = value

    def columns(a, n):
        return a.reshape(a.shape[0], n, 128).transpose(2, 1, 0).reshape(128, -1)

    put("g1", columns(f["norm1_g"], KD))
    put("g2", columns(f["norm2_g"], KD))
    put("gf", columns(f["final_norm_g"][None], KD))
    put("dnw", columns(f["dn_conv_w"][0], NQKV))
    put("scw", columns(f["sc_conv_w"][0], NSC))
    put("dng", f["dn_norm_g"][0][:, None])
    put("alog", np.broadcast_to(f["dn_a_log"][0], (128, H)))
    put("dtb", np.broadcast_to(f["dn_dt_bias"][0], (128, H)))
    put("dnst", columns(f["state_dn_conv"][0, 0], NQKV))
    put("scst", columns(f["state_sc_conv"][0, 0], NSC))
    arrays = {
        "x": x, "w": stream, "vec": vec, "const": constants(),
        "s0": np.ascontiguousarray(f["state_dn"][0, 0].transpose(1, 0, 2)),
        "keys": np.ascontiguousarray(f["peer_keys"][0].reshape(KD, NK, 128).transpose(2, 0, 1)),
    }
    outs = {"y": (128, KD, T), "sp": (128, H, 128), "ss": (128, H, 128),
            "dnc": (128, NQKV, 2, DN_TAPS - 1), "scc": (128, NSC, 2, SC_TAPS - 1)}
    scratch = {"qkv_s": (NCH, 128, NQKV, C), "z_s": (NZ, 128, T), "o_s": (NCH, 128, HC),
               "gates_s": (NG, 128, NTB, G2 * TB)}

    nc = bacc.Bacc("TRN2", target_bir_lowering=False, num_devices=1)
    args = [nc.dram_tensor(f"in_{n}", a.shape, F32, kind="ExternalInput").ap() for n, a in arrays.items()]
    args += [nc.dram_tensor(f"out_{n}", s, F32, kind="ExternalOutput").ap() for n, s in outs.items()]
    args += [nc.dram_tensor(n, s, F32, kind="Internal").ap() for n, s in scratch.items()]
    trunk_program(nc, *args)
    r = run_bass_kernel_spmd(nc, [{f"in_{n}": a for n, a in arrays.items()}], core_ids=[0]).results[0]

    y = r["out_y"].transpose(2, 1, 0).reshape(T, D)
    dn = [r[f"out_{n}"].transpose(1, 0, 2)[None, None] for n in ("sp", "ss")]
    dnc = r["out_dnc"].transpose(2, 3, 1, 0).reshape(2, DN_TAPS - 1, QKV)
    scc = r["out_scc"].transpose(2, 3, 1, 0).reshape(2, SC_TAPS - 1, SCW)
    out = (y[None, 0:TP], y[None, TP:], dn[0], dnc[None, None, 0], scc[None, None, 0],
           dn[1], dnc[None, None, 1], scc[None, None, 1])
    return tuple(np.ascontiguousarray(a) for a in out)
```

```python
import concourse.bass as bass
import numpy as np
from concourse import mybir

F32 = mybir.dt.float32
F32R = mybir.dt.float32r
U32 = mybir.dt.uint32
ALU = mybir.AluOpType
ACT = mybir.ActivationFunctionType
AX_X = mybir.AxisListType.X

D = 2048
TP, TS = 512, 64
T = TP + TS
HT = T // 2
KD = D // 128
C = 64
NCH = T // C
H = 8
HC = H * C
SCW, SC_TAPS = 1024, 3
QKV, DN_TAPS = 3072, 4
NSC, NQKV, NZ = SCW // 128, QKV // 128, 1024 // 128
DK = 128
NK = 128
TOPK = 16
HK = H * TOPK
G2 = 4
NG = NK // G2
TB = 36
NTB = T // TB
EPS = 1e-6
NEG = -1e30
LEVELS = 6
NPIECE = 8
FILL = 12
EARLY = 4
BLOCKS = (0, 128, 256, 384, T - 128)
NBL = len(BLOCKS)

P_A = 0
N_A = NQKV + 1
P_B = P_A + 2 * N_A
P_C = P_B + 6 * NSC
P_Z = P_C + 3 * KD
P_D = P_Z + 2 * NZ
P_E = P_D + 3 * KD
P_F = P_E + 2 * KD
P_G = P_F + 2 * KD
N_PIECES = P_G + 2 * 2 * G2 * NG

CONST = {}
_at = 0
for _name, _width in (("ones", 128), ("ident", 128), ("iota", 128), ("upper", C), ("negT", C), ("negL", C),
                      ("eye", C), ("levels", LEVELS * C), ("iota16", TOPK)):
    CONST[_name] = (_at, _width)
    _at += _width
N_CONST = _at
VEC = {}
_at = 0
for _name, _width in (("g1", KD), ("g2", KD), ("gf", KD), ("dnw", NQKV * DN_TAPS), ("scw", NSC * SC_TAPS),
                      ("dng", 1), ("alog", H), ("dtb", H), ("dnst", NQKV * (DN_TAPS - 1)),
                      ("scst", NSC * (SC_TAPS - 1))):
    VEC[_name] = (_at, _width)
    _at += _width
N_VEC = _at


def trunk_program(nc, x_in, w_in, vec_in, const_in, s0_in, keys_in, y_out, sp_out, ss_out, dnc_out, scc_out,
                  qkv_d, z_d, o_d, half_d, gates_d, hid_d):
    base = -(-nc.sbuf_base // 64) * 64
    CH = T * 4
    at = {}
    pos = base
    for name, size in (("XH", KD * CH), ("XL", KD * CH), ("MG", KD * CH), ("W", 6 * 4096), ("CV", 4 * N_CONST),
                       ("VV", 4 * N_VEC), ("TAIL", 4 * (NQKV * 6 + NSC * 4)), ("Y", KD * CH)):
        at[name] = pos
        pos += -(-size // 64) * 64
    at["L"] = pos
    end = nc.sbuf_usable_end

    def sb(name, shape, dtype, offset):
        size = int(np.prod(shape[1:])) * 4
        assert offset + size <= end, (name, offset + size, end)
        return nc.alloc_sbuf_tensor_at(name, shape, dtype, offset=offset)

    class Region:
        def __init__(self, offset, limit):
            self.pos, self.limit = offset, limit

        def take(self, name, shape, dtype=F32):
            t = sb(name, shape, dtype, self.pos)
            self.pos += -(-int(np.prod(shape[1:])) * 4 // 32) * 32
            assert self.pos <= self.limit, (name, self.pos, self.limit)
            return t

    xh = sb("xh", [128, KD, T], F32R, at["XH"])
    xl = sb("xl", [128, KD, T], F32R, at["XL"])
    mg = sb("mg", [128, KD, T], F32, at["MG"])
    yh = sb("yh", [128, NSC, T], F32R, at["Y"])
    yl = sb("yl", [128, NSC, T], F32R, at["Y"] + NSC * CH)
    wr = [sb(f"wr{i}", [128, NPIECE, 128], F32, at["W"] + 4096 * i) for i in range(2)]
    wh = [sb(f"wh{i}", [128, NPIECE, 128], F32R, at["W"] + 4096 * (2 + i)) for i in range(2)]
    wl = [sb(f"wl{i}", [128, NPIECE, 128], F32R, at["W"] + 4096 * (4 + i)) for i in range(2)]
    cst = sb("cst", [128, N_CONST], F32, at["CV"])
    vec = sb("vec", [128, N_VEC], F32, at["VV"])
    tail = sb("tail", [128, NQKV, 2, DN_TAPS - 1], F32, at["TAIL"])
    sctail = sb("sctail", [128, NSC, 2, SC_TAPS - 1], F32, at["TAIL"] + 4 * NQKV * 6)

    def const(name, rows=128):
        a, n = CONST[name]
        return cst[0:rows, a:a + n]

    def vector(name, j=None, n=1):
        a, m = VEC[name]
        return vec[:, a:a + m] if j is None else vec[:, bass.ds(a + j, n)]

    r = Region(at["L"], end)
    sq = [r.take(f"sq{i}", [128, T]) for i in range(2)]
    nt = [r.take(f"nt{i}", [128, T]) for i in range(2)]
    ms, rst = r.take("ms", [128, T]), r.take("rst", [128, T])
    r = Region(at["L"], end)
    AW = T + 2 * (DN_TAPS - 1)
    bar = r.take("bar", [128, T])
    cbuf = [r.take(f"cbuf{i}", [128, AW]) for i in range(2)]
    cv = [r.take(f"cv{i}", [128, AW]) for i in range(2)]
    sv = [r.take(f"sv{i}", [128, T]) for i in range(2)]
    r = Region(at["L"] + CH, end)
    lq = [r.take(f"lq{i}", [128, T]) for i in range(2)]
    ln = [r.take(f"ln{i}", [128, T]) for i in range(2)]
    lo_ = [r.take(f"lo{i}", [128, T]) for i in range(2)]
    r = Region(at["L"] + CH, end)
    SW = T + 2 * (SC_TAPS - 1)
    places = [r.pos]
    ctmp = r.take("ctmp", [128, T])
    places.append(r.pos)
    scb = r.take("scb", [128, SW])
    places.append(r.pos)
    scv = r.take("scv", [128, SW])
    places.append(r.pos)
    yt = r.take("yt", [128, T])
    csg = [sb(f"csg{i}", [128, T], F32, places[i]) for i in range(2)]
    cm = [sb(f"cm{i}", [128, T], F32, places[2 + i]) for i in range(2)]
    small = {n: r.take(n, [64, NCH * H]) for n in ("beta", "gtok", "gcum", "eg", "nbeg", "kdec", "sp1", "sp2")}
    egl = r.take("egl", [128, NCH * H])
    decay = r.take("decay", [64, H])
    xx = r.take("xx", [64, HC])
    yy = r.take("yy", [64, HC])
    lm = r.take("lm", [64, HC])
    pp = r.take("pp", [64, HC])
    oo = r.take("oo", [128, HC])
    m = Region(at["MG"], at["MG"] + KD * CH)
    qkv = m.take("qkv", [128, NQKV, C])
    state = m.take("state", [128, H, 128])
    sdec = m.take("sdec", [128, H, 128])
    vb = m.take("vb", [64, H, 128])
    kd = m.take("kd", [64, H, 128])
    rr = m.take("rr", [64, H, 128])
    el = m.take("el", [64, HC])
    ll = m.take("ll", [64, HC])
    att = m.take("att", [64, HC])
    m = Region(r.pos, end)
    egb = m.take("egb", [128, HC])
    qg = m.take("qg", [128, HC])
    r = Region(at["L"], end)
    sg = [r.take(f"sg{i}", [128, T]) for i in range(2)]
    dt = [r.take(f"dt{i}", [128, T]) for i in range(2)]
    xr = [r.take(f"xr{i}", [128, T]) for i in range(2)]
    hb = [r.take(f"hb{i}", [128, T]) for i in range(2)]
    r = Region(at["L"], end)
    go = [r.take(f"go{i}", [128, T]) for i in range(2)]
    gz = [r.take(f"gz{i}", [128, T]) for i in range(2)]
    gq = [r.take(f"gq{i}", [128, T]) for i in range(2)]
    gr = [r.take(f"gr{i}", [128, T]) for i in range(2)]
    gt_ = [r.take(f"gt_{i}", [128, T]) for i in range(2)]
    idx_at = (end - 3 * CH) // 64 * 64
    r = Region(idx_at, end)
    idxT = [r.take(n, [128, T]) for n in ("i1T", "i2T", "gateT")]
    r = Region(at["Y"], idx_at)
    keys = r.take("keys", [128, KD, NK])
    qh = [r.take(f"qh{i}", [128, T]) for i in range(2)]
    cand = r.take("cand", [128, NBL, TOPK, TOPK])
    mrall = sb("mrall", [128, NBL, 2, NK], F32, r.pos)
    sel = r.take("sel", [128, NBL, TOPK, TOPK])
    sel2 = r.take("sel2", [128, NBL, TOPK, TOPK])
    tv = r.take("tv", [128, NBL, 2, TOPK])
    ti = r.take("ti", [128, NBL, 2, TOPK], U32)
    tif = r.take("tif", [128, NBL, 2, TOPK])
    best = r.take("best", [128, NBL, TOPK])
    posu = r.take("posu", [128, NBL, TOPK], U32)
    posi = [r.take(f"posi{i}", [128, NBL, TOPK], U32) for i in range(2)]
    posf = [r.take(f"posf{i}", [128, NBL, TOPK]) for i in range(2)]
    pick = [r.take(f"pick{i}", [128, NBL, H, TOPK]) for i in range(2)]
    gate = r.take("gate", [128, NBL, H, TOPK])
    gsum = r.take("gsum", [128, NBL * H])
    GB = NK * TB * 4
    r = Region(at["Y"] + 2 * GB, idx_at)
    oa = [r.take(f"oa{i}", [128, 4, NK]) for i in range(2)]
    ob = [r.take(f"ob{i}", [128, 4, NK]) for i in range(2)]
    gbuf = [sb(f"gbuf{i}", [128, NK, TB], F32, at["Y"] + i * GB) for i in range(2)]
    r = Region(at["L"], end)
    gtile = [r.take(f"gtile{i}", [128, NTB, G2, TB]) for i in range(2)]
    mm = [r.take(f"mm{i}", [128, T]) for i in range(2)]
    gl_at = (idx_at - 2 * CH) // 64 * 64
    assert r.pos <= gl_at
    gl = [sb(f"gl{i}", [128, T], F32, gl_at + i * CH) for i in range(2)]
    assert at["Y"] + 2 * GB + 4 * 4 * NK * 4 <= gl_at

    ps = [nc.alloc_psum_tensor(f"ps{i}", [128, 2, 512], F32) for i in range(2)]
    aux = nc.alloc_psum_tensor("aux", [128, 4, 512], F32)
    raw_flat = aux[0:64, 2:4, :].rearrange("p a b -> p (a b)")[:, 0:T]
    raw_tok = raw_flat.rearrange("p (n c) -> p n c", c=C)

    names = """raw_full0 raw_full1 hi_done lo_done piece_used group_done evacuated0 evacuated1
        const_in x_loaded norm_sq norm_sum norm_ms norm_root norm_inv norm_scaled norm_hi norm_lo
        conv_step conv_done silu_done pads_set kept_sv0 kept_sv1
        l2_sq l2_sum l2_ss l2_root l2_inv l2_out kept_qk0 kept_qk1
        tok_ps beta_done sp_in sp_exp sp_one sp_ln sp_max decay_exp g_ready gc_ps gcum_done kdec_in kdec_done eg_done
        nbeg_done chunk_in s_init gu_done gcb_ps kq_ps masked_raw masked exp_done
        att_done l_raw l_done x1_in x1_done xt_ps y1_done qg_done lm_done p_ps p_copied z_ps y_upd x_upd
        v_ps vb_done k_ps kd_done sdec_done ks_ps r_raw r_done vn_ps vn_done o_ps o_copied o_kept
        sup_ps s_done s_kept sc_step sc_hi sc_lo
        half_kept0 half_kept1 merged hb_in0 hb_in1 kept_z0 kept_z1 z_read go_in0 go_in1 go_sq go_sum go_ss go_root go_inv go_raw go_scaled go_hi go_lo
        mg_hi mg_lo xr_in0 xr_in1 keys_in score_ps topk_step scores_read shifted picked gsum_step gate_exp pick_done pickT_ps
        pickT_done onehots gmat_ps gmat_out gates_kept0 gates_kept1
        gt_in0 gt_in1 hid_kept0 hid_kept1 gl_in0 gl_in1 m_done m_hi m_lo tails_kept y_kept0 y_kept1 dve_waited pe_waited""".split()
    S = {n: nc.alloc_semaphore(n) for n in names}

    def halves(t):
        return t.rearrange("p (a b) -> p a b", a=2)

    def both(slot):
        return ps[slot][:, :, 0:HT]

    def heads(t, n=C):
        return t.rearrange("p (h n) -> p h n", n=n)

    def pair(b):
        return aux[0:64, b:b + 2, :].rearrange("p a (h n) -> p (a h) n", n=128)

    def chunks(eng, run):
        run(0, "B", 0)
        with eng.Fori(1, NSC // 2) as n:
            run(n, "B", n)
        run(NSC // 2, "C", 0)
        with eng.Fori(NSC // 2 + 1, NSC) as n:
            run(n, "C", n - NSC // 2)
        run(NCH - 1, "Z", 0)

    def fill_base(kind, i):
        return {"B": HPB, "C": HPC, "Z": HPZ}[kind] + FILL // 2 * i

    def peel(eng, n, body):
        body(0)
        with eng.Fori(1, n) as i:
            body(i)

    EV_B = (N_A // 2 + 1, N_A // 2)
    EV_C = (EV_B[0] + 2 * NSC, EV_B[1] + NSC)
    EV_Z = (EV_C[0] + KD, EV_C[1] + KD)
    EV_D = (EV_Z[0] + NZ // 2, EV_Z[1] + NZ // 2)
    EV_E = (EV_D[0] + KD, EV_D[1] + KD)
    EV_F = (EV_E[0] + KD // 2, EV_E[1] + KD // 2)
    EV_G = (EV_F[0] + KD // 2, EV_F[1] + KD // 2)
    PER_G = (G2 + KD) // 2
    EV_END = (EV_G[0] + NG * PER_G, EV_G[1] + NG * PER_G)
    HPA, HPB, HPC, HPZ, HPD, HPE, HPF, HPG = (p // 2 for p in (P_A, P_B, P_C, P_Z, P_D, P_E, P_F, P_G))
    HPV = HPG + EARLY * G2
    HPS = HPV + (EARLY - 1) * 4
    EV_V = (EV_G[0] + EARLY * G2 // 2, EV_G[1] + EARLY * G2 // 2)
    EV_S = tuple(e + (EARLY - 1) * KD // 2 for e in EV_V)
    UNITS = TB // 4
    NP1 = NCH - 1

    block_context = nc.Block()
    block = block_context.__enter__()

    @block.sync
    def _(sp):
        def load(hp, slot):
            if not (isinstance(hp, int) and hp == 0):
                sp.wait_ge(S["lo_done"], 2 * hp + slot - 1)
            sp.dma_start(wr[slot][:, :, :].rearrange("p a n -> p (a n)"), w_in[2 * hp + slot, :, :]
                         ).then_inc(S[f"raw_full{slot}"], 16)

        def loads(hp, n, c0=0):
            for c in range(c0, c0 + n):
                load(hp + 2 + c // 2, c % 2)

        sp.dma_start(cst[:, :], const_in).then_inc(S["const_in"], 16)
        sp.dma_start(vec[:, :], vec_in).then_inc(S["const_in"], 16)
        sp.dma_start(mg[:, :, :], x_in).then_inc(S["x_loaded"], 16)
        for p in range(4):
            load(p // 2, p % 2)

        with sp.Fori(0, H) as i:
            loads(HPA + 2 * i, 4)
        with sp.Fori(0, H // 2) as i:
            for u in range(2):
                loads(HPA + 16 + 2 * i + u, 2)
                sp.wait_ge(S["silu_done"], 17 + 2 * i + u)
                sp.dma_start(qkv_d[:, :, 16 + 2 * i + u, :].rearrange("n p c -> p n c"),
                             sv[u][:, :].rearrange("p (n c) -> p n c", c=C)).then_inc(S[f"kept_sv{u}"], 16)
        loads(HPA + 24, 2)
        sp.dma_start(dnc_out, tail[:, :, :, :]).then_inc(S["tails_kept"], 16)
        with sp.Fori(0, H) as i:
            for u in range(2):
                sp.wait_ge(S["l2_out"], 2 * i + u + 1)
                sp.dma_start(qkv_d[:, :, 2 * i + u, :].rearrange("n p c -> p n c"),
                             lo_[u][:, :].rearrange("p (n c) -> p n c", c=C)).then_inc(S[f"kept_qk{u}"], 16)
        for u in range(2):
            sp.wait_ge(S[f"kept_sv{u}"], 16 * H // 2)
            sp.wait_ge(S[f"kept_qk{u}"], 16 * H)

        def chunk_load(n):
            sp.dma_start(qkv[:, :, :], qkv_d[n, :, :, :]).then_inc(S["chunk_in"], 16)

        def chunk_store(n):
            sp.wait_ge(S["o_copied"], n + 1)
            sp.dma_start(o_d[n, :, :], oo[:, :]).then_inc(S["o_kept"], 16)

        def run(n, kind, i):
            hp = fill_base(kind, i)
            last = kind == "Z"

            def half_store(s):
                u = s % 2
                sp.wait_ge(S["evacuated1"], EV_C[1] + 4 * i + s + 1)
                sp.dma_start(half_d[4 * i + s, :, :], cm[u][:, :]).then_inc(S[f"half_kept{u}"], 16)

            def z_store(m):
                u = m % 2
                sp.wait_ge(S[f"evacuated{u}"], EV_Z[u] + m // 2 + 1)
                sp.dma_start(z_d[m, :, :], csg[u][:, :]).then_inc(S[f"kept_z{u}"], 16)

            for k in range(FILL):
                if k == 9 and not last:
                    sp.wait_ge(S["ks_ps"], n + 1)
                    sp.wait_ge(S["qg_done"], n + 1)
                    chunk_load(n + 1)
                if k == 11:
                    chunk_store(n)
                loads(hp, 1, k)
                if kind == "C" and k % 3 == 0 and k:
                    half_store(k // 3 - 1)
                if kind == "Z" and k % 2 == 0 and k:
                    z_store(k // 2 - 1)
                if last and k == 0:
                    sp.wait_ge(S["s_done"], NP1)
                    sp.dma_start(sp_out, state[:, :, :]).then_inc(S["s_kept"], 16)
                    sp.wait_ge(S["s_kept"], 16)
                    sp.dma_start(state[:, :, :], s0_in).then_inc(S["s_init"], 16)
            if kind == "C":
                half_store(3)
            if kind == "Z":
                z_store(FILL // 2 - 1)
                for m in range(FILL // 2, NZ):
                    loads(hp + m, 2)
                    z_store(m)

        chunk_load(0)
        chunks(sp, run)
        sp.wait_ge(S["s_done"], NCH)
        sp.dma_start(ss_out, state[:, :, :]).then_inc(S["s_kept"], 16)
        sp.wait_ge(S["sc_lo"], NSC)
        sp.dma_start(scc_out, sctail[:, :, :, :]).then_inc(S["tails_kept"], 16)
        for u in range(2):
            sp.wait_ge(S[f"kept_z{u}"], 16 * NZ // 2)
            sp.wait_ge(S[f"half_kept{u}"], 16 * KD // 2)
        sp.wait_ge(S["o_kept"], 16 * NCH)

        def head_load(i):
            for u in range(2):
                if not isinstance(i, int):
                    sp.wait_ge(S["go_scaled"], 2 * i + u - 1)
                sp.dma_start(go[u][:, :].rearrange("p (n c) -> p n c", c=C),
                             o_d[:, :, bass.ds((2 * i + u) * C, C)].rearrange("n p c -> p n c")
                             ).then_inc(S[f"go_in{u}"], 16)
                sp.dma_start(gz[u][:, :], z_d[2 * i + u, :, :]).then_inc(S[f"go_in{u}"], 16)

        peel(sp, H // 2, head_load)

        def half_again(i):
            for u in range(2):
                loads(HPD + 3 * i, 3, 3 * u)
                if isinstance(i, int):
                    sp.wait_ge(S["go_lo"], H)
                else:
                    sp.wait_ge(S["merged"], 2 * i + u - 1)
                sp.dma_start(hb[u][:, :], half_d[2 * i + u, :, :]).then_inc(S[f"hb_in{u}"], 16)

        peel(sp, KD // 2, half_again)

        def x_again(i):
            for u in range(2):
                loads(HPE + 2 * i + u, 2)
                if isinstance(i, int):
                    sp.wait_ge(S["mg_lo"], KD)
                else:
                    sp.wait_ge(S[f"evacuated{u}"], EV_E[u] + i)
                sp.dma_start(xr[u][:, :], x_in[:, 2 * i + u, :]).then_inc(S[f"xr_in{u}"], 16)

        peel(sp, KD // 2, x_again)
        sp.dma_start(keys[:, :, :], keys_in).then_inc(S["keys_in"], 16)
        with sp.Fori(0, KD // 2) as i:
            loads(HPF + 2 * i, 4)

        with sp.Fori(0, NTB // 2) as i:
            for u in range(2):
                loads(HPG + 2 * i + u, 2)
                sp.wait_ge(S["gmat_out"], UNITS * (2 * i + u + 1))
                sp.dma_start(gates_d[:, :, 2 * i + u, :].rearrange("g p n -> p g n"),
                             gbuf[u][:, :, :].rearrange("p (g i) t -> p g (i t)", i=G2)
                             ).then_inc(S[f"gates_kept{u}"], 16)
                sp.wait_ge(S[f"evacuated{u}"], EV_G[u] + i + 1)
                sp.dma_start(hid_d[2 * i + u, :, :], gl[u][:, :]).then_inc(S[f"hid_kept{u}"], 16)
        for u in range(2):
            sp.wait_ge(S[f"gates_kept{u}"], 16 * NTB // 2)
            sp.wait_ge(S[f"hid_kept{u}"], 16 * NTB // 2)

        def gate_load(g, u):
            if not (isinstance(g, int) and g < 2):
                sp.wait_ge(S["m_done"], G2 * (g - 1))
            sp.dma_start(gtile[u][:, :, :, :].rearrange("p a i t -> p a (i t)"), gates_d[g, :, :, :]
                         ).then_inc(S[f"gt_in{u}"], 16)

        def hidden_load(g):
            for k in range(G2):
                if G2 * g + k >= 2:
                    sp.wait_ge(S["m_done"], G2 * g + k - 1)
                sp.dma_start(gl[k % 2][:, :], hid_d[G2 * g + k, :, :]).then_inc(S[f"gl_in{k % 2}"], 16)

        gate_load(0, 0)
        gate_load(1, 1)
        hidden_load(0)
        hidden_load(1)
        for g in range(EARLY - 1):
            gate_load(g + 2, g % 2)
            loads(HPV + 4 * g, 8)
            if g + 2 < EARLY:
                hidden_load(g + 2)

        def step(g, hp, par):
            loads(hp, 2 * G2)
            gate_load(g + 2, par)
            loads(hp + G2, 2 * G2)

        with sp.Fori(0, (NG - EARLY) // 2 - 1) as i:
            for u in range(2):
                step(EARLY - 1 + 2 * i + u, HPS + 8 * (2 * i + u), 1 - u)
        step(NG - 3, HPS + 8 * (NG - 2 - EARLY), 1)
        loads(HPS + 8 * (NG - 1 - EARLY), 16)
        loads(HPS + 8 * (NG - EARLY), 4)

        def y_store(i):
            for u in range(2):
                sp.wait_ge(S["norm_scaled"], 2 * KD + 2 * i + u + 1)
                sp.dma_start(y_out[:, 2 * i + u, :], nt[u][:, :]).then_inc(S[f"y_kept{u}"], 16)

        with sp.Fori(0, KD // 2) as i:
            y_store(i)
        for u in range(2):
            sp.wait_ge(S[f"y_kept{u}"], 16 * KD // 2)
        sp.wait_ge(S["s_kept"], 32)
        sp.wait_ge(S["tails_kept"], 32)

    @block.gpsimd
    def _(pool):
        with pool.Fori(0, N_PIECES // 2) as i:
            for u in range(2):
                pool.wait_ge(S["hi_done"], 2 * i + u + 1)
                pool.tensor_tensor(wl[u][:, :, :], wr[u][:, :, :], wh[u][:, :, :].bitcast(F32),
                                   ALU.subtract).then_inc(S["lo_done"], 1)

    @block.scalar
    def _(act):
        def hi(hp, slot):
            act.wait_ge(S[f"raw_full{slot}"], 16 * hp + 16)
            if not (isinstance(hp, int) and hp == 0):
                act.wait_ge(S["piece_used"], 2 * hp + slot - 1)
            act.activation(wh[slot][:, :, :], wr[slot][:, :, :], ACT.Copy).then_inc(S["hi_done"], 1)

        def his(hp, n, c0=0):
            for c in range(c0, c0 + n):
                hi(hp + 1 + c // 2, c % 2)

        def norm(c, ready):
            ready()
            for k in range(KD):
                if k >= 2:
                    act.wait_ge(S["norm_sum"], KD * c + k - 1)
                act.activation(sq[k % 2][:, :], mg[:, k, :], ACT.Square).then_inc(S["norm_sq"], 1)
            act.wait_ge(S["norm_ms"], c + 1)
            act.activation(rst[:, :], ms[:, :], ACT.Sqrt).then_inc(S["norm_root"], 1)
            if c < 2:
                for k in range(KD):
                    act.wait_ge(S["norm_scaled"], KD * c + k + 1)
                    act.activation(xh[:, k, :], nt[k % 2][:, :], ACT.Copy).then_inc(S["norm_hi"], 1)

        for u in range(2):
            hi(0, u)
        norm(0, lambda: (act.wait_ge(S["x_loaded"], 16), act.wait_ge(S["const_in"], 32)))

        def qkv_in(m, i, u, piece, ev, first):
            his(piece, 2)
            act.wait_ge(S["piece_used"], 2 * piece + 2)
            if first:
                act.wait_ge(S["pads_set"], 2)
            else:
                act.wait_ge(S["conv_done"], m - 1)
            a, n = VEC["dnst"]
            w = DN_TAPS - 1
            act.activation(cbuf[u][:, w:w + HT], ps[u][:, 0, 0:HT], ACT.Copy)
            act.activation(cbuf[u][:, w + HT:w + TP], ps[u][:, 1, 0:TP - HT], ACT.Copy)
            act.activation(cbuf[u][:, w + TP:2 * w + TP], vec[:, bass.ds(a + m * w, w)], ACT.Copy)
            act.activation(cbuf[u][:, 2 * w + TP:AW], ps[u][:, 1, TP - HT:HT], ACT.Copy)
            act.activation(tail[:, m, :, :], ps[u][:, 1, HT - 2 * TS:HT].rearrange(
                "p (a b) -> p a b", a=2)[:, :, TS - w:TS], ACT.Copy).then_inc(S[f"evacuated{u}"], 1)

        def silu_out(m, u, out):
            act.wait_ge(S["conv_done"], m + 1)
            w = DN_TAPS - 1
            act.activation(out[:, 0:TP], cv[u][:, 0:TP], ACT.Silu)
            act.activation(out[:, TP:T], cv[u][:, TP + w:T + w], ACT.Silu).then_inc(S["silu_done"], 1)

        def qk_unit(i):
            for u in range(2):
                m = 2 * i + u
                qkv_in(m, i, u, HPA + m, i, isinstance(i, int))
                if isinstance(i, int) and u == 0:
                    act.wait_ge(S["norm_lo"], KD)
                silu_out(m, u, mg[:, m, :])

        peel(act, H, qk_unit)

        def v_unit(i):
            for u in range(2):
                m = 16 + 2 * i + u
                qkv_in(m, i, u, HPA + m, i, False)
                if not isinstance(i, int):
                    act.wait_ge(S[f"kept_sv{u}"], 16 * i)
                silu_out(m, u, sv[u])

        peel(act, H // 2, v_unit)
        his(HPA + 24, 2)
        act.wait_ge(S["piece_used"], P_B)
        act.activation(halves(bar[:, :]), both(0), ACT.Copy).then_inc(S["evacuated0"], 1)

        for u in range(2):
            act.wait_ge(S[f"kept_sv{u}"], 16 * H // 2)

        def l2_unit(i):
            for u in range(2):
                m = 2 * i + u
                if not isinstance(i, int):
                    act.wait_ge(S["l2_sum"], m - 1)
                    act.wait_ge(S[f"kept_qk{u}"], 16 * i)
                act.activation(lq[u][:, :], mg[:, m, :], ACT.Square).then_inc(S["l2_sq"], 1)
            for u in range(2):
                m = 2 * i + u
                act.wait_ge(S["l2_ss"], m + 1)
                act.activation(ln[u][:, :], ln[u][:, :], ACT.Sqrt).then_inc(S["l2_root"], 1)

        act.wait_ge(S["silu_done"], 16)
        peel(act, H, l2_unit)

        act.wait_ge(S["tok_ps"], 1)
        for u in range(2):
            act.wait_ge(S[f"kept_qk{u}"], 16 * H)
        act.activation(heads(small["beta"][:, :], H), raw_tok[:, :, 0:H], ACT.Sigmoid).then_inc(S["beta_done"], 1)
        act.activation(decay[:, :], vector("alog")[0:64, :], ACT.Exp).then_inc(S["decay_exp"], 1)
        act.wait_ge(S["sp_in"], 1)
        act.activation(small["sp2"][:, :], small["sp2"][:, :], ACT.Exp, scale=-1.0).then_inc(S["sp_exp"], 1)
        act.wait_ge(S["sp_one"], 1)
        act.activation(small["sp2"][:, :], small["sp2"][:, :], ACT.Ln).then_inc(S["sp_ln"], 1)
        act.wait_ge(S["gc_ps"], 1)
        act.activation(small["eg"][:, :], aux[0:64, 0, 0:NCH * H], ACT.Exp)
        act.activation(egl[:, :], aux[:, 1, 0:NCH * H], ACT.Exp).then_inc(S["eg_done"], 1)
        act.wait_ge(S["kdec_in"], 1)
        act.activation(small["kdec"][:, :], small["kdec"][:, :], ACT.Exp).then_inc(S["kdec_done"], 1)

        def fill(k, kind, i):
            hp = fill_base(kind, i)
            his(hp, 1, k)
            if kind == "B":
                j = 2 * i + k // 6
                if k % 6 == 1:
                    act.wait_ge(S["evacuated1"], EV_B[1] + j)
                    act.wait_ge(S["piece_used"], 2 * hp + k + 1)
                    act.activation(halves(ctmp[:, :]), both(0), ACT.Copy).then_inc(S["evacuated0"], 1)
                if k in (6, 11):
                    j = 2 * i + k // 7
                    act.wait_ge(S["evacuated0"], EV_B[0] + 2 * j + 2)
                    act.activation(yh[:, j, :], yt[:, :], ACT.Copy).then_inc(S["sc_hi"], 1)
            if kind == "C" and k % 3 == 1:
                m = 4 * i + k // 3
                act.wait_ge(S["evacuated1"], EV_C[1] + m - 1)
                act.wait_ge(S["piece_used"], 2 * hp + k + 1)
                act.activation(halves(csg[k // 3 % 2][:, :]), both(0), ACT.Sigmoid).then_inc(S["evacuated0"], 1)
            if kind == "Z" and k % 2 == 1:
                z_out(k // 2, 2 * hp + k + 1)

        def z_out(m, used):
            u = m % 2
            act.wait_ge(S["evacuated1"], EV_Z[1])
            if m >= 2:
                act.wait_ge(S[f"kept_z{u}"], 16 * (m // 2))
            act.wait_ge(S["piece_used"], used)
            act.activation(halves(csg[u][:, :]), both(u), ACT.Silu).then_inc(S[f"evacuated{u}"], 1)

        def delta(n, kind, i):
            act.wait_ge(S["masked"], 2 * n + 1)
            act.activation(pp[:, :], pp[:, :], ACT.Exp).then_inc(S["exp_done"], 1)
            act.wait_ge(S["masked"], 2 * n + 2)
            act.activation(el[:, :], el[:, :], ACT.Exp).then_inc(S["exp_done"], 1)
            act.activation(egb[:, :], aux[:, 1, :], ACT.Exp).then_inc(S["exp_done"], 1)
            fill(0, kind, i)
            act.wait_ge(S["xt_ps"], n + 1)
            act.activation(yy[:, :], aux[0:64, 3, :], ACT.Copy).then_inc(S["y1_done"], 1)
            fill(1, kind, i)
            fills = {1: (2, 3), 2: (4,), 3: (5, 6), 4: (7,), 5: (8,)}
            for l in range(1, LEVELS):
                act.wait_ge(S["p_ps"], 5 * n + l)
                act.activation(pp[:, :], aux[0:64, 2, :], ACT.Copy).then_inc(S["p_copied"], 1)
                for k in fills[l]:
                    fill(k, kind, i)
            fill(9, kind, i)
            act.wait_ge(S["vn_ps"], n + 1)
            act.activation(vb[:, :, :], pair(2), ACT.Copy).then_inc(S["vn_done"], 1)
            fill(10, kind, i)
            if not (isinstance(n, int) and n == 0):
                act.wait_ge(S["o_kept"], 16 * n)
            act.wait_ge(S["o_ps"], n + 1)
            act.activation(oo[:, :], aux[:, 0, :], ACT.Copy).then_inc(S["o_copied"], 1)
            fill(11, kind, i)

        chunks(act, delta)
        for m in range(FILL // 2, NZ):
            his(HPZ + m, 2)
            z_out(m, 2 * (HPZ + m) + 2)

        def gates(hp, i, ev):
            for u in range(2):
                his(hp, 2, 3 * u)
                if not isinstance(i, int):
                    act.wait_ge(S["evacuated1"], ev[1] + 2 * i + u - 1)
                act.wait_ge(S["piece_used"], 2 * hp + 3 * u + 2)
                act.activation(halves(sg[u][:, :]), both(0), ACT.Sigmoid).then_inc(S["evacuated0"], 1)
                his(hp, 1, 3 * u + 2)

        act.wait_ge(S["o_kept"], 16 * NCH)
        act.wait_ge(S["sc_lo"], NSC)
        act.wait_ge(S["s_done"], NCH)
        for u in range(2):
            act.wait_ge(S[f"kept_z{u}"], 16 * NZ // 2)
            act.wait_ge(S[f"half_kept{u}"], 16 * KD // 2)

        act.wait_ge(S["piece_used"], P_Z)

        def gated(i):
            for u in range(2):
                h = 2 * i + u
                act.wait_ge(S[f"go_in{u}"], 32 * i + 32)
                if not isinstance(i, int):
                    act.wait_ge(S["go_sum"], h - 1)
                act.activation(gq[u][:, :], go[u][:, :], ACT.Square).then_inc(S["go_sq"], 1)
            for u in range(2):
                act.wait_ge(S["go_ss"], 2 * i + u + 1)
                act.activation(gr[u][:, :], gr[u][:, :], ACT.Sqrt).then_inc(S["go_root"], 1)
            for u in range(2):
                act.wait_ge(S["go_scaled"], 2 * i + u + 1)
                act.activation(yh[:, 2 * i + u, :], gt_[u][:, :], ACT.Copy).then_inc(S["go_hi"], 1)

        peel(act, H // 2, gated)
        act.wait_ge(S["go_lo"], H)
        peel(act, KD // 2, lambda i: gates(HPD + 3 * i, i, EV_D))
        act.wait_ge(S["piece_used"], P_E)
        act.wait_ge(S["merged"], KD)
        for k in range(KD):
            act.activation(xh[:, k, :], mg[:, k, :], ACT.Copy).then_inc(S["mg_hi"], 1)
        with act.Fori(0, KD // 2) as i:
            his(HPE + 2 * i, 4)
        norm(1, lambda: (act.wait_ge(S["evacuated0"], EV_F[0]), act.wait_ge(S["evacuated1"], EV_F[1])))

        def queries(h):
            for u in range(2):
                his(HPF + 2 * h + u, 2)
                if not isinstance(h, int):
                    act.wait_ge(S["score_ps"], h)
                act.wait_ge(S["piece_used"], P_F + 4 * h + 2 * u + 2)
                act.activation(halves(qh[u][:, :]), both(u), ACT.Copy).then_inc(S[f"evacuated{u}"], 1)

        peel(act, H, queries)
        act.wait_ge(S["shifted"], H)
        act.activation(gate[:, :, :, :], gate[:, :, :, :], ACT.Exp).then_inc(S["gate_exp"], 1)
        act.wait_ge(S["pickT_ps"], 1)
        flat = aux[:, :, :].rearrange("p a b -> p (a b)")
        for x in range(3):
            c = 128 * NBL * x
            act.activation(idxT[x][:, 0:TP], flat[:, c:c + TP], ACT.Copy)
            done = act.activation(idxT[x][:, TP:T], flat[:, c + 128 * NBL - TS:c + 128 * NBL], ACT.Copy)
        done.then_inc(S["pickT_done"], 1)

        def gmats(i):
            for b in range(2):
                if not isinstance(i, int):
                    act.wait_ge(S[f"gates_kept{b}"], 16 * i)
                for r_ in range(UNITS):
                    un = UNITS * b + r_
                    act.wait_ge(S["gmat_ps"], 2 * UNITS * i + un + 1)
                    act.activation(gbuf[b][:, :, 4 * r_:4 * r_ + 4],
                                   aux[:, un % 2, :].rearrange("p (t i) -> p i t", t=4),
                                   ACT.Copy).then_inc(S["gmat_out"], 1)
                    hp = HPG + 2 * i + b
                    if r_ == 3:
                        his(hp, 1)
                    if r_ == 7:
                        his(hp, 1, 1)
                        if not isinstance(i, int):
                            act.wait_ge(S[f"hid_kept{b}"], 16 * i)
                        act.wait_ge(S["piece_used"], 2 * hp + 2)
                        act.activation(halves(gl[b][:, :]), both(b), ACT.Gelu).then_inc(S[f"evacuated{b}"], 1)

        peel(act, NTB // 2, gmats)
        for u in range(2):
            act.wait_ge(S[f"gates_kept{u}"], 16 * NTB // 2)

        def hidden(hp, g, par, last=False):
            for k in range(G2):
                q = k % 2
                his(hp + k, 2)
                act.wait_ge(S["piece_used"], 2 * (hp + k) + 2)
                act.wait_ge(S["m_done"], G2 * g + k - 1)
                act.activation(halves(gl[q][:, :]), both(q), ACT.Gelu).then_inc(S[f"evacuated{q}"], 1)
                act.wait_ge(S["m_done"], G2 * g + k + 1)
                act.activation(yh[:, G2 * par + k, :], mm[q][:, :], ACT.Copy).then_inc(S["m_hi"], 1)

        def early(g):
            if g >= 2:
                act.wait_ge(S["piece_used"], 2 * (HPV + 4 * (g - 1)))
            for k in range(G2):
                act.wait_ge(S["m_done"], G2 * g + k + 1)
                act.activation(yh[:, G2 * (g % 2) + k, :], mm[k % 2][:, :], ACT.Copy).then_inc(S["m_hi"], 1)

        early(0)
        early(1)
        for g in range(EARLY - 1):
            his(HPV + 4 * g, 8)
            if g + 2 < EARLY:
                early(g + 2)

        with act.Fori(0, (NG - EARLY) // 2 - 1) as i:
            for u in range(2):
                hp = HPS + 8 * (2 * i + u)
                hidden(hp, EARLY + 2 * i + u, u)
                his(hp + G2, 8)
        for g in range(NG - 3, NG - 1):
            hp = HPS + 8 * (g + 1 - EARLY)
            hidden(hp, g + 1, (g + 1) % 2)
            his(hp + G2, 8)
        his(HPS + 8 * (NG - EARLY), 6)
        norm(2, lambda: (act.wait_ge(S["evacuated0"], EV_END[0]), act.wait_ge(S["evacuated1"], EV_END[1])))

    @block.vector
    def _(dve):
        def wait(name, value):
            dve.wait_ge(S[name], value)

        def norm(c, ready):
            ready()
            wait("norm_sum", KD * (c + 1))
            dve.tensor_scalar(halves(ms[:, :]), aux[:, 0:2, 0:HT], 1.0 / D, EPS, ALU.mult, ALU.add
                              ).then_inc(S["norm_ms"], 1)
            wait("norm_root", c + 1)
            dve.reciprocal(ms[:, :], rst[:, :]).then_inc(S["norm_inv"], 1)
            wait("norm_inv", c + 1)
            for k in range(0, KD, 2):
                for u in range(2):
                    if k:
                        if c < 2:
                            wait("norm_lo", KD * c + k + u - 1)
                        else:
                            wait(f"y_kept{u}", 16 * k // 2)
                    dve.scalar_tensor_tensor(nt[u][:, :], mg[:, k + u, :], vector(("g1", "g2", "gf")[c], k + u),
                                             ms[:, :], ALU.mult, ALU.mult).then_inc(S["norm_scaled"], 1)
                if c < 2:
                    for u in range(2):
                        wait("norm_hi", KD * c + k + u + 1)
                        dve.tensor_tensor(xl[:, k + u, :], nt[u][:, :], xh[:, k + u, :].bitcast(F32),
                                          ALU.subtract).then_inc(S["norm_lo"], 1)

        norm(0, lambda: wait("const_in", 32))
        wait("norm_lo", KD)
        for u in range(2):
            dve.memset(cbuf[u][:, 0:DN_TAPS - 1], 0.0).then_inc(S["pads_set"], 1)

        def conv(m, i, u):
            wait(f"evacuated{u}", i + 1)
            if u < 2 and not (isinstance(m, int) and m < 2):
                wait("silu_done", m - 1)
            w = DN_TAPS - 1
            n = AW - w
            a, _n = VEC["dnw"]
            dve.tensor_scalar(cv[u][:, 0:n], cbuf[u][:, 0:n], vec[:, bass.ds(a + DN_TAPS * m, 1)], None,
                              ALU.mult).then_inc(S["conv_step"], 1)
            for k in range(1, DN_TAPS):
                wait("conv_step", w * m + k)
                dve.scalar_tensor_tensor(cv[u][:, 0:n], cbuf[u][:, k:k + n],
                                         vec[:, bass.ds(a + DN_TAPS * m + k, 1)], cv[u][:, 0:n],
                                         ALU.mult, ALU.add
                                         ).then_inc(S["conv_step"] if k < w else S["conv_done"], 1)

        def conv_pair(i):
            for u in range(2):
                conv(2 * i + u, i, u)

        peel(dve, NQKV // 2, conv_pair)

        for u in range(2):
            wait(f"kept_sv{u}", 16 * H // 2)

        def l2(i, scale):
            first = isinstance(i, int)
            for u in range(2):
                m = 2 * i + u
                wait("l2_sum", m + 1)
                if not first:
                    wait("l2_out", m - 1)
                dve.tensor_scalar(halves(ln[u][:, :]), aux[:, 2 * u:2 * u + 2, 0:HT], scale, scale * EPS,
                                  ALU.mult, ALU.add).then_inc(S["l2_ss"], 1)
            for u in range(2):
                m = 2 * i + u
                wait("l2_root", m + 1)
                dve.reciprocal(ln[u][:, :], ln[u][:, :]).then_inc(S["l2_inv"], 1)
            for u in range(2):
                m = 2 * i + u
                wait("l2_inv", m + 1)
                if not first:
                    wait(f"kept_qk{u}", 16 * i)
                dve.tensor_tensor(lo_[u][:, :], mg[:, m, :], ln[u][:, :], ALU.mult).then_inc(S["l2_out"], 1)

        l2(0, float(DK))
        with dve.Fori(1, H // 2) as i:
            l2(i, float(DK))
        with dve.Fori(H // 2, H) as i:
            l2(i, 1.0)

        sp1, sp2 = small["sp1"][:, :], small["sp2"][:, :]
        for u in range(2):
            wait(f"kept_qk{u}", 16 * H)
        wait("tok_ps", 1)
        wait("beta_done", 1)
        dve.tensor_tensor(heads(sp1, H), raw_tok[:, :, 32:32 + H],
                          vector("dtb")[0:64, :].unsqueeze(1).to_broadcast([64, NCH, H]), ALU.add
                          ).then_inc(S["sp_max"], 1)
        wait("sp_max", 1)
        dve.tensor_scalar(sp2, sp1, -1.0, None, ALU.mult).then_inc(S["sp_max"], 1)
        wait("sp_max", 2)
        dve.tensor_tensor(sp2, sp2, sp1, ALU.max).then_inc(S["sp_in"], 1)
        wait("sp_exp", 1)
        dve.tensor_scalar(sp2, sp2, 1.0, None, ALU.add).then_inc(S["sp_one"], 1)
        wait("sp_ln", 1)
        dve.scalar_tensor_tensor(sp1, sp1, 0.0, sp2, ALU.max, ALU.add).then_inc(S["sp_max"], 1)
        wait("sp_max", 3)
        wait("decay_exp", 1)
        dve.scalar_tensor_tensor(heads(small["gtok"][:, :], H), heads(sp1, H), -1.0,
                                 decay[:, :].unsqueeze(1).to_broadcast([64, NCH, H]), ALU.mult, ALU.mult
                                 ).then_inc(S["g_ready"], 1)
        wait("gc_ps", 1)
        wait("eg_done", 1)
        dve.tensor_copy(small["gcum"][:, :], aux[0:64, 0, 0:NCH * H]).then_inc(S["gcum_done"], 1)
        wait("gcum_done", 1)
        dve.tensor_tensor(small["kdec"][:, :], aux[0:64, 1, 0:NCH * H], small["gcum"][:, :], ALU.subtract
                          ).then_inc(S["kdec_in"], 1)
        dve.tensor_tensor(small["nbeg"][:, :], small["beta"][:, :], small["eg"][:, :], ALU.mult
                          ).then_inc(S["nbeg_done"], 1)
        wait("nbeg_done", 1)
        wait("kdec_done", 1)
        dve.memset(scb[:, 0:SC_TAPS - 1], 0.0).then_inc(S["pads_set"], 1)
        dve.memset(state[:, :, :], 0.0).then_inc(S["pads_set"], 1)
        wait("pads_set", 4)

        def per_token(name, n, width=C):
            return small[name][:, bass.ds(n * H, H)].unsqueeze(2).to_broadcast([64, H, width])

        def per_mask(t):
            return t.unsqueeze(1).to_broadcast([64, H, C])

        def level(l):
            a, _n = CONST["levels"]
            return cst[0:64, a + C * l:a + C * l + C]

        def delta(n, kind, i):
            first = isinstance(n, int) and n == 0
            dve.tensor_tensor(heads(lm[:, :]), per_token("gtok", n), per_mask(const("upper", 64)), ALU.mult
                              ).then_inc(S["gu_done"], 1)
            wait("gcb_ps", n + 1)
            dve.tensor_tensor(heads(pp[:, :]), heads(aux[0:64, 1, :]), per_token("gcum", n), ALU.subtract
                              ).then_inc(S["masked_raw"], 1)
            dve.tensor_tensor(heads(el[:, :]), per_token("gcum", n), heads(aux[0:64, 1, :]), ALU.subtract
                              ).then_inc(S["masked_raw"], 1)
            wait("masked_raw", 2 * n + 2)
            dve.tensor_tensor(heads(pp[:, :]), heads(pp[:, :]), per_mask(const("negT", 64)), ALU.add
                              ).then_inc(S["masked"], 1)
            dve.tensor_tensor(heads(el[:, :]), heads(el[:, :]), per_mask(const("negL", 64)), ALU.add
                              ).then_inc(S["masked"], 1)
            wait("kq_ps", n + 1)
            wait("exp_done", 3 * n + 1)
            dve.tensor_tensor(att[:, :], pp[:, :], aux[0:64, 2, :], ALU.mult).then_inc(S["att_done"], 1)
            wait("exp_done", 3 * n + 2)
            dve.tensor_tensor(ll[:, :], el[:, :], aux[0:64, 0, :], ALU.mult).then_inc(S["l_raw"], 1)
            wait("l_raw", n + 1)
            dve.tensor_tensor(heads(ll[:, :]), heads(ll[:, :]), per_token("beta", n), ALU.mult
                              ).then_inc(S["l_done"], 1)
            wait("l_done", n + 1)
            dve.tensor_tensor(heads(xx[:, :]), heads(ll[:, :]), per_mask(level(0)), ALU.mult
                              ).then_inc(S["x1_in"], 1)
            wait("x1_in", n + 1)
            dve.tensor_tensor(heads(xx[:, :]), per_mask(const("eye", 64)), heads(xx[:, :]), ALU.subtract
                              ).then_inc(S["x1_done"], 1)
            dve.tensor_tensor(heads(lm[:, :]), heads(ll[:, :]), per_mask(level(1)), ALU.mult
                              ).then_inc(S["lm_done"], 1)
            fill(0, kind, i)
            wait("exp_done", 3 * n + 3)
            dve.tensor_tensor(qg[:, :], qkv[:, 0:H, :].rearrange("p h c -> p (h c)"), egb[:, :], ALU.mult
                              ).then_inc(S["qg_done"], 1)
            wait("v_ps", n + 1)
            dve.tensor_tensor(vb[:, :, :], pair(0), per_token("beta", n, 128), ALU.mult
                              ).then_inc(S["vb_done"], 1)
            wait("y1_done", n + 1)
            fill(1, kind, i)
            for l in range(1, LEVELS):
                if l < LEVELS - 1:
                    wait("p_ps", 5 * n + l)
                    dve.tensor_tensor(heads(lm[:, :]), heads(ll[:, :]), per_mask(level(l + 1)), ALU.mult
                                      ).then_inc(S["lm_done"], 1)
                if l == 1:
                    wait("k_ps", n + 1)
                    dve.tensor_tensor(kd[:, :, :], pair(0), per_token("kdec", n, 128), ALU.mult
                                      ).then_inc(S["kd_done"], 1)
                    fill(2, kind, i)
                if l == 3:
                    if not first:
                        wait("s_done", n)
                    if isinstance(n, int) and n == NP1:
                        wait("s_init", 16)
                    dve.tensor_tensor(sdec[:, :, :], state[:, :, :],
                                      egl[:, bass.ds(n * H, H)].unsqueeze(2).to_broadcast([128, H, 128]),
                                      ALU.mult).then_inc(S["sdec_done"], 1)
                    fill(5, kind, i)
                wait("z_ps", 5 * n + l)
                dve.tensor_tensor(yy[:, :], yy[:, :], aux[0:64, 3, :], ALU.subtract).then_inc(S["y_upd"], 1)
                if l < LEVELS - 1:
                    dve.tensor_tensor(xx[:, :], xx[:, :], aux[0:64, 2, :], ALU.subtract).then_inc(S["x_upd"], 1)
                    wait("y_upd", 5 * n + l)
                    wait("x_upd", 4 * n + l)
                fill((3, 4, 6, 7, 8)[l - 1], kind, i)
            wait("ks_ps", n + 1)
            dve.tensor_tensor(rr[:, :, :], pair(0), per_token("nbeg", n, 128), ALU.mult).then_inc(S["r_raw"], 1)
            wait("r_raw", n + 1)
            dve.tensor_tensor(rr[:, :, :], vb[:, :, :], rr[:, :, :], ALU.subtract).then_inc(S["r_done"], 1)
            fill(9, kind, i)
            fill(10, kind, i)
            wait("sup_ps", n + 1)
            wait("sdec_done", n + 1)
            dve.tensor_tensor(state[:, :, :], sdec[:, :, :],
                              aux[:, 2:4, :].rearrange("p a (h n) -> p (a h) n", n=128), ALU.add
                              ).then_inc(S["s_done"], 1)
            fill(11, kind, i)

        def fill(k, kind, i):
            hp = fill_base(kind, i)
            if kind == "B":
                j = 2 * i + k // 6
                if k % 6 == 3:
                    short_conv(j, 2 * hp + k + 1)
                if k % 6 == 5:
                    short_out(j, 2 * hp + k + 1)
                if k in (7, 11):
                    j = 2 * i + k // 8
                    wait("sc_hi", j + 1)
                    dve.tensor_tensor(yl[:, j, :], yt[:, :], yh[:, j, :].bitcast(F32), ALU.subtract
                                      ).then_inc(S["sc_lo"], 1)
            if kind == "C" and k % 3 == 2:
                s = k // 3
                m = 4 * i + s
                wait("evacuated0", EV_C[0] + m + 1)
                if s >= 2:
                    wait(f"half_kept{s % 2}", 16 * (2 * i + s // 2))
                elif isinstance(i, int):
                    wait("sc_lo", NSC)
                else:
                    wait(f"half_kept{s}", 32 * i)
                wait("piece_used", 2 * hp + k + 1)
                dve.tensor_tensor(halves(cm[s % 2][:, :]), halves(csg[s % 2][:, :]), both(1), ALU.mult
                                  ).then_inc(S["evacuated1"], 1)

        def short_conv(j, used):
            w = SC_TAPS - 1
            a, _n = VEC["scst"]
            b, _n = VEC["scw"]
            n = SW - w
            wait("evacuated0", EV_B[0] + 2 * j + 1)
            wait("piece_used", used)
            dve.tensor_copy(scb[:, w + TP:2 * w + TP], vec[:, bass.ds(a + w * j, w)])
            dve.tensor_tensor(scb[:, w:w + HT], ctmp[:, 0:HT], ps[1][:, 0, 0:HT], ALU.mult)
            dve.tensor_tensor(scb[:, w + HT:w + TP], ctmp[:, HT:TP], ps[1][:, 1, 0:TP - HT], ALU.mult)
            dve.tensor_tensor(scb[:, 2 * w + TP:SW], ctmp[:, TP:T], ps[1][:, 1, TP - HT:HT], ALU.mult
                              ).then_inc(S["evacuated1"], 1)
            wait("evacuated1", EV_B[1] + j + 1)
            dve.tensor_copy(sctail[:, j, 0, :], scb[:, TP:TP + w])
            dve.tensor_copy(sctail[:, j, 1, :], scb[:, SW - w:SW])
            dve.tensor_scalar(scv[:, 0:n], scb[:, 0:n], vec[:, bass.ds(b + SC_TAPS * j, 1)], None, ALU.mult
                              ).then_inc(S["sc_step"], 1)
            for k in range(1, SC_TAPS):
                wait("sc_step", SC_TAPS * j + k)
                dve.scalar_tensor_tensor(scv[:, 0:n], scb[:, k:k + n], vec[:, bass.ds(b + SC_TAPS * j + k, 1)],
                                         scv[:, 0:n], ALU.mult, ALU.add).then_inc(S["sc_step"], 1)
            wait("sc_step", SC_TAPS * j + SC_TAPS)

        def short_out(j, used):
            w = SC_TAPS - 1
            if not (isinstance(j, int) and j == 0):
                wait("sc_lo", j)
            wait("piece_used", used)
            dve.tensor_tensor(yt[:, 0:HT], scv[:, 0:HT], ps[0][:, 0, 0:HT], ALU.mult)
            dve.tensor_tensor(yt[:, HT:TP], scv[:, HT:TP], ps[0][:, 1, 0:TP - HT], ALU.mult)
            dve.tensor_tensor(yt[:, TP:T], scv[:, TP + w:T + w], ps[0][:, 1, TP - HT:HT], ALU.mult
                              ).then_inc(S["evacuated0"], 1)

        chunks(dve, delta)

        def gated(i):
            first = isinstance(i, int)
            for u in range(2):
                wait("go_sum", 2 * i + u + 1)
                dve.tensor_scalar(halves(gr[u][:, :]), aux[:, 2 * u:2 * u + 2, 0:HT], 1.0 / 128, EPS,
                                  ALU.mult, ALU.add).then_inc(S["go_ss"], 1)
            for u in range(2):
                wait("go_root", 2 * i + u + 1)
                dve.reciprocal(gr[u][:, :], gr[u][:, :]).then_inc(S["go_inv"], 1)
            for u in range(2):
                h = 2 * i + u
                wait("go_inv", h + 1)
                if not first:
                    wait("go_lo", h - 1)
                dve.tensor_tensor(gt_[u][:, :], go[u][:, :], gr[u][:, :], ALU.mult).then_inc(S["go_raw"], 1)
            for u in range(2):
                wait("go_raw", 2 * i + u + 1)
                dve.scalar_tensor_tensor(gt_[u][:, :], gt_[u][:, :], vector("dng", 0), gz[u][:, :],
                                         ALU.mult, ALU.mult).then_inc(S["go_scaled"], 1)
            for u in range(2):
                h = 2 * i + u
                wait("go_hi", h + 1)
                dve.tensor_tensor(yl[:, h, :], gt_[u][:, :], yh[:, h, :].bitcast(F32), ALU.subtract
                                  ).then_inc(S["go_lo"], 1)

        wait("s_kept", 32)
        wait("o_kept", 16 * NCH)
        peel(dve, H // 2, gated)
        wait("go_lo", H)
        with dve.Fori(0, KD // 2) as i:
            for u in range(2):
                m = 2 * i + u
                wait("evacuated0", EV_D[0] + m + 1)
                wait("piece_used", P_D + 6 * i + 3 * u + 3)
                dve.tensor_tensor(halves(dt[u][:, :]), halves(sg[u][:, :]), both(1), ALU.mult
                                  ).then_inc(S["evacuated1"], 1)
                wait("evacuated1", EV_D[1] + m + 1)
                wait(f"hb_in{u}", 16 * i + 16)
                dve.tensor_tensor(mg[:, m, :], hb[u][:, :], dt[u][:, :], ALU.add).then_inc(S["merged"], 1)
        for k in range(KD):
            wait("mg_hi", k + 1)
            dve.tensor_tensor(xl[:, k, :], mg[:, k, :], xh[:, k, :].bitcast(F32), ALU.subtract
                              ).then_inc(S["mg_lo"], 1)
        wait("mg_lo", KD)
        with dve.Fori(0, KD // 2) as i:
            for u in range(2):
                wait(f"xr_in{u}", 16 * i + 16)
                wait("piece_used", P_E + 4 * i + 2 * u + 2)
                dve.tensor_tensor(halves(mg[:, 2 * i + u, :]), halves(xr[u][:, :]), both(u), ALU.add
                                  ).then_inc(S[f"evacuated{u}"], 1)
        for u in range(2):
            wait(f"evacuated{u}", EV_F[u])
        norm(1, lambda: None)
        wait("norm_lo", 2 * KD)

        NEGMAX = -3.0e38
        STEPS = 11

        def plain_wait(name, value):
            wait(name, value)
            if not isinstance(value, int):
                dve.sem_inc(S["dve_waited"])

        def topk(h):
            count = [0]

            def step(ins):
                count[0] += 1
                ins.then_inc(S["topk_step"], 1)
                plain_wait("topk_step", STEPS * h + count[0])

            def score(b, s):
                c = (b % 2) * 256 + s * NK
                return aux[:, b // 2, c:c + NK]

            def sums(t, b):
                return t[:, b, :, :].rearrange("p a b -> p (a b)")

            both_ = [(b, s) for b in range(NBL) for s in range(2)]
            plain_wait("score_ps", h + 1)
            for b, s in both_:
                last = dve.max(tv[:, b, s, 0:8], score(b, s))
            step(last)
            for b, s in both_:
                dve.max_index(ti[:, b, s, 0:8], tv[:, b, s, 0:8], score(b, s))
                last = dve.match_replace(mrall[:, b, s, :], tv[:, b, s, 0:8], score(b, s), NEGMAX)
            last.then_inc(S["scores_read"], 1)
            plain_wait("scores_read", h + 1)
            for b, s in both_:
                last = dve.max(tv[:, b, s, 8:16], mrall[:, b, s, :])
            step(last)
            for b, s in both_:
                last = dve.max_index(ti[:, b, s, 8:16], tv[:, b, s, 8:16], mrall[:, b, s, :])
            for b in range(NBL):
                last = dve.tensor_tensor(cand[:, b, :, :], tv[:, b, 0, :].unsqueeze(2).to_broadcast([128, TOPK, TOPK]),
                                         tv[:, b, 1, :].unsqueeze(1).to_broadcast([128, TOPK, TOPK]), ALU.add)
            step(last)
            dve.tensor_copy(tif[:, :, :, :], ti[:, :, :, :])
            for b in range(NBL):
                last = dve.max(best[:, b, 0:8], sums(cand, b))
            step(last)
            for b in range(NBL):
                dve.max_index(posu[:, b, 0:8], best[:, b, 0:8], sums(cand, b))
                last = dve.match_replace(sums(sel, b), best[:, b, 0:8], sums(cand, b), NEGMAX)
            step(last)
            for b in range(NBL):
                last = dve.max(best[:, b, 8:16], sums(sel, b))
            step(last)
            for b in range(NBL):
                last = dve.max_index(posu[:, b, 8:16], best[:, b, 8:16], sums(sel, b))
            step(last)
            dve.tensor_tensor(gate[:, :, h, :], best[:, :, :], best[:, :, 0:1].to_broadcast([128, NBL, TOPK]),
                              ALU.subtract).then_inc(S["shifted"], 1)
            dve.tensor_scalar(posi[0][:, :, :], posu[:, :, :], 4, None, ALU.logical_shift_right)
            step(dve.tensor_scalar(posi[1][:, :, :], posu[:, :, :], TOPK - 1, None, ALU.bitwise_and))
            for s in range(2):
                last = dve.tensor_copy(posf[s][:, :, :], posi[s][:, :, :])
            step(last)
            i16 = const("iota16").unsqueeze(1).to_broadcast([128, NBL * TOPK, TOPK])
            bufs = (sel, sel2)
            for s in range(2):
                last = dve.tensor_tensor(bufs[s][:, :, :, :].rearrange("p b k j -> p (b k) j"), i16,
                                         posf[s][:, :, :].rearrange("p b k -> p (b k)").unsqueeze(2)
                                         .to_broadcast([128, NBL * TOPK, TOPK]), ALU.is_equal)
            step(last)
            for s in range(2):
                last = dve.tensor_tensor(bufs[s][:, :, :, :], bufs[s][:, :, :, :],
                                         tif[:, :, s, :].unsqueeze(2).to_broadcast([128, NBL, TOPK, TOPK]),
                                         ALU.mult)
            step(last)
            for s in range(2):
                last = dve.reduce_sum(pick[s][:, :, h, :], bufs[s][:, :, :, :], AX_X)
            last.then_inc(S["picked"], 1)
            assert count[0] == STEPS, count[0]

        with dve.Fori(0, H) as h:
            topk(h)
        wait("gate_exp", 1)
        gates_all = gate[:, :, :, :].rearrange("p b h k -> p (b h) k")
        dve.reduce_sum(gsum[:, :], gates_all, AX_X).then_inc(S["gsum_step"], 1)
        wait("gsum_step", 1)
        dve.reciprocal(gsum[:, :], gsum[:, :]).then_inc(S["gsum_step"], 1)
        wait("gsum_step", 2)
        dve.tensor_tensor(gates_all, gates_all, gsum[:, :].unsqueeze(2).to_broadcast([128, NBL * H, TOPK]),
                          ALU.mult).then_inc(S["pick_done"], 1)

        wait("pickT_done", 1)

        def onehots(i):
            for u in range(2):
                if not isinstance(i, int):
                    wait("gmat_ps", 2 * i + u - 1)
                for c in range(4):
                    t = bass.ds(8 * i + 4 * u + c, 1)
                    dve.tensor_scalar(oa[u][:, c, :], const("iota"), idxT[0][:, t], idxT[2][:, t],
                                      ALU.is_equal, ALU.mult)
                    last = dve.tensor_scalar(ob[u][:, c, :], const("iota"), idxT[1][:, t], None, ALU.is_equal)
                last.then_inc(S["onehots"], 1)

        peel(dve, T // 8, onehots)
        for u in range(2):
            wait(f"gates_kept{u}", 16 * NTB // 2)

        def gate_hidden(g, par, k):
            q = k % 2
            if not (isinstance(g, int) and g == 0 and k < 2):
                wait("m_lo", G2 * g + k - 1)
            dve.tensor_tensor(mm[q][:, :].rearrange("p (a t) -> p a t", t=TB),
                              gl[q][:, :].rearrange("p (a t) -> p a t", t=TB),
                              gtile[par][:, :, k, :], ALU.mult).then_inc(S["m_done"], 1)
            wait("m_hi", G2 * g + k + 1)
            dve.tensor_tensor(yl[:, G2 * par + k, :], mm[q][:, :], yh[:, G2 * par + k, :].bitcast(F32),
                              ALU.subtract).then_inc(S["m_lo"], 1)

        def early(g):
            wait(f"gt_in{g % 2}", 16 * (g // 2 + 1))
            for k in range(G2):
                wait(f"gl_in{k % 2}", 16 * ((G2 * g + k) // 2 + 1))
                gate_hidden(g, g % 2, k)

        def hidden(g, gi, par):
            wait(f"gt_in{par}", 16 * (EARLY // 2) + 16 * gi + 16)
            for k in range(G2):
                wait(f"evacuated{k % 2}", EV_S[k % 2] + PER_G * (g - EARLY) + k // 2 + 1)
                gate_hidden(g, par, k)

        def collect(hp, g):
            for d in range(KD // 2):
                wait("group_done", (KD // 2) * g + d + 1)
                dve.tensor_tensor(halves(mg[:, 2 * d, :]), halves(mg[:, 2 * d, :]), both(0), ALU.add
                                  ).then_inc(S["evacuated0"], 1)
                wait("piece_used", 2 * hp + d + 1)
                dve.tensor_tensor(halves(mg[:, 2 * d + 1, :]), halves(mg[:, 2 * d + 1, :]), both(1), ALU.add
                                  ).then_inc(S["evacuated1"], 1)

        early(0)
        early(1)
        for g in range(EARLY - 1):
            collect(HPV + 4 * g, g)
            if g + 2 < EARLY:
                early(g + 2)
        with dve.Fori(0, (NG - EARLY) // 2 - 1) as i:
            for u in range(2):
                hidden(EARLY + 2 * i + u, i, u)
                collect(HPS + 8 * (2 * i + u) + G2, EARLY - 1 + 2 * i + u)
        for g in range(NG - 3, NG - 1):
            hidden(g + 1, (NG - EARLY) // 2 - 1, (g + 1) % 2)
            collect(HPS + 8 * (g + 1 - EARLY) + G2, g)
        collect(HPS + 8 * (NG - EARLY), NG - 1)
        for u in range(2):
            wait(f"evacuated{u}", EV_END[u])
        norm(2, lambda: None)

    @block.tensor
    def _(pe):
        def piece(hp, c, slot, high, low, k0, first, last, tiles_=range(NPIECE), done=("piece_used",),
                  between=lambda t: None):
            w = c % 2
            for t in tiles_:
                for half in range(2):
                    cols = slice(half * HT, (half + 1) * HT)
                    k = k0 + t - tiles_[0]
                    for x, (a, b) in enumerate(((wh, high), (wh, low), (wl, high))):
                        mm_ = pe.matmul(ps[slot][:, half, 0:HT], a[w][:, t, :], b[:, k, cols],
                                        start=first and t == tiles_[0] and x == 0,
                                        stop=last and t == tiles_[-1] and x == 2)
                if t < tiles_[-1]:
                    between(t)
            mm_.then_inc(S[done[0]], 1)

        def product(hp, c0, slot, ev, high, low, n):
            if not (isinstance(ev, int) and ev == 0):
                pe.wait_ge(S[f"evacuated{slot}"], ev)
            for c in range(n):
                pe.wait_ge(S["lo_done"], 2 * hp + c0 + c + 1)
                piece(hp, c0 + c, slot, high, low, NPIECE * c, c == 0, c == n - 1)

        def norm(c):
            for k in range(KD):
                pe.wait_ge(S["norm_sq"], KD * c + k + 1)
                for half in range(2):
                    last = pe.matmul(aux[:, half, 0:HT], const("ones"), sq[k % 2][:, half * HT:(half + 1) * HT],
                                     start=k == 0, stop=k == KD - 1)
                last.then_inc(S["norm_sum"], 1)

        pe.wait_ge(S["const_in"], 32)
        norm(0)
        pe.wait_ge(S["norm_lo"], KD)

        def a_pair(i):
            for u in range(2):
                product(HPA + 2 * i + u, 0, u, i, xh, xl, 2)

        peel(pe, N_A // 2, a_pair)
        product(HPA + N_A - 1, 0, 0, N_A // 2, xh, xl, 2)

        def l2(i):
            for u in range(2):
                m = 2 * i + u
                pe.wait_ge(S["l2_sq"], m + 1)
                if not isinstance(i, int):
                    pe.wait_ge(S["l2_ss"], m - 1)
                for half in range(2):
                    last = pe.matmul(aux[:, 2 * u + half, 0:HT], const("ones"),
                                     lq[u][:, half * HT:(half + 1) * HT], start=True, stop=True)
                last.then_inc(S["l2_sum"], 1)

        peel(pe, H, l2)
        pe.wait_ge(S["evacuated0"], EV_B[0])
        pe.wait_ge(S["l2_ss"], 2 * H)
        for n in range(NCH):
            last = pe.transpose(raw_flat[:, n * C:(n + 1) * C], bar[0:64, n * C:(n + 1) * C],
                                const("ident", 64)[:, 0:64])
        last.then_inc(S["tok_ps"], 1)
        pe.wait_ge(S["g_ready"], 1)
        pe.matmul(aux[0:64, 0, 0:NCH * H], const("upper", 64), small["gtok"][:, :], start=True, stop=True)
        pe.matmul(aux[:, 1, 0:NCH * H], const("ones", 64), small["gtok"][:, :], start=True, stop=True
                  ).then_inc(S["gc_ps"], 1)
        pe.wait_ge(S["kdec_in"], 1)
        pe.wait_ge(S["eg_done"], 1)

        def pe_wait(sem, value):
            pe.wait_ge(sem, value)
            if not isinstance(value, int):
                pe.sem_inc(S["pe_waited"])

        def fill(k, kind, i):
            hp = fill_base(kind, i)
            if kind == "B":
                j, group, part = 2 * i + k // 6, k % 6 // 2, k % 2
                slot = group % 2
                ev = (EV_B[0] + 2 * j, EV_B[1] + j, EV_B[0] + 2 * j + 1)[group]
                data, n = (xh, xl), 2
            elif kind == "C":
                m, part = 4 * i + k // 3, k % 3 % 2
                slot = k % 3 // 2
                ev = EV_C[slot] + m
                data, n = ((xh, xl), 2) if slot == 0 else ((yh, yl), 1)
            else:
                slot, part = k // 2 % 2, k % 2
                ev = EV_Z[slot] + k // 4
                data, n = (xh, xl), 2
            if part == 0:
                pe.wait_ge(S[f"evacuated{slot}"], ev)
            if kind == "C" and k == 2:
                pe.wait_ge(S["sc_lo"], NSC)
            pe.wait_ge(S["lo_done"], 2 * hp + k + 1)
            piece(hp, k, slot, *data, NPIECE * part, part == 0, part == n - 1)

        def delta(n, kind, i):
            first = isinstance(n, int) and n == 0

            def per_head(out, left, right, start=True, stop=True):
                for h in range(H):
                    last = pe.matmul(out(h), left(h), right(h), start=start, stop=stop)
                return last

            q_h = lambda h: qkv[:, h, :]
            k_h = lambda h: qkv[:, H + h, :]
            v_h = lambda h: qkv[:, 2 * H + h, :]
            sq_h = lambda t: (lambda h: t[:, h * C:(h + 1) * C])
            bank = lambda b, rows=64: (lambda h: aux[0:rows, b, h * C:(h + 1) * C])
            wide = lambda b, rows=64: (lambda h: aux[0:rows, b + h // 4, (h % 4) * 128:(h % 4 + 1) * 128])
            pe_wait(S["gu_done"], n + 1)
            if not first:
                pe_wait(S["r_done"], n)
            pe.matmul(aux[:, 1, :], const("ones", 64), lm[:, :], start=True, stop=True).then_inc(S["gcb_ps"], 1)
            pe_wait(S["chunk_in"], 16 * n + 16)
            if not first:
                pe_wait(S["s_done"], n)
                pe_wait(S["o_copied"], n)
            per_head(bank(2), k_h, q_h)
            per_head(bank(0), k_h, k_h).then_inc(S["kq_ps"], 1)
            fill(0, kind, i)
            pe_wait(S["x1_done"], n + 1)
            for h in range(H):
                last = pe.transpose(aux[0:64, 3, h * C:(h + 1) * C], xx[:, h * C:(h + 1) * C],
                                    const("ident", 64)[:, 0:64])
            last.then_inc(S["xt_ps"], 1)
            pe_wait(S["exp_done"], 3 * n + 3)
            for h in range(H):
                last = pe.transpose(wide(0)(h), v_h(h), const("ident"))
            last.then_inc(S["v_ps"], 1)
            fill(1, kind, i)
            pe_wait(S["att_done"], n + 1)
            for l in range(1, LEVELS):
                if l == 1:
                    pe_wait(S["y1_done"], n + 1)
                else:
                    pe_wait(S["y_upd"], 5 * n + l - 1)
                    pe_wait(S["x_upd"], 4 * n + l - 1)
                pe_wait(S["lm_done"], 5 * n + l)
                per_head(bank(2), sq_h(lm), sq_h(yy)).then_inc(S["p_ps"], 1)
                if l == 1:
                    pe_wait(S["vb_done"], n + 1)
                    for h in range(H):
                        last = pe.transpose(wide(0)(h), k_h(h), const("ident"))
                    last.then_inc(S["k_ps"], 1)
                    fill(2, kind, i)
                if l == 3:
                    fill(5, kind, i)
                pe_wait(S["p_copied"], 5 * n + l)
                last = per_head(bank(3), sq_h(xx), sq_h(pp))
                if l < LEVELS - 1:
                    last = per_head(bank(2), sq_h(pp), sq_h(xx))
                last.then_inc(S["z_ps"], 1)
                fill((3, 4, 6, 7, 8)[l - 1], kind, i)
            if isinstance(n, int) and n == NP1:
                pe_wait(S["s_init"], 16)
            if first:
                pe_wait(S["pads_set"], 4)
            pe_wait(S["kd_done"], n + 1)
            per_head(wide(0), k_h, lambda h: state[:, h, :]).then_inc(S["ks_ps"], 1)
            fill(9, kind, i)
            pe_wait(S["r_done"], n + 1)
            pe_wait(S["y_upd"], 5 * n + 5)
            per_head(wide(2), sq_h(yy), lambda h: rr[:, h, :]).then_inc(S["vn_ps"], 1)
            fill(10, kind, i)
            pe_wait(S["vn_done"], n + 1)
            pe_wait(S["qg_done"], n + 1)
            for h in range(H):
                pe.matmul(bank(0, 128)(h), state[:, h, :], qg[:, h * C:(h + 1) * C], start=True, stop=False)
                last = pe.matmul(bank(0, 128)(h), vb[:, h, :], att[:, h * C:(h + 1) * C], start=False, stop=True)
            last.then_inc(S["o_ps"], 1)
            per_head(wide(2, 128), lambda h: kd[:, h, :], lambda h: vb[:, h, :]).then_inc(S["sup_ps"], 1)
            fill(11, kind, i)

        chunks(pe, delta)
        for m in range(FILL // 2, NZ):
            product(HPZ + m, 0, m % 2, EV_Z[m % 2] + m // 2, xh, xl, 2)

        def branch(hp0, ev):
            with pe.Fori(0, KD // 2) as i:
                for u in range(2):
                    product(hp0 + 3 * i, 3 * u, 0, ev[0] + 2 * i + u, xh, xl, 2)
                    product(hp0 + 3 * i, 3 * u + 2, 1, ev[1] + 2 * i + u, yh, yl, 1)

        pe.wait_ge(S["s_done"], NCH)
        pe.wait_ge(S["o_copied"], NCH)

        def gated(i):
            for u in range(2):
                h = 2 * i + u
                pe.wait_ge(S["go_sq"], h + 1)
                if not isinstance(i, int):
                    pe.wait_ge(S["go_ss"], h - 1)
                for half in range(2):
                    last = pe.matmul(aux[:, 2 * u + half, 0:HT], const("ones"),
                                     gq[u][:, half * HT:(half + 1) * HT], start=True, stop=True)
                last.then_inc(S["go_sum"], 1)

        peel(pe, H // 2, gated)
        pe.wait_ge(S["go_lo"], H)
        branch(HPD, EV_D)
        pe.wait_ge(S["mg_lo"], KD)
        with pe.Fori(0, KD // 2) as i:
            for u in range(2):
                product(HPE + 2 * i + u, 0, u, EV_E[u] + i, xh, xl, 2)
        norm(1)
        pe.wait_ge(S["norm_lo"], 2 * KD)

        def queries(h):
            for u in range(2):
                product(HPF + 2 * h + u, 0, u, EV_F[u] + h, xh, xl, 2)
            for u in range(2):
                pe.wait_ge(S[f"evacuated{u}"], EV_F[u] + h + 1)
            if not isinstance(h, int):
                pe.wait_ge(S["scores_read"], h)
            for b, t0 in enumerate(BLOCKS):
                for u in range(2):
                    c = (b % 2) * 256 + u * NK
                    last = pe.matmul(aux[:, b // 2, c:c + NK], qh[u][:, t0:t0 + 128], keys[:, 2 * h + u, :],
                                     start=True, stop=True)
            last.then_inc(S["score_ps"], 1)

        pe.wait_ge(S["keys_in"], 16)
        peel(pe, H, queries)

        def turn():
            pe.wait_ge(S["pick_done"], 1)
            flat = aux[:, :, :].rearrange("p a b -> p (a b)")
            for x, t in enumerate((pick[0], pick[1], gate)):
                for b in range(NBL):
                    c = 128 * (NBL * x + b)
                    last = pe.transpose(flat[:, c:c + 128], t[:, b, :, :].rearrange("p h k -> p (h k)"),
                                        const("ident"))
            last.then_inc(S["pickT_ps"], 1)

        def gmats(i):
            for b in range(2):
                hp = HPG + 2 * i + b

                def unit(r_):
                    un = UNITS * b + r_
                    u = un % 2
                    pe.wait_ge(S["onehots"], 2 * UNITS * i + un + 1)
                    if not (isinstance(i, int) and un < 2):
                        pe.wait_ge(S["gmat_out"], 2 * UNITS * i + un - 1)
                    for c in range(4):
                        last = pe.matmul(aux[:, u, c * NK:(c + 1) * NK], oa[u][:, c, :], ob[u][:, c, :],
                                         start=True, stop=True)
                    last.then_inc(S["gmat_ps"], 1)

                pe.wait_ge(S[f"evacuated{b}"], EV_G[b] + i)
                for c in range(2):
                    pe.wait_ge(S["lo_done"], 2 * hp + c + 1)
                    piece(hp, c, b, xh, xl, NPIECE * c, c == 0, c == 1,
                          between=lambda t: unit(4 * c + t // 2) if t % 2 else None)
                    unit(4 * c + 3)
                unit(8)

        turn()
        pe.wait_ge(S["pickT_done"], 1)
        peel(pe, NTB // 2, gmats)

        def hidden(hp, ev0, ev1):
            for k in range(G2):
                product(hp + k, 0, k % 2, (ev0, ev1)[k % 2] + k // 2, xh, xl, 2)

        def values(hp, g, par, ev):
            pe.wait_ge(S["m_lo"], G2 * g + G2)
            for d in range(KD // 2):
                pe.wait_ge(S["lo_done"], 2 * hp + d + 1)
                for x in range(2):
                    pe.wait_ge(S[f"evacuated{x}"], ev[x] + d)
                    piece(hp, d, x, yh, yl, G2 * par, True, True, range(G2 * x, G2 * x + G2),
                          ("group_done", "piece_used")[x:])

        for g in range(EARLY - 1):
            values(HPV + 4 * g, g, g % 2, [e + g * KD // 2 for e in EV_V])

        def step(g, hp, par):
            base = [e + PER_G * (g - EARLY + 1) for e in EV_S]
            hidden(hp, base[0], base[1])
            values(hp + G2, g, par, [e + G2 // 2 for e in base])

        with pe.Fori(0, (NG - EARLY) // 2) as i:
            for u in range(2):
                step(EARLY - 1 + 2 * i + u, HPS + 8 * (2 * i + u), 1 - u)
        values(HPS + 8 * (NG - EARLY), NG - 1, 1, [e - KD // 2 for e in EV_END])
        norm(2)

    block_context.__exit__(None, None, None)


def constants():
    t = np.zeros((128, N_CONST), np.float32)

    def put(name, value):
        a, n = CONST[name]
        t[0:value.shape[0], a:a + n] = value

    i, j = np.arange(C)[:, None], np.arange(C)[None, :]
    put("ones", np.ones((128, 128), np.float32))
    put("ident", np.eye(128, dtype=np.float32))
    put("iota", np.broadcast_to(np.arange(128, dtype=np.float32), (128, 128)))
    put("upper", (i <= j).astype(np.float32))
    put("negT", np.where(j >= i, 0.0, NEG).astype(np.float32))
    put("negL", np.where(j < i, 0.0, NEG).astype(np.float32))
    put("eye", np.eye(C, dtype=np.float32))
    put("levels", np.concatenate([((i >> (l + 1)) == (j >> (l + 1))) & ((i >> l) % 2 == 1) & ((j >> l) % 2 == 0)
                                  for l in range(LEVELS)], axis=1).astype(np.float32))
    put("iota16", np.broadcast_to(np.arange(TOPK, dtype=np.float32), (128, TOPK)))
    return t


def pieces(w):
    k, m = w.shape
    return w.reshape(k // 1024, NPIECE, 128, m // 128, 128).transpose(3, 0, 2, 1, 4).reshape(-1, 128, 1024)


def kernel(x_prompt, x_sample, state_dn, state_dn_conv, state_sc_conv, norm1_g, w_in, sc_conv_w, dn_conv_w,
           dn_a_log, dn_dt_bias, dn_norm_g, w_br_sc, w_br_dn, w_o, norm2_g, peer_wq, peer_keys, peer_u,
           peer_v, final_norm_g):
    import concourse.bacc as bacc
    from concourse.bass_utils import run_bass_kernel_spmd

    f = {n: np.asarray(a) for n, a in dict(
        x_prompt=x_prompt, x_sample=x_sample, state_dn=state_dn, state_dn_conv=state_dn_conv,
        state_sc_conv=state_sc_conv, norm1_g=norm1_g, w_in=w_in, sc_conv_w=sc_conv_w, dn_conv_w=dn_conv_w,
        dn_a_log=dn_a_log, dn_dt_bias=dn_dt_bias, dn_norm_g=dn_norm_g, w_br_sc=w_br_sc, w_br_dn=w_br_dn,
        w_o=w_o, norm2_g=norm2_g, peer_wq=peer_wq, peer_keys=peer_keys, peer_u=peer_u, peer_v=peer_v,
        final_norm_g=final_norm_g).items()}
    x = np.concatenate([f["x_prompt"][0], f["x_sample"][0]], axis=0)
    x = np.ascontiguousarray(x.T.reshape(KD, 128, T).transpose(1, 0, 2))

    w = f["w_in"][0]
    edges = np.cumsum((0, SCW, SCW, SCW, QKV, 1024, H, H, D, D))
    sc_b, sc_c, sc_h, qkv_w, z_w, beta_w, a_w, gsc_w, gdn_w = (w[:, a:b] for a, b in zip(edges, edges[1:]))
    ba = np.zeros((D, 128), np.float32)
    ba[:, 0:H] = beta_w
    ba[:, 32:32 + H] = a_w
    stream = [pieces(qkv_w), pieces(ba)]
    stream.append(np.stack([pieces(m).reshape(NSC, 2, 128, 1024) for m in (sc_c, sc_h, sc_b)], axis=1
                           ).reshape(-1, 128, 1024))

    def gate_and_branch(gate_w, branch_w):
        return np.concatenate([pieces(gate_w).reshape(KD, 2, 128, 1024),
                               pieces(branch_w).reshape(KD, 1, 128, 1024)], axis=1).reshape(-1, 128, 1024)

    stream += [gate_and_branch(gsc_w, f["w_br_sc"][0]), pieces(z_w), gate_and_branch(gdn_w, f["w_br_dn"][0])]
    stream += [pieces(f["w_o"][0]), pieces(f["peer_wq"][0])]
    u = f["peer_u"][0].reshape(NK, NG, G2, 2, NPIECE, 128).transpose(1, 2, 3, 5, 4, 0).reshape(NG, 2 * G2, 128, 1024)
    v = f["peer_v"][0].reshape(NK, NG, G2, KD // 2, 2, 128).transpose(1, 3, 0, 4, 2, 5).reshape(
        NG, KD // 2, 128, 1024)
    stream += [u[g] for g in range(EARLY)] + [v[g] for g in range(EARLY - 1)]
    for g in range(EARLY - 1, NG - 1):
        stream += [u[g + 1], v[g]]
    stream.append(v[NG - 1])
    stream = np.concatenate(stream, axis=0)
    assert stream.shape == (N_PIECES, 128, 1024)

    vec = np.zeros((128, N_VEC), np.float32)

    def put(name, value):
        a, n = VEC[name]
        vec[:, a:a + n] = value

    def columns(a, n):
        return a.reshape(a.shape[0], n, 128).transpose(2, 1, 0).reshape(128, -1)

    put("g1", columns(f["norm1_g"], KD))
    put("g2", columns(f["norm2_g"], KD))
    put("gf", columns(f["final_norm_g"][None], KD))
    put("dnw", columns(f["dn_conv_w"][0], NQKV))
    put("scw", columns(f["sc_conv_w"][0], NSC))
    put("dng", f["dn_norm_g"][0][:, None])
    put("alog", np.broadcast_to(f["dn_a_log"][0], (128, H)))
    put("dtb", np.broadcast_to(f["dn_dt_bias"][0], (128, H)))
    put("dnst", columns(f["state_dn_conv"][0, 0], NQKV))
    put("scst", columns(f["state_sc_conv"][0, 0], NSC))
    arrays = {
        "x": x, "w": stream, "vec": vec, "const": constants(),
        "s0": np.ascontiguousarray(f["state_dn"][0, 0].transpose(1, 0, 2)),
        "keys": np.ascontiguousarray(f["peer_keys"][0].reshape(KD, NK, 128).transpose(2, 0, 1)),
    }
    outs = {"y": (128, KD, T), "sp": (128, H, 128), "ss": (128, H, 128),
            "dnc": (128, NQKV, 2, DN_TAPS - 1), "scc": (128, NSC, 2, SC_TAPS - 1)}
    scratch = {"qkv_s": (NCH, 128, NQKV, C), "z_s": (NZ, 128, T), "o_s": (NCH, 128, HC),
               "half_s": (KD, 128, T), "gates_s": (NG, 128, NTB, G2 * TB), "hid_s": (EARLY * G2, 128, T)}

    nc = bacc.Bacc("TRN2", target_bir_lowering=False, num_devices=1)
    args = [nc.dram_tensor(f"in_{n}", a.shape, F32, kind="ExternalInput").ap() for n, a in arrays.items()]
    args += [nc.dram_tensor(f"out_{n}", s, F32, kind="ExternalOutput").ap() for n, s in outs.items()]
    args += [nc.dram_tensor(n, s, F32, kind="Internal").ap() for n, s in scratch.items()]
    trunk_program(nc, *args)
    r = run_bass_kernel_spmd(nc, [{f"in_{n}": a for n, a in arrays.items()}], core_ids=[0]).results[0]

    y = r["out_y"].transpose(2, 1, 0).reshape(T, D)
    dn = [r[f"out_{n}"].transpose(1, 0, 2)[None, None] for n in ("sp", "ss")]
    dnc = r["out_dnc"].transpose(2, 3, 1, 0).reshape(2, DN_TAPS - 1, QKV)
    scc = r["out_scc"].transpose(2, 3, 1, 0).reshape(2, SC_TAPS - 1, SCW)
    out = (y[None, 0:TP], y[None, TP:], dn[0], dnc[None, None, 0], scc[None, None, 0],
           dn[1], dnc[None, None, 1], scc[None, None, 1])
    return tuple(np.ascontiguousarray(a) for a in out)
```

```python
import concourse.bass as bass
import numpy as np
from concourse import mybir

F32 = mybir.dt.float32
F32R = mybir.dt.float32r
U32 = mybir.dt.uint32
ALU = mybir.AluOpType
ACT = mybir.ActivationFunctionType
AX_X = mybir.AxisListType.X

D = 2048
TP, TS = 512, 64
T = TP + TS
HT = T // 2
KD = D // 128
C = 64
NCH = T // C
H = 8
HC = H * C
SCW, SC_TAPS = 1024, 3
QKV, DN_TAPS = 3072, 4
NSC, NQKV, NZ = SCW // 128, QKV // 128, 1024 // 128
DK = 128
NK = 128
TOPK = 16
HK = H * TOPK
G2 = 4
NG = NK // G2
TB = 48
NTB = T // TB
EPS = 1e-6
NEG = -1e30
LEVELS = 6
NPIECE = 8
FILL = 12
EARLY = 6
KEPT = (EARLY - 1) * G2
PLAIN = KEPT - NTB
BLOCKS = (0, 128, 256, 384, T - 128)
NBL = len(BLOCKS)

Y_PARTS = ((0, 4), (4, 8), (8, 12), (12, 14), (14, KD))

P_A = 0
N_A = NQKV + 1
P_B = P_A + 2 * N_A
P_C = P_B + 6 * NSC
P_Z = P_C + 3 * KD
P_D = P_Z + 2 * NZ
P_D2 = P_D + 2 * KD
P_E = P_D2 + KD
P_F = P_E + 2 * KD
P_G = P_F + 2 * KD
N_PIECES = P_G + 2 * 2 * G2 * NG

CONST = {}
_at = 0
for _name, _width in (("ones", 128), ("ident", 128), ("iota", 128), ("upper", C), ("negT", C), ("negL", C),
                      ("eye", C), ("levels", LEVELS * C), ("iota16", TOPK)):
    CONST[_name] = (_at, _width)
    _at += _width
N_CONST = _at
VEC = {}
_at = 0
for _name, _width in (("g1", KD), ("g2", KD), ("gf", KD), ("dnw", NQKV * DN_TAPS), ("scw", NSC * SC_TAPS),
                      ("dng", 1), ("alog", H), ("dtb", H), ("dnst", NQKV * (DN_TAPS - 1)),
                      ("scst", NSC * (SC_TAPS - 1))):
    VEC[_name] = (_at, _width)
    _at += _width
N_VEC = _at


def trunk_program(nc, x_in, w_in, vec_in, const_in, s0_in, keys_in, y_out, sp_out, ss_out, dnc_out, scc_out,
                  qkv_d, z_d, o_d, half_d, sig_d, gates_d, hid_d):
    base = -(-nc.sbuf_base // 64) * 64
    CH = T * 4
    at = {}
    pos = base
    for name, size in (("XH", KD * CH), ("XL", KD * CH), ("MG", KD * CH), ("W", 6 * 4096), ("CV", 4 * N_CONST),
                       ("VV", 4 * N_VEC), ("TAIL", 4 * (NQKV * 6 + NSC * 4)), ("Y", KD * CH)):
        at[name] = pos
        pos += -(-size // 64) * 64
    at["L"] = pos
    end = nc.sbuf_usable_end

    def sb(name, shape, dtype, offset):
        size = int(np.prod(shape[1:])) * 4
        assert offset + size <= end, (name, offset + size, end)
        return nc.alloc_sbuf_tensor_at(name, shape, dtype, offset=offset)

    class Region:
        def __init__(self, offset, limit):
            self.pos, self.limit = offset, limit

        def take(self, name, shape, dtype=F32):
            t = sb(name, shape, dtype, self.pos)
            self.pos += -(-int(np.prod(shape[1:])) * 4 // 32) * 32
            assert self.pos <= self.limit, (name, self.pos, self.limit)
            return t

    xh = sb("xh", [128, KD, T], F32R, at["XH"])
    xl = sb("xl", [128, KD, T], F32R, at["XL"])
    mg = sb("mg", [128, KD, T], F32, at["MG"])
    yh = sb("yh", [128, NSC, T], F32R, at["Y"])
    yl = sb("yl", [128, NSC, T], F32R, at["Y"] + NSC * CH)
    wr = [sb(f"wr{i}", [128, NPIECE, 128], F32, at["W"] + 4096 * i) for i in range(2)]
    wh = [sb(f"wh{i}", [128, NPIECE, 128], F32R, at["W"] + 4096 * (2 + i)) for i in range(2)]
    wl = [sb(f"wl{i}", [128, NPIECE, 128], F32R, at["W"] + 4096 * (4 + i)) for i in range(2)]
    cst = sb("cst", [128, N_CONST], F32, at["CV"])
    vec = sb("vec", [128, N_VEC], F32, at["VV"])
    tail = sb("tail", [128, NQKV, 2, DN_TAPS - 1], F32, at["TAIL"])
    sctail = sb("sctail", [128, NSC, 2, SC_TAPS - 1], F32, at["TAIL"] + 4 * NQKV * 6)

    def const(name, rows=128):
        a, n = CONST[name]
        return cst[0:rows, a:a + n]

    def vector(name, j=None, n=1):
        a, m = VEC[name]
        return vec[:, a:a + m] if j is None else vec[:, bass.ds(a + j, n)]

    r = Region(at["L"] + 8 * CH, end)
    sq = [r.take(f"sq{i}", [128, T]) for i in range(2)]
    nt = [r.take(f"nt{i}", [128, T]) for i in range(2)]
    ms, rst = r.take("ms", [128, T]), r.take("rst", [128, T])
    r = Region(at["L"], end)
    AW = T + 2 * (DN_TAPS - 1)
    bar = r.take("bar", [128, T])
    cbuf = [r.take(f"cbuf{i}", [128, AW]) for i in range(2)]
    cv = [r.take(f"cv{i}", [128, AW]) for i in range(2)]
    sv = [r.take(f"sv{i}", [128, T]) for i in range(2)]
    lq = [r.take(f"lq{i}", [128, T]) for i in range(2)]
    ln = [r.take(f"ln{i}", [128, T]) for i in range(2)]
    lo_ = [r.take(f"lo{i}", [128, T]) for i in range(2)]
    r = Region(at["L"] + CH, end)
    SW = T + 2 * (SC_TAPS - 1)
    places = [r.pos]
    ctmp = r.take("ctmp", [128, T])
    places.append(r.pos)
    scb = r.take("scb", [128, SW])
    places.append(r.pos)
    scv = r.take("scv", [128, SW])
    places.append(r.pos)
    yt = r.take("yt", [128, T])
    csg = [sb(f"csg{i}", [128, T], F32, places[i]) for i in range(2)]
    cm = [sb(f"cm{i}", [128, T], F32, places[2 + i]) for i in range(2)]
    small = {n: r.take(n, [64, NCH * H]) for n in ("beta", "gtok", "gcum", "eg", "nbeg", "kdec", "sp1", "sp2")}
    egl = r.take("egl", [128, NCH * H])
    decay = r.take("decay", [64, H])
    xx = r.take("xx", [64, HC])
    yy = r.take("yy", [64, HC])
    lm = r.take("lm", [64, HC])
    pp = r.take("pp", [64, HC])
    oo = r.take("oo", [128, HC])
    m = Region(at["MG"], at["MG"] + KD * CH)
    qkv = m.take("qkv", [128, NQKV, C])
    state = m.take("state", [128, H, 128])
    sdec = m.take("sdec", [128, H, 128])
    vb = m.take("vb", [64, H, 128])
    kd = m.take("kd", [64, H, 128])
    rr = m.take("rr", [64, H, 128])
    el = m.take("el", [64, HC])
    ll = m.take("ll", [64, HC])
    att = m.take("att", [64, HC])
    m = Region(r.pos, end)
    egb = m.take("egb", [128, HC])
    qg = m.take("qg", [128, HC])
    r = Region(at["L"], end)
    sgr = [r.take(f"sgr{i}", [128, T]) for i in range(2)]
    dt = [r.take(f"dt{i}", [128, T]) for i in range(2)]
    xr = [r.take(f"xr{i}", [128, T]) for i in range(2)]
    hb = [r.take(f"hb{i}", [128, T]) for i in range(2)]
    r = Region(at["L"], end)
    go = [r.take(f"go{i}", [128, T]) for i in range(2)]
    gz = [r.take(f"gz{i}", [128, T]) for i in range(2)]
    gq = [r.take(f"gq{i}", [128, T]) for i in range(2)]
    gr = [r.take(f"gr{i}", [128, T]) for i in range(2)]
    gt_ = [r.take(f"gt_{i}", [128, T]) for i in range(2)]
    sgd = [r.take(f"sgd{i}", [128, T]) for i in range(2)]
    idx_at = (end - 3 * CH) // 64 * 64
    r = Region(idx_at, end)
    idxT = [r.take(n, [128, T]) for n in ("i1T", "i2T", "gateT")]
    r = Region(at["Y"], idx_at)
    keys = r.take("keys", [128, KD, NK])
    qh = [r.take(f"qh{i}", [128, T]) for i in range(2)]
    cand = r.take("cand", [128, NBL, TOPK, TOPK])
    mrall = sb("mrall", [128, NBL, 2, NK], F32, r.pos)
    sel = r.take("sel", [128, NBL, TOPK, TOPK])
    sel2 = r.take("sel2", [128, NBL, TOPK, TOPK])
    tv = r.take("tv", [128, NBL, 2, TOPK])
    ti = r.take("ti", [128, NBL, 2, TOPK], U32)
    tif = r.take("tif", [128, NBL, 2, TOPK])
    best = r.take("best", [128, NBL, TOPK])
    posu = r.take("posu", [128, NBL, TOPK], U32)
    posi = [r.take(f"posi{i}", [128, NBL, TOPK], U32) for i in range(2)]
    posf = [r.take(f"posf{i}", [128, NBL, TOPK]) for i in range(2)]
    pick = [r.take(f"pick{i}", [128, NBL, H, TOPK]) for i in range(2)]
    gate = r.take("gate", [128, NBL, H, TOPK])
    gsum = r.take("gsum", [128, NBL * H])
    GB = NK * TB * 4
    r = Region(at["Y"] + 2 * GB, idx_at)
    oa = [r.take(f"oa{i}", [128, 4, NK]) for i in range(2)]
    ob = [r.take(f"ob{i}", [128, 4, NK]) for i in range(2)]
    gbuf = [sb(f"gbuf{i}", [128, NK, TB], F32, at["Y"] + i * GB) for i in range(2)]
    r = Region(at["L"], end)
    gtile = [r.take(f"gtile{i}", [128, NTB, G2, TB]) for i in range(2)]
    mm = [r.take(f"mm{i}", [128, T]) for i in range(2)]
    gl_at = (idx_at - 2 * CH) // 64 * 64
    assert r.pos <= gl_at
    gl = [sb(f"gl{i}", [128, T], F32, gl_at + i * CH) for i in range(2)]
    assert at["Y"] + 2 * GB + 4 * 4 * NK * 4 <= gl_at

    ps = [nc.alloc_psum_tensor(f"ps{i}", [128, 2, 512], F32) for i in range(2)]
    aux = nc.alloc_psum_tensor("aux", [128, 4, 512], F32)
    raw_flat = aux[0:64, 2:4, :].rearrange("p a b -> p (a b)")[:, 0:T]
    raw_tok = raw_flat.rearrange("p (n c) -> p n c", c=C)

    names = """raw_full0 raw_full1 hi_done lo_done piece_used group_done evacuated0 evacuated1
        const_in x_in0 x_in1 x_in2 x_in3 norm_sq norm_sum norm_ms norm_root norm_inv norm_step norm_scaled norm_hi norm_lo
        conv_step conv_done silu_done pads_set kept_sv0 kept_sv1
        l2_sq l2_sum l2_ss l2_root l2_step l2_out kept_qk0 kept_qk1
        tok_ps beta_done sp_in sp_exp sp_one sp_ln sp_max decay_exp g_ready gc_ps gcum_done kdec_in kdec_done eg_done
        nbeg_done chunk_in s_init gu_done gcb_ps kq_ps masked_raw masked exp_done
        att_done l_raw l_done x1_in x1_done xt_ps y1_done qg_done lm_done p_ps p_copied z_ps y_upd x_upd
        v_ps vb_done k_ps kd_done sdec_done ks_ps r_raw r_done vn_ps vn_done o_ps o_copied o_kept
        sup_ps s_done s_kept sc_step sc_hi sc_lo
        half_kept0 half_kept1 merged hb_in0 hb_in1 kept_z0 kept_z1 go_in0 go_in1 go_sq go_sum go_ss go_root go_step
        sig_kept0 sig_kept1 go_scaled go_hi go_lo
        mg_hi mg_lo xr_in0 xr_in1 keys_in score_ps topk_step scores_read shifted picked gsum_step gate_exp pick_done pickT_ps
        pickT_done onehots gmat_ps gmat_out gates_kept0 gates_kept1
        gt_in0 gt_in1 hid_kept0 hid_kept1 gl_in0 gl_in1 m_done m_hi m_lo tails_kept y_kept dve_waited act_waited pe_waited""".split()
    S = {n: nc.alloc_semaphore(n) for n in names}

    def halves(t):
        return t.rearrange("p (a b) -> p a b", a=2)

    def both(slot):
        return ps[slot][:, :, 0:HT]

    def heads(t, n=C):
        return t.rearrange("p (h n) -> p h n", n=n)

    def pair(b):
        return aux[0:64, b:b + 2, :].rearrange("p a (h n) -> p (a h) n", n=128)

    def chunks(eng, run):
        run(0, "B", 0)
        with eng.Fori(1, NSC // 2) as n:
            run(n, "B", n)
        run(NSC // 2, "C", 0)
        with eng.Fori(NSC // 2 + 1, NSC) as n:
            run(n, "C", n - NSC // 2)
        run(NCH - 1, "Z", 0)

    def fill_base(kind, i):
        return {"B": HPB, "C": HPC, "Z": HPZ}[kind] + FILL // 2 * i

    def peel(eng, n, body):
        body(0)
        with eng.Fori(1, n) as i:
            body(i)

    EV_B = (N_A // 2 + 1, N_A // 2)
    EV_C = (EV_B[0] + 2 * NSC, EV_B[1] + NSC)
    EV_Z = (EV_C[0] + KD, EV_C[1] + KD)
    EV_D = (EV_Z[0] + NZ // 2, EV_Z[1] + NZ // 2)
    EV_D2 = (EV_D[0] + KD // 2, EV_D[1] + KD // 2)
    EV_E = (EV_D2[0] + KD // 2, EV_D2[1] + KD // 2)
    EV_F = (EV_E[0] + KD // 2, EV_E[1] + KD // 2)
    EV_G = (EV_F[0] + KD // 2, EV_F[1] + KD // 2)
    PER_G = (G2 + KD) // 2
    EV_END = (EV_G[0] + NG * PER_G, EV_G[1] + NG * PER_G)
    HPA, HPB, HPC, HPZ, HPD, HPD2, HPE, HPF, HPG = (
        p // 2 for p in (P_A, P_B, P_C, P_Z, P_D, P_D2, P_E, P_F, P_G))
    HPU = HPG + KEPT
    HPV = HPU + G2
    HPS = HPV + (EARLY - 1) * 4
    EV_U = (EV_G[0] + KEPT // 2, EV_G[1] + KEPT // 2)
    EV_V = (EV_G[0] + EARLY * G2 // 2, EV_G[1] + EARLY * G2 // 2)
    EV_S = tuple(e + (EARLY - 1) * KD // 2 for e in EV_V)
    UNITS = TB // 4
    NP1 = NCH - 1
    AFTER = (0, 2, 3, 5, 6)

    block_context = nc.Block()
    block = block_context.__enter__()

    @block.sync
    def _(sp):
        def load(hp, slot):
            if not (isinstance(hp, int) and hp == 0):
                sp.wait_ge(S["lo_done"], 2 * hp + slot - 1)
            sp.dma_start(wr[slot][:, :, :].rearrange("p a n -> p (a n)"), w_in[2 * hp + slot, :, :]
                         ).then_inc(S[f"raw_full{slot}"], 16)

        def loads(hp, n, c0=0):
            for c in range(c0, c0 + n):
                load(hp + 2 + c // 2, c % 2)

        sp.dma_start(cst[:, :], const_in).then_inc(S["const_in"], 16)
        sp.dma_start(vec[:, :], vec_in).then_inc(S["const_in"], 16)
        for q in range(4):
            ks = slice(KD // 4 * q, KD // 4 * (q + 1))
            sp.dma_start(mg[:, ks, :], x_in[:, ks, :]).then_inc(S[f"x_in{q}"], 16)
        for p in range(4):
            load(p // 2, p % 2)

        def qk_store(m, u):
            sp.wait_ge(S["l2_out"], m + 1)
            sp.dma_start(qkv_d[:, :, m, :].rearrange("n p c -> p n c"),
                         lo_[u][:, :].rearrange("p (n c) -> p n c", c=C)).then_inc(S[f"kept_qk{u}"], 16)

        def qk_stores(i):
            loads(HPA + 2 * i, 2)
            if not isinstance(i, int):
                qk_store(2 * i - 1, 1)
            loads(HPA + 2 * i + 1, 2)
            qk_store(2 * i, 0)

        peel(sp, H, qk_stores)
        qk_store(2 * H - 1, 1)
        with sp.Fori(0, H // 2) as i:
            for u in range(2):
                loads(HPA + 16 + 2 * i + u, 2)
                sp.wait_ge(S["silu_done"], 17 + 2 * i + u)
                sp.dma_start(qkv_d[:, :, 16 + 2 * i + u, :].rearrange("n p c -> p n c"),
                             sv[u][:, :].rearrange("p (n c) -> p n c", c=C)).then_inc(S[f"kept_sv{u}"], 16)
        loads(HPA + 24, 2)
        sp.dma_start(dnc_out, tail[:, :, :, :]).then_inc(S["tails_kept"], 16)
        for u in range(2):
            sp.wait_ge(S[f"kept_sv{u}"], 16 * H // 2)
            sp.wait_ge(S[f"kept_qk{u}"], 16 * H)

        def chunk_load(n):
            sp.dma_start(qkv[:, :, :], qkv_d[n, :, :, :]).then_inc(S["chunk_in"], 16)

        def chunk_store(n):
            sp.wait_ge(S["o_copied"], n + 1)
            sp.dma_start(o_d[n, :, :], oo[:, :]).then_inc(S["o_kept"], 16)

        def run(n, kind, i):
            hp = fill_base(kind, i)
            last = kind == "Z"

            def half_store(s):
                u = s % 2
                sp.wait_ge(S["evacuated1"], EV_C[1] + 4 * i + s + 1)
                sp.dma_start(half_d[4 * i + s, :, :], cm[u][:, :]).then_inc(S[f"half_kept{u}"], 16)

            def z_store(m):
                u = m % 2
                sp.wait_ge(S[f"evacuated{u}"], EV_Z[u] + m // 2 + 1)
                sp.dma_start(z_d[m, :, :], csg[u][:, :]).then_inc(S[f"kept_z{u}"], 16)

            for k in range(FILL):
                if k == 9 and not last:
                    sp.wait_ge(S["ks_ps"], n + 1)
                    sp.wait_ge(S["qg_done"], n + 1)
                    chunk_load(n + 1)
                if k == 11:
                    chunk_store(n)
                loads(hp, 1, k)
                if kind == "C" and k % 3 == 0 and k:
                    half_store(k // 3 - 1)
                if kind == "Z" and k % 2 == 0 and k:
                    z_store(k // 2 - 1)
                if last and k == 0:
                    sp.wait_ge(S["s_done"], NP1)
                    sp.dma_start(sp_out, state[:, :, :]).then_inc(S["s_kept"], 16)
                    sp.wait_ge(S["s_kept"], 16)
                    sp.dma_start(state[:, :, :], s0_in).then_inc(S["s_init"], 16)
            if kind == "C":
                half_store(3)
            if kind == "Z":
                z_store(FILL // 2 - 1)
                for m in range(FILL // 2, NZ):
                    loads(hp + m, 2)
                    z_store(m)

        chunk_load(0)
        chunks(sp, run)
        sp.wait_ge(S["s_done"], NCH)
        sp.dma_start(ss_out, state[:, :, :]).then_inc(S["s_kept"], 16)
        sp.wait_ge(S["sc_lo"], NSC)
        sp.dma_start(scc_out, sctail[:, :, :, :]).then_inc(S["tails_kept"], 16)
        for u in range(2):
            sp.wait_ge(S[f"kept_z{u}"], 16 * NZ // 2)
            sp.wait_ge(S[f"half_kept{u}"], 16 * KD // 2)
        sp.wait_ge(S["o_kept"], 16 * NCH)

        def head_load(i):
            for u in range(2):
                if not isinstance(i, int):
                    sp.wait_ge(S["go_scaled"], 2 * i + u - 1)
                sp.dma_start(go[u][:, :].rearrange("p (n c) -> p n c", c=C),
                             o_d[:, :, bass.ds((2 * i + u) * C, C)].rearrange("n p c -> p n c")
                             ).then_inc(S[f"go_in{u}"], 16)
                sp.dma_start(gz[u][:, :], z_d[2 * i + u, :, :]).then_inc(S[f"go_in{u}"], 16)

        def gates_and_heads(i):
            for m in range(4):
                u = m % 2
                loads(HPD + 4 * i + m, 2)
                sp.wait_ge(S[f"evacuated{u}"], EV_D[u] + 2 * i + m // 2 + 1)
                sp.dma_start(sig_d[4 * i + m, :, :], sgd[u][:, :]).then_inc(S[f"sig_kept{u}"], 16)

        head_load(0)
        gates_and_heads(0)
        with sp.Fori(1, H // 2) as i:
            head_load(i)
            gates_and_heads(i)
        for u in range(2):
            sp.wait_ge(S[f"sig_kept{u}"], 16 * KD // 2)
        sp.wait_ge(S["go_lo"], H)

        def half_again(i):
            for u in range(2):
                loads(HPD2 + i, 1, u)
                if not isinstance(i, int):
                    sp.wait_ge(S["merged"], 2 * i + u - 1)
                sp.dma_start(hb[u][:, :], half_d[2 * i + u, :, :]).then_inc(S[f"hb_in{u}"], 16)
                sp.dma_start(sgr[u][:, :], sig_d[2 * i + u, :, :]).then_inc(S[f"hb_in{u}"], 16)

        peel(sp, KD // 2, half_again)

        def x_again(i):
            for u in range(2):
                loads(HPE + 2 * i + u, 2)
                if not isinstance(i, int):
                    sp.wait_ge(S[f"evacuated{u}"], EV_E[u] + i)
                sp.dma_start(xr[u][:, :], x_in[:, 2 * i + u, :]).then_inc(S[f"xr_in{u}"], 16)

        peel(sp, KD // 2, x_again)
        sp.dma_start(keys[:, :, :], keys_in).then_inc(S["keys_in"], 16)
        with sp.Fori(0, KD // 2) as i:
            loads(HPF + 2 * i, 4)

        for k in range(PLAIN):
            loads(HPG + k, 2)
            sp.wait_ge(S[f"evacuated{k % 2}"], EV_G[k % 2] + k // 2 + 1)
            sp.dma_start(hid_d[k, :, :], gl[k % 2][:, :]).then_inc(S[f"hid_kept{k % 2}"], 16)
        with sp.Fori(0, NTB // 2) as i:
            for u in range(2):
                loads(HPG + PLAIN + 2 * i + u, 2)
                sp.wait_ge(S["gmat_out"], UNITS * (2 * i + u + 1))
                sp.dma_start(gates_d[:, :, 2 * i + u, :].rearrange("g p n -> p g n"),
                             gbuf[u][:, :, :].rearrange("p (g i) t -> p g (i t)", i=G2)
                             ).then_inc(S[f"gates_kept{u}"], 16)
                sp.wait_ge(S[f"evacuated{u}"], EV_G[u] + PLAIN // 2 + i + 1)
                sp.dma_start(hid_d[PLAIN + 2 * i + u, :, :], gl[u][:, :]).then_inc(S[f"hid_kept{u}"], 16)

        loads(HPU, 2)
        for u in range(2):
            sp.wait_ge(S[f"gates_kept{u}"], 16 * NTB // 2)
            sp.wait_ge(S[f"hid_kept{u}"], 16 * KEPT // 2)

        def gate_load(g, u):
            if not (isinstance(g, int) and g < 2):
                sp.wait_ge(S["m_done"], G2 * (g - 1))
            sp.dma_start(gtile[u][:, :, :, :].rearrange("p a i t -> p a (i t)"), gates_d[g, :, :, :]
                         ).then_inc(S[f"gt_in{u}"], 16)

        def hidden_load(g, k):
            sp.wait_ge(S["m_done"], G2 * g + k - 1)
            sp.dma_start(gl[k % 2][:, :], hid_d[G2 * (g - 1) + k, :, :]).then_inc(S[f"gl_in{k % 2}"], 16)

        gate_load(0, 0)
        loads(HPU + 1, 2)
        gate_load(1, 1)
        loads(HPU + 2, 4)
        for g in range(EARLY - 1):
            hidden_load(g + 1, 0)
            hidden_load(g + 1, 1)
            gate_load(g + 2, g % 2)
            for d in range(KD // 2):
                loads(HPV + 4 * g, 1, d)
                if d in (1, 3):
                    hidden_load(g + 1, 2 + d // 2)

        def step(g, hp, par):
            loads(hp, 2 * G2)
            gate_load(g + 2, par)
            loads(hp + G2, 2 * G2)

        with sp.Fori(0, (NG - EARLY) // 2 - 1) as i:
            for u in range(2):
                step(EARLY - 1 + 2 * i + u, HPS + 8 * (2 * i + u), 1 - u)
        step(NG - 3, HPS + 8 * (NG - 2 - EARLY), 1)
        loads(HPS + 8 * (NG - 1 - EARLY), 16)
        loads(HPS + 8 * (NG - EARLY), 4)

        for a, b in Y_PARTS:
            sp.wait_ge(S["norm_scaled"], 2 * KD + b)
            sp.dma_start(y_out[:, a:b, :], mg[:, a:b, :]).then_inc(S["y_kept"], 16)
        sp.wait_ge(S["y_kept"], 16 * len(Y_PARTS))
        sp.wait_ge(S["s_kept"], 32)
        sp.wait_ge(S["tails_kept"], 32)

    @block.gpsimd
    def _(pool):
        with pool.Fori(0, N_PIECES // 2) as i:
            for u in range(2):
                pool.wait_ge(S["hi_done"], 2 * i + u + 1)
                pool.tensor_tensor(wl[u][:, :, :], wr[u][:, :, :], wh[u][:, :, :].bitcast(F32),
                                   ALU.subtract).then_inc(S["lo_done"], 1)

    @block.scalar
    def _(act):
        def hi(hp, slot):
            act.wait_ge(S[f"raw_full{slot}"], 16 * hp + 16)
            if not (isinstance(hp, int) and hp == 0):
                act.wait_ge(S["piece_used"], 2 * hp + slot - 1)
            act.activation(wh[slot][:, :, :], wr[slot][:, :, :], ACT.Copy).then_inc(S["hi_done"], 1)

        def his(hp, n, c0=0):
            for c in range(c0, c0 + n):
                hi(hp + 1 + c // 2, c % 2)

        def square(c, k, u):
            if not (isinstance(k, int) and KD * c + k < 2):
                act.wait_ge(S["norm_sum"], KD * c + k - 1)
            act.activation(sq[u][:, :], mg[:, k, :], ACT.Square).then_inc(S["norm_sq"], 1)

        def norm(c):
            act.wait_ge(S["norm_ms"], c + 1)
            act.activation(rst[:, :], ms[:, :], ACT.Sqrt).then_inc(S["norm_root"], 1)
            if c < 2:
                for k in range(KD):
                    act.wait_ge(S["norm_scaled"], KD * c + k + 1)
                    act.activation(xh[:, k, :], nt[k % 2][:, :], ACT.Copy).then_inc(S["norm_hi"], 1)

        for u in range(2):
            hi(0, u)
        act.wait_ge(S["const_in"], 32)
        for k in range(KD):
            if k % (KD // 4) == 0:
                act.wait_ge(S[f"x_in{k // (KD // 4)}"], 16)
            square(0, k, k % 2)
        norm(0)

        def qkv_in(m, i, u, piece, ev, first):
            his(piece, 2)
            act.wait_ge(S["piece_used"], 2 * piece + 2)
            if first:
                act.wait_ge(S["pads_set"], 2)
            else:
                act.wait_ge(S["conv_done"], m - 1)
            a, n = VEC["dnst"]
            w = DN_TAPS - 1
            act.activation(cbuf[u][:, w:w + HT], ps[u][:, 0, 0:HT], ACT.Copy)
            act.activation(cbuf[u][:, w + HT:w + TP], ps[u][:, 1, 0:TP - HT], ACT.Copy)
            act.activation(cbuf[u][:, w + TP:2 * w + TP], vec[:, bass.ds(a + m * w, w)], ACT.Copy)
            act.activation(cbuf[u][:, 2 * w + TP:AW], ps[u][:, 1, TP - HT:HT], ACT.Copy)
            act.activation(tail[:, m, :, :], ps[u][:, 1, HT - 2 * TS:HT].rearrange(
                "p (a b) -> p a b", a=2)[:, :, TS - w:TS], ACT.Copy).then_inc(S[f"evacuated{u}"], 1)

        def silu_out(m, u, out):
            act.wait_ge(S["conv_done"], m + 1)
            w = DN_TAPS - 1
            act.activation(out[:, 0:TP], cv[u][:, 0:TP], ACT.Silu)
            act.activation(out[:, TP:T], cv[u][:, TP + w:T + w], ACT.Silu).then_inc(S["silu_done"], 1)

        def l2_square(m, u):
            if not (isinstance(m, int) and m < 2):
                act.wait_ge(S["l2_out"], m - 1)
            act.wait_ge(S["silu_done"], m + 1)
            act.sem_inc(S["act_waited"])
            act.activation(lq[u][:, :], mg[:, m, :], ACT.Square).then_inc(S["l2_sq"], 1)

        def l2_root(m, u):
            act.wait_ge(S["l2_ss"], m + 1)
            act.activation(lq[u][:, :], ln[u][:, :], ACT.Sqrt).then_inc(S["l2_root"], 1)

        def qk_unit(i):
            for u in range(2):
                m = 2 * i + u
                qkv_in(m, i, u, HPA + m, i, isinstance(i, int))
                if isinstance(i, int) and u == 0:
                    act.wait_ge(S["norm_lo"], KD)
                else:
                    l2_root(m - 1, 1 - u)
                silu_out(m, u, mg[:, m, :])
                l2_square(m, u)

        peel(act, H, qk_unit)
        l2_root(2 * H - 1, 1)

        def v_unit(i):
            for u in range(2):
                m = 16 + 2 * i + u
                qkv_in(m, i, u, HPA + m, i, False)
                if not isinstance(i, int):
                    act.wait_ge(S[f"kept_sv{u}"], 16 * i)
                silu_out(m, u, sv[u])

        peel(act, H // 2, v_unit)
        his(HPA + 24, 2)
        act.wait_ge(S["piece_used"], P_B)
        act.activation(halves(bar[:, :]), both(0), ACT.Copy).then_inc(S["evacuated0"], 1)

        for u in range(2):
            act.wait_ge(S[f"kept_sv{u}"], 16 * H // 2)

        act.wait_ge(S["tok_ps"], 1)
        for u in range(2):
            act.wait_ge(S[f"kept_qk{u}"], 16 * H)
        act.activation(heads(small["beta"][:, :], H), raw_tok[:, :, 0:H], ACT.Sigmoid).then_inc(S["beta_done"], 1)
        act.activation(decay[:, :], vector("alog")[0:64, :], ACT.Exp).then_inc(S["decay_exp"], 1)
        act.wait_ge(S["sp_in"], 1)
        act.activation(small["sp2"][:, :], small["sp2"][:, :], ACT.Exp, scale=-1.0).then_inc(S["sp_exp"], 1)
        act.wait_ge(S["sp_one"], 1)
        act.activation(small["sp2"][:, :], small["sp2"][:, :], ACT.Ln).then_inc(S["sp_ln"], 1)
        act.wait_ge(S["gc_ps"], 1)
        act.activation(small["eg"][:, :], aux[0:64, 0, 0:NCH * H], ACT.Exp)
        act.activation(egl[:, :], aux[:, 1, 0:NCH * H], ACT.Exp).then_inc(S["eg_done"], 1)
        act.wait_ge(S["kdec_in"], 1)
        act.activation(small["kdec"][:, :], small["kdec"][:, :], ACT.Exp).then_inc(S["kdec_done"], 1)

        def fill(k, kind, i):
            hp = fill_base(kind, i)
            his(hp, 1, k)
            if kind == "B":
                j = 2 * i + k // 6
                if k % 6 == 1:
                    act.wait_ge(S["evacuated1"], EV_B[1] + j)
                    act.wait_ge(S["piece_used"], 2 * hp + k + 1)
                    act.activation(halves(ctmp[:, :]), both(0), ACT.Copy).then_inc(S["evacuated0"], 1)
                if k in (6, 11):
                    j = 2 * i + k // 7
                    act.wait_ge(S["evacuated0"], EV_B[0] + 2 * j + 2)
                    act.activation(yh[:, j, :], yt[:, :], ACT.Copy).then_inc(S["sc_hi"], 1)
            if kind == "C" and k % 3 == 1:
                m = 4 * i + k // 3
                act.wait_ge(S["evacuated1"], EV_C[1] + m - 1)
                act.wait_ge(S["piece_used"], 2 * hp + k + 1)
                act.activation(halves(csg[k // 3 % 2][:, :]), both(0), ACT.Sigmoid).then_inc(S["evacuated0"], 1)
            if kind == "Z" and k % 2 == 1:
                z_out(k // 2, 2 * hp + k + 1)

        def z_out(m, used):
            u = m % 2
            act.wait_ge(S["evacuated1"], EV_Z[1])
            if m >= 2:
                act.wait_ge(S[f"kept_z{u}"], 16 * (m // 2))
            act.wait_ge(S["piece_used"], used)
            act.activation(halves(csg[u][:, :]), both(u), ACT.Silu).then_inc(S[f"evacuated{u}"], 1)

        def delta(n, kind, i):
            act.wait_ge(S["masked"], 2 * n + 1)
            act.activation(pp[:, :], pp[:, :], ACT.Exp).then_inc(S["exp_done"], 1)
            act.wait_ge(S["masked"], 2 * n + 2)
            act.activation(el[:, :], el[:, :], ACT.Exp).then_inc(S["exp_done"], 1)
            act.activation(egb[:, :], aux[:, 1, :], ACT.Exp).then_inc(S["exp_done"], 1)
            fill(0, kind, i)
            act.wait_ge(S["xt_ps"], n + 1)
            act.activation(yy[:, :], aux[0:64, 3, :], ACT.Copy).then_inc(S["y1_done"], 1)
            fill(1, kind, i)
            fills = {1: (2, 3), 2: (4,), 3: (5, 6), 4: (7,), 5: (8,)}
            for l in range(1, LEVELS):
                act.wait_ge(S["p_ps"], 5 * n + l)
                act.activation(pp[:, :], aux[0:64, 2, :], ACT.Copy).then_inc(S["p_copied"], 1)
                for k in fills[l]:
                    fill(k, kind, i)
            fill(9, kind, i)
            act.wait_ge(S["vn_ps"], n + 1)
            act.activation(vb[:, :, :], pair(2), ACT.Copy).then_inc(S["vn_done"], 1)
            fill(10, kind, i)
            if not (isinstance(n, int) and n == 0):
                act.wait_ge(S["o_kept"], 16 * n)
            act.wait_ge(S["o_ps"], n + 1)
            act.activation(oo[:, :], aux[:, 0, :], ACT.Copy).then_inc(S["o_copied"], 1)
            fill(11, kind, i)

        chunks(act, delta)
        for m in range(FILL // 2, NZ):
            his(HPZ + m, 2)
            z_out(m, 2 * (HPZ + m) + 2)

        def gate_dn(i, m):
            u = m % 2
            his(HPD + 4 * i + m, 2)
            if not (isinstance(i, int) and m < 2):
                act.wait_ge(S[f"sig_kept{u}"], 16 * (2 * i + m // 2))
            act.wait_ge(S["piece_used"], P_D + 8 * i + 2 * m + 2)
            act.activation(halves(sgd[u][:, :]), both(u), ACT.Sigmoid).then_inc(S[f"evacuated{u}"], 1)

        act.wait_ge(S["o_kept"], 16 * NCH)
        act.wait_ge(S["sc_lo"], NSC)
        act.wait_ge(S["s_done"], NCH)
        for u in range(2):
            act.wait_ge(S[f"kept_z{u}"], 16 * NZ // 2)
            act.wait_ge(S[f"half_kept{u}"], 16 * KD // 2)
        act.wait_ge(S["piece_used"], P_Z)

        def gated(i):
            for u in range(2):
                h = 2 * i + u
                act.wait_ge(S[f"go_in{u}"], 32 * i + 32)
                if not isinstance(i, int):
                    act.wait_ge(S["go_scaled"], h - 1)
                act.activation(gq[u][:, :], go[u][:, :], ACT.Square).then_inc(S["go_sq"], 1)
            gate_dn(i, 0)
            for u in range(2):
                act.wait_ge(S["go_ss"], 2 * i + u + 1)
                act.activation(gq[u][:, :], gr[u][:, :], ACT.Sqrt).then_inc(S["go_root"], 1)
            gate_dn(i, 1)
            gate_dn(i, 2)
            for u in range(2):
                act.wait_ge(S["go_scaled"], 2 * i + u + 1)
                act.activation(yh[:, 2 * i + u, :], gt_[u][:, :], ACT.Copy).then_inc(S["go_hi"], 1)
            gate_dn(i, 3)

        peel(act, H // 2, gated)

        def merged_hi(m):
            act.wait_ge(S["merged"], m + 1)
            act.activation(xh[:, m, :], mg[:, m, :], ACT.Copy).then_inc(S["mg_hi"], 1)

        act.wait_ge(S["piece_used"], P_D2)

        def d2(i):
            his(HPD2 + i, 1)
            if not isinstance(i, int):
                merged_hi(2 * i - 1)
            his(HPD2 + i, 1, 1)
            merged_hi(2 * i)

        peel(act, KD // 2, d2)
        merged_hi(KD - 1)

        def e(i):
            his(HPE + 2 * i, 2)
            if not isinstance(i, int):
                act.wait_ge(S["evacuated1"], EV_E[1] + i)
                square(1, 2 * i - 1, 1)
            his(HPE + 2 * i + 1, 2)
            act.wait_ge(S["evacuated0"], EV_E[0] + i + 1)
            square(1, 2 * i, 0)

        peel(act, KD // 2, e)
        act.wait_ge(S["evacuated1"], EV_F[1])
        square(1, KD - 1, 1)
        act.wait_ge(S["piece_used"], P_F)
        norm(1)

        def queries(h):
            for u in range(2):
                his(HPF + 2 * h + u, 2)
                if not isinstance(h, int):
                    act.wait_ge(S["score_ps"], h)
                act.wait_ge(S["piece_used"], P_F + 4 * h + 2 * u + 2)
                act.activation(halves(qh[u][:, :]), both(u), ACT.Copy).then_inc(S[f"evacuated{u}"], 1)

        peel(act, H, queries)

        def plain(k):
            his(HPG + k, 2)
            if k >= 2:
                act.wait_ge(S[f"hid_kept{k % 2}"], 16 * (k // 2))
            act.wait_ge(S["piece_used"], P_G + 2 * k + 2)
            act.activation(halves(gl[k % 2][:, :]), both(k % 2), ACT.Gelu).then_inc(S[f"evacuated{k % 2}"], 1)

        for k in range(PLAIN - 2):
            plain(k)
        act.wait_ge(S["shifted"], H)
        act.activation(gate[:, :, :, :], gate[:, :, :, :], ACT.Exp).then_inc(S["gate_exp"], 1)
        for k in range(PLAIN - 2, PLAIN):
            plain(k)
        act.wait_ge(S["pickT_ps"], 1)
        flat = aux[:, :, :].rearrange("p a b -> p (a b)")
        for x in range(3):
            c = 128 * NBL * x
            act.activation(idxT[x][:, 0:TP], flat[:, c:c + TP], ACT.Copy)
            done = act.activation(idxT[x][:, TP:T], flat[:, c + 128 * NBL - TS:c + 128 * NBL], ACT.Copy)
        done.then_inc(S["pickT_done"], 1)

        def gmats(i):
            for b in range(2):
                if not isinstance(i, int):
                    act.wait_ge(S[f"gates_kept{b}"], 16 * i)
                for r_ in range(UNITS):
                    un = UNITS * b + r_
                    act.wait_ge(S["gmat_ps"], 2 * UNITS * i + un + 1)
                    act.activation(gbuf[b][:, :, 4 * r_:4 * r_ + 4],
                                   aux[:, un % 2, :].rearrange("p (t i) -> p i t", t=4),
                                   ACT.Copy).then_inc(S["gmat_out"], 1)
                    hp = HPG + PLAIN + 2 * i + b
                    if r_ == UNITS // 2 - 1:
                        his(hp, 1)
                    if r_ == UNITS - 1:
                        his(hp, 1, 1)
                        act.wait_ge(S[f"hid_kept{b}"], 16 * i + 16 * PLAIN // 2)
                        act.wait_ge(S["piece_used"], 2 * hp + 2)
                        act.activation(halves(gl[b][:, :]), both(b), ACT.Gelu).then_inc(S[f"evacuated{b}"], 1)

        peel(act, NTB // 2, gmats)

        def hidden(hp, g, par, last=False):
            for k in range(G2):
                q = k % 2
                his(hp + k, 2)
                act.wait_ge(S["piece_used"], 2 * (hp + k) + 2)
                act.wait_ge(S["m_done"], G2 * g + k - 1)
                act.activation(halves(gl[q][:, :]), both(q), ACT.Gelu).then_inc(S[f"evacuated{q}"], 1)
                act.wait_ge(S["m_done"], G2 * g + k + 1)
                act.activation(yh[:, G2 * par + k, :], mm[q][:, :], ACT.Copy).then_inc(S["m_hi"], 1)

        for k in range(G2):
            his(HPU + k, 2)
            if k < 2:
                act.wait_ge(S[f"hid_kept{k}"], 16 * KEPT // 2)
            else:
                act.wait_ge(S["m_done"], k - 1)
            act.wait_ge(S["piece_used"], 2 * (HPU + k) + 2)
            act.activation(halves(gl[k % 2][:, :]), both(k % 2), ACT.Gelu).then_inc(S[f"evacuated{k % 2}"], 1)
            if k == 1:
                for u in range(2):
                    act.wait_ge(S[f"gates_kept{u}"], 16 * NTB // 2)
            for j in {1: (0, 1), 2: (2,), 3: (3,)}.get(k, ()):
                act.wait_ge(S["m_done"], j + 1)
                act.activation(yh[:, j, :], mm[j % 2][:, :], ACT.Copy).then_inc(S["m_hi"], 1)
        for g in range(EARLY - 1):
            for d in range(KD // 2):
                his(HPV + 4 * g, 1, d)
                if d % 2 == 0:
                    k = d // 2
                    act.wait_ge(S["m_done"], G2 * (g + 1) + k + 1)
                    act.activation(yh[:, G2 * ((g + 1) % 2) + k, :], mm[k % 2][:, :], ACT.Copy
                                   ).then_inc(S["m_hi"], 1)

        with act.Fori(0, (NG - EARLY) // 2 - 1) as i:
            for u in range(2):
                hp = HPS + 8 * (2 * i + u)
                hidden(hp, EARLY + 2 * i + u, u)
                his(hp + G2, 8)
        for g in range(NG - 3, NG - 1):
            hp = HPS + 8 * (g + 1 - EARLY)
            hidden(hp, g + 1, (g + 1) % 2)
            his(hp + G2, 8)
        for k in range(KD):
            if k % 2 == 0 and k // 2 < KD // 2 - 2:
                his(HPS + 8 * (NG - EARLY), 1, k // 2)
            act.wait_ge(S[f"evacuated{k % 2}"], EV_END[k % 2] - KD // 2 + k // 2 + 1)
            square(2, k, k % 2)
        norm(2)

    @block.vector
    def _(dve):
        def wait(name, value):
            dve.wait_ge(S[name], value)

        def refined(ss, root, sem, count):
            for ins in (lambda: dve.reciprocal(root, root),
                        lambda: dve.tensor_tensor(ss, ss, root, ALU.mult),
                        lambda: dve.tensor_tensor(ss, ss, root, ALU.mult),
                        lambda: dve.tensor_scalar(ss, ss, -0.5, 1.5, ALU.mult, ALU.add)):
                ins().then_inc(S[sem], 1)
                count = count + 1
                wait(sem, count)

        def norm(c):
            wait("norm_sum", KD * (c + 1))
            dve.tensor_scalar(halves(ms[:, :]), aux[:, 0:2, 0:HT], 1.0 / D, EPS, ALU.mult, ALU.add
                              ).then_inc(S["norm_ms"], 1)
            wait("norm_root", c + 1)
            refined(ms[:, :], rst[:, :], "norm_step", 4 * c)
            dve.tensor_tensor(ms[:, :], ms[:, :], rst[:, :], ALU.mult).then_inc(S["norm_inv"], 1)
            wait("norm_inv", c + 1)
            for k in range(0, KD, 2):
                for u in range(2):
                    if k and c < 2:
                        wait("norm_lo", KD * c + k + u - 1)
                    out = nt[u][:, :] if c < 2 else mg[:, k + u, :]
                    dve.scalar_tensor_tensor(out, mg[:, k + u, :], vector(("g1", "g2", "gf")[c], k + u),
                                             ms[:, :], ALU.mult, ALU.mult).then_inc(S["norm_scaled"], 1)
                if c < 2:
                    for u in range(2):
                        wait("norm_hi", KD * c + k + u + 1)
                        dve.tensor_tensor(xl[:, k + u, :], nt[u][:, :], xh[:, k + u, :].bitcast(F32),
                                          ALU.subtract).then_inc(S["norm_lo"], 1)

        wait("const_in", 32)
        norm(0)
        wait("norm_lo", KD)
        for u in range(2):
            dve.memset(cbuf[u][:, 0:DN_TAPS - 1], 0.0).then_inc(S["pads_set"], 1)

        def conv(m, i, u):
            wait(f"evacuated{u}", i + 1)
            if u < 2 and not (isinstance(m, int) and m < 2):
                wait("silu_done", m - 1)
            w = DN_TAPS - 1
            n = AW - w
            a, _n = VEC["dnw"]
            dve.tensor_scalar(cv[u][:, 0:n], cbuf[u][:, 0:n], vec[:, bass.ds(a + DN_TAPS * m, 1)], None,
                              ALU.mult).then_inc(S["conv_step"], 1)
            for k in range(1, DN_TAPS):
                wait("conv_step", w * m + k)
                dve.scalar_tensor_tensor(cv[u][:, 0:n], cbuf[u][:, k:k + n],
                                         vec[:, bass.ds(a + DN_TAPS * m + k, 1)], cv[u][:, 0:n],
                                         ALU.mult, ALU.add
                                         ).then_inc(S["conv_step"] if k < w else S["conv_done"], 1)

        def l2_sum(m, u, scale):
            wait("l2_sum", m + 1)
            dve.tensor_scalar(halves(ln[u][:, :]), aux[:, 2 * u:2 * u + 2, 0:HT], scale, scale * EPS,
                              ALU.mult, ALU.add).then_inc(S["l2_ss"], 1)

        def l2_scale(m, u):
            wait("l2_root", m + 1)
            refined(ln[u][:, :], lq[u][:, :], "l2_step", 5 * m)
            if not (isinstance(m, int) and m < 2):
                wait(f"kept_qk{u}", 8 * (m - u))
            dve.tensor_tensor(lo_[u][:, :], mg[:, m, :], lq[u][:, :], ALU.mult).then_inc(S["l2_step"], 1)
            wait("l2_step", 5 * m + 5)
            dve.tensor_tensor(lo_[u][:, :], lo_[u][:, :], ln[u][:, :], ALU.mult).then_inc(S["l2_out"], 1)
            wait("l2_out", m + 1)

        def qk_pair(i, scales):
            for u in range(2):
                m = 2 * i + u
                if scales[u]:
                    l2_sum(m - 1, 1 - u, scales[u])
                conv(m, i, u)
                if scales[u]:
                    l2_scale(m - 1, 1 - u)

        Q_SCALE = float(DK)
        qk_pair(0, (None, Q_SCALE))
        qk_pair(1, (Q_SCALE, Q_SCALE))
        with dve.Fori(2, H // 2) as i:
            qk_pair(i, (Q_SCALE, Q_SCALE))
        with dve.Fori(H // 2, H // 2 + 1) as i:
            qk_pair(i, (Q_SCALE, 1.0))
        with dve.Fori(H // 2 + 1, H) as i:
            qk_pair(i, (1.0, 1.0))
        l2_sum(2 * H - 1, 1, 1.0)
        l2_scale(2 * H - 1, 1)
        with dve.Fori(H, NQKV // 2) as i:
            for u in range(2):
                conv(2 * i + u, i, u)

        for u in range(2):
            wait(f"kept_sv{u}", 16 * H // 2)

        sp1, sp2 = small["sp1"][:, :], small["sp2"][:, :]
        for u in range(2):
            wait(f"kept_qk{u}", 16 * H)
        wait("tok_ps", 1)
        wait("beta_done", 1)
        dve.tensor_tensor(heads(sp1, H), raw_tok[:, :, 32:32 + H],
                          vector("dtb")[0:64, :].unsqueeze(1).to_broadcast([64, NCH, H]), ALU.add
                          ).then_inc(S["sp_max"], 1)
        wait("sp_max", 1)
        dve.tensor_scalar(sp2, sp1, -1.0, None, ALU.mult).then_inc(S["sp_max"], 1)
        wait("sp_max", 2)
        dve.tensor_tensor(sp2, sp2, sp1, ALU.max).then_inc(S["sp_in"], 1)
        wait("sp_exp", 1)
        dve.tensor_scalar(sp2, sp2, 1.0, None, ALU.add).then_inc(S["sp_one"], 1)
        wait("sp_ln", 1)
        dve.scalar_tensor_tensor(sp1, sp1, 0.0, sp2, ALU.max, ALU.add).then_inc(S["sp_max"], 1)
        wait("sp_max", 3)
        wait("decay_exp", 1)
        dve.scalar_tensor_tensor(heads(small["gtok"][:, :], H), heads(sp1, H), -1.0,
                                 decay[:, :].unsqueeze(1).to_broadcast([64, NCH, H]), ALU.mult, ALU.mult
                                 ).then_inc(S["g_ready"], 1)
        wait("gc_ps", 1)
        wait("eg_done", 1)
        dve.tensor_copy(small["gcum"][:, :], aux[0:64, 0, 0:NCH * H]).then_inc(S["gcum_done"], 1)
        wait("gcum_done", 1)
        dve.tensor_tensor(small["kdec"][:, :], aux[0:64, 1, 0:NCH * H], small["gcum"][:, :], ALU.subtract
                          ).then_inc(S["kdec_in"], 1)
        dve.tensor_tensor(small["nbeg"][:, :], small["beta"][:, :], small["eg"][:, :], ALU.mult
                          ).then_inc(S["nbeg_done"], 1)
        wait("nbeg_done", 1)
        wait("kdec_done", 1)
        dve.memset(scb[:, 0:SC_TAPS - 1], 0.0).then_inc(S["pads_set"], 1)
        dve.memset(state[:, :, :], 0.0).then_inc(S["pads_set"], 1)
        wait("pads_set", 4)

        def per_token(name, n, width=C):
            return small[name][:, bass.ds(n * H, H)].unsqueeze(2).to_broadcast([64, H, width])

        def per_mask(t):
            return t.unsqueeze(1).to_broadcast([64, H, C])

        def level(l):
            a, _n = CONST["levels"]
            return cst[0:64, a + C * l:a + C * l + C]

        def delta(n, kind, i):
            first = isinstance(n, int) and n == 0
            dve.tensor_tensor(heads(lm[:, :]), per_token("gtok", n), per_mask(const("upper", 64)), ALU.mult
                              ).then_inc(S["gu_done"], 1)
            wait("gcb_ps", n + 1)
            dve.tensor_tensor(heads(pp[:, :]), heads(aux[0:64, 1, :]), per_token("gcum", n), ALU.subtract
                              ).then_inc(S["masked_raw"], 1)
            dve.tensor_tensor(heads(el[:, :]), per_token("gcum", n), heads(aux[0:64, 1, :]), ALU.subtract
                              ).then_inc(S["masked_raw"], 1)
            wait("masked_raw", 2 * n + 2)
            dve.tensor_tensor(heads(pp[:, :]), heads(pp[:, :]), per_mask(const("negT", 64)), ALU.add
                              ).then_inc(S["masked"], 1)
            dve.tensor_tensor(heads(el[:, :]), heads(el[:, :]), per_mask(const("negL", 64)), ALU.add
                              ).then_inc(S["masked"], 1)
            wait("kq_ps", n + 1)
            wait("exp_done", 3 * n + 1)
            dve.tensor_tensor(att[:, :], pp[:, :], aux[0:64, 2, :], ALU.mult).then_inc(S["att_done"], 1)
            wait("exp_done", 3 * n + 2)
            dve.tensor_tensor(ll[:, :], el[:, :], aux[0:64, 0, :], ALU.mult).then_inc(S["l_raw"], 1)
            wait("l_raw", n + 1)
            dve.tensor_tensor(heads(ll[:, :]), heads(ll[:, :]), per_token("beta", n), ALU.mult
                              ).then_inc(S["l_done"], 1)
            wait("l_done", n + 1)
            dve.tensor_tensor(heads(xx[:, :]), heads(ll[:, :]), per_mask(level(0)), ALU.mult
                              ).then_inc(S["x1_in"], 1)
            wait("x1_in", n + 1)
            dve.tensor_tensor(heads(xx[:, :]), per_mask(const("eye", 64)), heads(xx[:, :]), ALU.subtract
                              ).then_inc(S["x1_done"], 1)
            dve.tensor_tensor(heads(lm[:, :]), heads(ll[:, :]), per_mask(level(1)), ALU.mult
                              ).then_inc(S["lm_done"], 1)
            fill(0, kind, i)
            wait("exp_done", 3 * n + 3)
            dve.tensor_tensor(qg[:, :], qkv[:, 0:H, :].rearrange("p h c -> p (h c)"), egb[:, :], ALU.mult
                              ).then_inc(S["qg_done"], 1)
            wait("v_ps", n + 1)
            dve.tensor_tensor(vb[:, :, :], pair(0), per_token("beta", n, 128), ALU.mult
                              ).then_inc(S["vb_done"], 1)
            wait("y1_done", n + 1)
            fill(1, kind, i)
            for l in range(1, LEVELS):
                if l < LEVELS - 1:
                    wait("p_ps", 5 * n + l)
                    dve.tensor_tensor(heads(lm[:, :]), heads(ll[:, :]), per_mask(level(l + 1)), ALU.mult
                                      ).then_inc(S["lm_done"], 1)
                if l == 1:
                    wait("k_ps", n + 1)
                    dve.tensor_tensor(kd[:, :, :], pair(0), per_token("kdec", n, 128), ALU.mult
                                      ).then_inc(S["kd_done"], 1)
                    fill(2, kind, i)
                if l == 3:
                    if not first:
                        wait("s_done", n)
                    if isinstance(n, int) and n == NP1:
                        wait("s_init", 16)
                    dve.tensor_tensor(sdec[:, :, :], state[:, :, :],
                                      egl[:, bass.ds(n * H, H)].unsqueeze(2).to_broadcast([128, H, 128]),
                                      ALU.mult).then_inc(S["sdec_done"], 1)
                    fill(5, kind, i)
                wait("z_ps", 5 * n + l)
                dve.tensor_tensor(yy[:, :], yy[:, :], aux[0:64, 3, :], ALU.subtract).then_inc(S["y_upd"], 1)
                if l < LEVELS - 1:
                    dve.tensor_tensor(xx[:, :], xx[:, :], aux[0:64, 2, :], ALU.subtract).then_inc(S["x_upd"], 1)
                    wait("y_upd", 5 * n + l)
                    wait("x_upd", 4 * n + l)
                fill((3, 4, 6, 7, 8)[l - 1], kind, i)
            wait("ks_ps", n + 1)
            dve.tensor_tensor(rr[:, :, :], pair(0), per_token("nbeg", n, 128), ALU.mult).then_inc(S["r_raw"], 1)
            wait("r_raw", n + 1)
            dve.tensor_tensor(rr[:, :, :], vb[:, :, :], rr[:, :, :], ALU.subtract).then_inc(S["r_done"], 1)
            fill(9, kind, i)
            fill(10, kind, i)
            wait("sup_ps", n + 1)
            wait("sdec_done", n + 1)
            dve.tensor_tensor(state[:, :, :], sdec[:, :, :],
                              aux[:, 2:4, :].rearrange("p a (h n) -> p (a h) n", n=128), ALU.add
                              ).then_inc(S["s_done"], 1)
            fill(11, kind, i)

        def fill(k, kind, i):
            hp = fill_base(kind, i)
            if kind == "B":
                j = 2 * i + k // 6
                if k % 6 == 3:
                    short_conv(j, 2 * hp + k + 1)
                if k % 6 == 5:
                    short_out(j, 2 * hp + k + 1)
                if k in (7, 11):
                    j = 2 * i + k // 8
                    wait("sc_hi", j + 1)
                    dve.tensor_tensor(yl[:, j, :], yt[:, :], yh[:, j, :].bitcast(F32), ALU.subtract
                                      ).then_inc(S["sc_lo"], 1)
            if kind == "C" and k % 3 == 2:
                s = k // 3
                m = 4 * i + s
                wait("evacuated0", EV_C[0] + m + 1)
                if s >= 2:
                    wait(f"half_kept{s % 2}", 16 * (2 * i + s // 2))
                elif isinstance(i, int):
                    wait("sc_lo", NSC)
                else:
                    wait(f"half_kept{s}", 32 * i)
                wait("piece_used", 2 * hp + k + 1)
                dve.tensor_tensor(halves(cm[s % 2][:, :]), halves(csg[s % 2][:, :]), both(1), ALU.mult
                                  ).then_inc(S["evacuated1"], 1)

        def short_conv(j, used):
            w = SC_TAPS - 1
            a, _n = VEC["scst"]
            b, _n = VEC["scw"]
            n = SW - w
            wait("evacuated0", EV_B[0] + 2 * j + 1)
            wait("piece_used", used)
            dve.tensor_copy(scb[:, w + TP:2 * w + TP], vec[:, bass.ds(a + w * j, w)])
            dve.tensor_tensor(scb[:, w:w + HT], ctmp[:, 0:HT], ps[1][:, 0, 0:HT], ALU.mult)
            dve.tensor_tensor(scb[:, w + HT:w + TP], ctmp[:, HT:TP], ps[1][:, 1, 0:TP - HT], ALU.mult)
            dve.tensor_tensor(scb[:, 2 * w + TP:SW], ctmp[:, TP:T], ps[1][:, 1, TP - HT:HT], ALU.mult
                              ).then_inc(S["evacuated1"], 1)
            wait("evacuated1", EV_B[1] + j + 1)
            dve.tensor_copy(sctail[:, j, 0, :], scb[:, TP:TP + w])
            dve.tensor_copy(sctail[:, j, 1, :], scb[:, SW - w:SW])
            dve.tensor_scalar(scv[:, 0:n], scb[:, 0:n], vec[:, bass.ds(b + SC_TAPS * j, 1)], None, ALU.mult
                              ).then_inc(S["sc_step"], 1)
            for k in range(1, SC_TAPS):
                wait("sc_step", SC_TAPS * j + k)
                dve.scalar_tensor_tensor(scv[:, 0:n], scb[:, k:k + n], vec[:, bass.ds(b + SC_TAPS * j + k, 1)],
                                         scv[:, 0:n], ALU.mult, ALU.add).then_inc(S["sc_step"], 1)
            wait("sc_step", SC_TAPS * j + SC_TAPS)

        def short_out(j, used):
            w = SC_TAPS - 1
            if not (isinstance(j, int) and j == 0):
                wait("sc_lo", j)
            wait("piece_used", used)
            dve.tensor_tensor(yt[:, 0:HT], scv[:, 0:HT], ps[0][:, 0, 0:HT], ALU.mult)
            dve.tensor_tensor(yt[:, HT:TP], scv[:, HT:TP], ps[0][:, 1, 0:TP - HT], ALU.mult)
            dve.tensor_tensor(yt[:, TP:T], scv[:, TP + w:T + w], ps[0][:, 1, TP - HT:HT], ALU.mult
                              ).then_inc(S["evacuated0"], 1)

        chunks(dve, delta)

        def gated(i):
            first = isinstance(i, int)
            for u in range(2):
                wait("go_sum", 2 * i + u + 1)
                dve.tensor_scalar(halves(gr[u][:, :]), aux[:, 2 * u:2 * u + 2, 0:HT], 1.0 / 128, EPS,
                                  ALU.mult, ALU.add).then_inc(S["go_ss"], 1)
            for u in range(2):
                h = 2 * i + u
                wait("go_root", h + 1)
                refined(gr[u][:, :], gq[u][:, :], "go_step", 6 * h)
                if not first:
                    wait("go_lo", h - 1)
                dve.tensor_tensor(gt_[u][:, :], go[u][:, :], gq[u][:, :], ALU.mult).then_inc(S["go_step"], 1)
                wait("go_step", 6 * h + 5)
                dve.tensor_tensor(gt_[u][:, :], gt_[u][:, :], gr[u][:, :], ALU.mult).then_inc(S["go_step"], 1)
                wait("go_step", 6 * h + 6)
                dve.scalar_tensor_tensor(gt_[u][:, :], gt_[u][:, :], vector("dng", 0), gz[u][:, :],
                                         ALU.mult, ALU.mult).then_inc(S["go_scaled"], 1)
            for u in range(2):
                h = 2 * i + u
                wait("go_hi", h + 1)
                dve.tensor_tensor(yl[:, h, :], gt_[u][:, :], yh[:, h, :].bitcast(F32), ALU.subtract
                                  ).then_inc(S["go_lo"], 1)

        wait("s_kept", 32)
        wait("o_kept", 16 * NCH)
        peel(dve, H // 2, gated)
        wait("go_lo", H)

        def merged_lo(m):
            wait("mg_hi", m + 1)
            dve.tensor_tensor(xl[:, m, :], mg[:, m, :], xh[:, m, :].bitcast(F32), ALU.subtract
                              ).then_inc(S["mg_lo"], 1)

        def d2(i):
            for u in range(2):
                m = 2 * i + u
                wait(f"hb_in{u}", 32 * i + 32)
                wait("piece_used", P_D2 + m + 1)
                dve.tensor_tensor(halves(dt[u][:, :]), halves(sgr[u][:, :]), both(u), ALU.mult
                                  ).then_inc(S[f"evacuated{u}"], 1)
                wait(f"evacuated{u}", EV_D2[u] + i + 1)
                dve.tensor_tensor(mg[:, m, :], hb[u][:, :], dt[u][:, :], ALU.add).then_inc(S["merged"], 1)
                if not (isinstance(m, int) and m == 0):
                    merged_lo(m - 1)

        peel(dve, KD // 2, d2)
        merged_lo(KD - 1)
        wait("mg_lo", KD)
        with dve.Fori(0, KD // 2) as i:
            for u in range(2):
                wait(f"xr_in{u}", 16 * i + 16)
                wait("piece_used", P_E + 4 * i + 2 * u + 2)
                dve.tensor_tensor(halves(mg[:, 2 * i + u, :]), halves(xr[u][:, :]), both(u), ALU.add
                                  ).then_inc(S[f"evacuated{u}"], 1)
        for u in range(2):
            wait(f"evacuated{u}", EV_F[u])
        norm(1)
        wait("norm_lo", 2 * KD)

        NEGMAX = -3.0e38
        STEPS = 11

        def plain_wait(name, value):
            wait(name, value)
            if not isinstance(value, int):
                dve.sem_inc(S["dve_waited"])

        def topk(h):
            count = [0]

            def step(ins):
                count[0] += 1
                ins.then_inc(S["topk_step"], 1)
                plain_wait("topk_step", STEPS * h + count[0])

            def score(b, s):
                c = (b % 2) * 256 + s * NK
                return aux[:, b // 2, c:c + NK]

            def sums(t, b):
                return t[:, b, :, :].rearrange("p a b -> p (a b)")

            both_ = [(b, s) for b in range(NBL) for s in range(2)]
            plain_wait("score_ps", h + 1)
            for b, s in both_:
                last = dve.max(tv[:, b, s, 0:8], score(b, s))
            step(last)
            for b, s in both_:
                dve.max_index(ti[:, b, s, 0:8], tv[:, b, s, 0:8], score(b, s))
                last = dve.match_replace(mrall[:, b, s, :], tv[:, b, s, 0:8], score(b, s), NEGMAX)
            last.then_inc(S["scores_read"], 1)
            plain_wait("scores_read", h + 1)
            for b, s in both_:
                last = dve.max(tv[:, b, s, 8:16], mrall[:, b, s, :])
            step(last)
            for b, s in both_:
                last = dve.max_index(ti[:, b, s, 8:16], tv[:, b, s, 8:16], mrall[:, b, s, :])
            for b in range(NBL):
                last = dve.tensor_tensor(cand[:, b, :, :], tv[:, b, 0, :].unsqueeze(2).to_broadcast([128, TOPK, TOPK]),
                                         tv[:, b, 1, :].unsqueeze(1).to_broadcast([128, TOPK, TOPK]), ALU.add)
            step(last)
            dve.tensor_copy(tif[:, :, :, :], ti[:, :, :, :])
            for b in range(NBL):
                last = dve.max(best[:, b, 0:8], sums(cand, b))
            step(last)
            for b in range(NBL):
                dve.max_index(posu[:, b, 0:8], best[:, b, 0:8], sums(cand, b))
                last = dve.match_replace(sums(sel, b), best[:, b, 0:8], sums(cand, b), NEGMAX)
            step(last)
            for b in range(NBL):
                last = dve.max(best[:, b, 8:16], sums(sel, b))
            step(last)
            for b in range(NBL):
                last = dve.max_index(posu[:, b, 8:16], best[:, b, 8:16], sums(sel, b))
            step(last)
            dve.tensor_tensor(gate[:, :, h, :], best[:, :, :], best[:, :, 0:1].to_broadcast([128, NBL, TOPK]),
                              ALU.subtract).then_inc(S["shifted"], 1)
            dve.tensor_scalar(posi[0][:, :, :], posu[:, :, :], 4, None, ALU.logical_shift_right)
            step(dve.tensor_scalar(posi[1][:, :, :], posu[:, :, :], TOPK - 1, None, ALU.bitwise_and))
            for s in range(2):
                last = dve.tensor_copy(posf[s][:, :, :], posi[s][:, :, :])
            step(last)
            i16 = const("iota16").unsqueeze(1).to_broadcast([128, NBL * TOPK, TOPK])
            bufs = (sel, sel2)
            for s in range(2):
                last = dve.tensor_tensor(bufs[s][:, :, :, :].rearrange("p b k j -> p (b k) j"), i16,
                                         posf[s][:, :, :].rearrange("p b k -> p (b k)").unsqueeze(2)
                                         .to_broadcast([128, NBL * TOPK, TOPK]), ALU.is_equal)
            step(last)
            for s in range(2):
                last = dve.tensor_tensor(bufs[s][:, :, :, :], bufs[s][:, :, :, :],
                                         tif[:, :, s, :].unsqueeze(2).to_broadcast([128, NBL, TOPK, TOPK]),
                                         ALU.mult)
            step(last)
            for s in range(2):
                last = dve.reduce_sum(pick[s][:, :, h, :], bufs[s][:, :, :, :], AX_X)
            last.then_inc(S["picked"], 1)
            assert count[0] == STEPS, count[0]

        with dve.Fori(0, H) as h:
            topk(h)
        wait("gate_exp", 1)
        gates_all = gate[:, :, :, :].rearrange("p b h k -> p (b h) k")
        dve.reduce_sum(gsum[:, :], gates_all, AX_X).then_inc(S["gsum_step"], 1)
        wait("gsum_step", 1)
        dve.reciprocal(gsum[:, :], gsum[:, :]).then_inc(S["gsum_step"], 1)
        wait("gsum_step", 2)
        dve.tensor_tensor(gates_all, gates_all, gsum[:, :].unsqueeze(2).to_broadcast([128, NBL * H, TOPK]),
                          ALU.mult).then_inc(S["pick_done"], 1)

        wait("pickT_done", 1)

        def onehots(i):
            for u in range(2):
                if not isinstance(i, int):
                    wait("gmat_ps", 2 * i + u - 1)
                for c in range(4):
                    t = bass.ds(8 * i + 4 * u + c, 1)
                    dve.tensor_scalar(oa[u][:, c, :], const("iota"), idxT[0][:, t], idxT[2][:, t],
                                      ALU.is_equal, ALU.mult)
                    last = dve.tensor_scalar(ob[u][:, c, :], const("iota"), idxT[1][:, t], None, ALU.is_equal)
                last.then_inc(S["onehots"], 1)

        peel(dve, T // 8, onehots)
        for u in range(2):
            wait(f"gates_kept{u}", 16 * NTB // 2)

        def gated(g, par, k):
            q = k % 2
            if not (isinstance(g, int) and g == 0 and k < 2):
                wait("m_lo", G2 * g + k - 1)
            dve.tensor_tensor(mm[q][:, :].rearrange("p (a t) -> p a t", t=TB),
                              gl[q][:, :].rearrange("p (a t) -> p a t", t=TB),
                              gtile[par][:, :, k, :], ALU.mult).then_inc(S["m_done"], 1)

        def gated_low(g, par, k):
            wait("m_hi", G2 * g + k + 1)
            dve.tensor_tensor(yl[:, G2 * par + k, :], mm[k % 2][:, :], yh[:, G2 * par + k, :].bitcast(F32),
                              ALU.subtract).then_inc(S["m_lo"], 1)

        def hidden(g, gi, par):
            wait(f"gt_in{par}", 16 * (EARLY // 2) + 16 * gi + 16)
            for k in range(G2):
                wait(f"evacuated{k % 2}", EV_S[k % 2] + PER_G * (g - EARLY) + k // 2 + 1)
                gated(g, par, k)
                gated_low(g, par, k)

        def collect(hp, g, low=lambda d: None, high=lambda d: None):
            for d in range(KD // 2):
                wait("group_done", (KD // 2) * g + d + 1)
                dve.tensor_tensor(halves(mg[:, 2 * d, :]), halves(mg[:, 2 * d, :]), both(0), ALU.add
                                  ).then_inc(S["evacuated0"], 1)
                low(d)
                wait("piece_used", 2 * hp + d + 1)
                dve.tensor_tensor(halves(mg[:, 2 * d + 1, :]), halves(mg[:, 2 * d + 1, :]), both(1), ALU.add
                                  ).then_inc(S["evacuated1"], 1)
                high(d)

        def kept_high(g):
            def high(d):
                k = d // 2
                if d % 2 == 0:
                    wait(f"gt_in{g % 2}", 16 * (g // 2 + 1))
                    wait(f"gl_in{k % 2}", 16 * ((G2 * (g - 1) + k) // 2 + 1))
                    gated(g, g % 2, k)
            return high

        def kept_low(g):
            return lambda d: gated_low(g, g % 2, d // 2) if d % 2 else None

        wait("gt_in0", 16)
        for k in range(G2):
            wait(f"evacuated{k % 2}", EV_U[k % 2] + k // 2 + 1)
            gated(0, 0, k)
            gated_low(0, 0, k)
        for g in range(EARLY - 1):
            collect(HPV + 4 * g, g, kept_low(g + 1), kept_high(g + 1))
        with dve.Fori(0, (NG - EARLY) // 2 - 1) as i:
            for u in range(2):
                hidden(EARLY + 2 * i + u, i, u)
                collect(HPS + 8 * (2 * i + u) + G2, EARLY - 1 + 2 * i + u)
        for g in range(NG - 3, NG - 1):
            hidden(g + 1, (NG - EARLY) // 2 - 1, (g + 1) % 2)
            collect(HPS + 8 * (g + 1 - EARLY) + G2, g)
        collect(HPS + 8 * (NG - EARLY), NG - 1)
        for u in range(2):
            wait(f"evacuated{u}", EV_END[u])
        norm(2)

    @block.tensor
    def _(pe):
        def piece(hp, c, slot, high, low, k0, first, last, tiles_=range(NPIECE), done=("piece_used",),
                  between=lambda t: None, ready=None):
            w = c % 2
            for t in tiles_:
                if ready:
                    ready(k0 + t)
                for half in range(2):
                    cols = slice(half * HT, (half + 1) * HT)
                    k = k0 + t - tiles_[0]
                    for x, (a, b) in enumerate(((wh, high), (wh, low), (wl, high))):
                        mm_ = pe.matmul(ps[slot][:, half, 0:HT], a[w][:, t, :], b[:, k, cols],
                                        start=first and t == tiles_[0] and x == 0,
                                        stop=last and t == tiles_[-1] and x == 2)
                if t < tiles_[-1]:
                    between(t)
            mm_.then_inc(S[done[0]], 1)

        def product(hp, c0, slot, ev, high, low, n, ready=None):
            if not (isinstance(ev, int) and ev == 0):
                pe.wait_ge(S[f"evacuated{slot}"], ev)
            for c in range(n):
                pe.wait_ge(S["lo_done"], 2 * hp + c0 + c + 1)
                piece(hp, c0 + c, slot, high, low, NPIECE * c, c == 0, c == n - 1, ready=ready)

        def norm_sum(c, k, u, start=False, stop=False):
            pe.wait_ge(S["norm_sq"], KD * c + k + 1)
            for half in range(2):
                last = pe.matmul(aux[:, half, 0:HT], const("ones"), sq[u][:, half * HT:(half + 1) * HT],
                                 start=start, stop=stop)
            last.then_inc(S["norm_sum"], 1)

        def chunk_ready(c):
            return lambda k: pe.wait_ge(S["norm_lo"], KD * c + k + 1)

        pe.wait_ge(S["const_in"], 32)
        for k in range(KD):
            norm_sum(0, k, k % 2, k == 0, k == KD - 1)

        def l2_sum(m, u):
            pe.wait_ge(S["l2_sq"], m + 1)
            if not (isinstance(m, int) and m < 2):
                pe.wait_ge(S["l2_ss"], m - 1)
            for half in range(2):
                last = pe.matmul(aux[:, 2 * u + half, 0:HT], const("ones"),
                                 lq[u][:, half * HT:(half + 1) * HT], start=True, stop=True)
            last.then_inc(S["l2_sum"], 1)

        def qk_pair(i):
            first = isinstance(i, int) and i == 0
            product(HPA + 2 * i, 0, 0, i, xh, xl, 2, chunk_ready(0) if first else None)
            if not first:
                l2_sum(2 * i - 1, 1)
            product(HPA + 2 * i + 1, 0, 1, i, xh, xl, 2)
            l2_sum(2 * i, 0)

        qk_pair(0)
        qk_pair(1)
        with pe.Fori(2, H) as i:
            qk_pair(i)
        l2_sum(2 * H - 1, 1)
        with pe.Fori(H, N_A // 2) as i:
            for u in range(2):
                product(HPA + 2 * i + u, 0, u, i, xh, xl, 2)
        product(HPA + N_A - 1, 0, 0, N_A // 2, xh, xl, 2)

        pe.wait_ge(S["evacuated0"], EV_B[0])
        pe.wait_ge(S["l2_ss"], 2 * H)
        for n in range(NCH):
            last = pe.transpose(raw_flat[:, n * C:(n + 1) * C], bar[0:64, n * C:(n + 1) * C],
                                const("ident", 64)[:, 0:64])
        last.then_inc(S["tok_ps"], 1)
        pe.wait_ge(S["g_ready"], 1)
        pe.matmul(aux[0:64, 0, 0:NCH * H], const("upper", 64), small["gtok"][:, :], start=True, stop=True)
        pe.matmul(aux[:, 1, 0:NCH * H], const("ones", 64), small["gtok"][:, :], start=True, stop=True
                  ).then_inc(S["gc_ps"], 1)
        pe.wait_ge(S["kdec_in"], 1)
        pe.wait_ge(S["eg_done"], 1)

        def pe_wait(sem, value):
            pe.wait_ge(sem, value)
            if not isinstance(value, int):
                pe.sem_inc(S["pe_waited"])

        def fill(k, kind, i):
            hp = fill_base(kind, i)
            if kind == "B":
                j, group, part = 2 * i + k // 6, k % 6 // 2, k % 2
                slot = group % 2
                ev = (EV_B[0] + 2 * j, EV_B[1] + j, EV_B[0] + 2 * j + 1)[group]
                data, n = (xh, xl), 2
            elif kind == "C":
                m, part = 4 * i + k // 3, k % 3 % 2
                slot = k % 3 // 2
                ev = EV_C[slot] + m
                data, n = ((xh, xl), 2) if slot == 0 else ((yh, yl), 1)
            else:
                slot, part = k // 2 % 2, k % 2
                ev = EV_Z[slot] + k // 4
                data, n = (xh, xl), 2
            if part == 0:
                pe.wait_ge(S[f"evacuated{slot}"], ev)
            if kind == "C" and k == 2:
                pe.wait_ge(S["sc_lo"], NSC)
            pe.wait_ge(S["lo_done"], 2 * hp + k + 1)
            piece(hp, k, slot, *data, NPIECE * part, part == 0, part == n - 1)

        def delta(n, kind, i):
            first = isinstance(n, int) and n == 0

            def per_head(out, left, right, start=True, stop=True):
                for h in range(H):
                    last = pe.matmul(out(h), left(h), right(h), start=start, stop=stop)
                return last

            q_h = lambda h: qkv[:, h, :]
            k_h = lambda h: qkv[:, H + h, :]
            v_h = lambda h: qkv[:, 2 * H + h, :]
            sq_h = lambda t: (lambda h: t[:, h * C:(h + 1) * C])
            bank = lambda b, rows=64: (lambda h: aux[0:rows, b, h * C:(h + 1) * C])
            wide = lambda b, rows=64: (lambda h: aux[0:rows, b + h // 4, (h % 4) * 128:(h % 4 + 1) * 128])
            pe_wait(S["gu_done"], n + 1)
            if not first:
                pe_wait(S["r_done"], n)
            pe.matmul(aux[:, 1, :], const("ones", 64), lm[:, :], start=True, stop=True).then_inc(S["gcb_ps"], 1)
            pe_wait(S["chunk_in"], 16 * n + 16)
            if not first:
                pe_wait(S["s_done"], n)
                pe_wait(S["o_copied"], n)
            per_head(bank(2), k_h, q_h)
            per_head(bank(0), k_h, k_h).then_inc(S["kq_ps"], 1)
            fill(0, kind, i)
            pe_wait(S["x1_done"], n + 1)
            for h in range(H):
                last = pe.transpose(aux[0:64, 3, h * C:(h + 1) * C], xx[:, h * C:(h + 1) * C],
                                    const("ident", 64)[:, 0:64])
            last.then_inc(S["xt_ps"], 1)
            pe_wait(S["exp_done"], 3 * n + 3)
            for h in range(H):
                last = pe.transpose(wide(0)(h), v_h(h), const("ident"))
            last.then_inc(S["v_ps"], 1)
            fill(1, kind, i)
            pe_wait(S["att_done"], n + 1)
            for l in range(1, LEVELS):
                if l == 1:
                    pe_wait(S["y1_done"], n + 1)
                else:
                    pe_wait(S["y_upd"], 5 * n + l - 1)
                    pe_wait(S["x_upd"], 4 * n + l - 1)
                pe_wait(S["lm_done"], 5 * n + l)
                per_head(bank(2), sq_h(lm), sq_h(yy)).then_inc(S["p_ps"], 1)
                if l == 1:
                    pe_wait(S["vb_done"], n + 1)
                    for h in range(H):
                        last = pe.transpose(wide(0)(h), k_h(h), const("ident"))
                    last.then_inc(S["k_ps"], 1)
                    fill(2, kind, i)
                if l == 3:
                    fill(5, kind, i)
                pe_wait(S["p_copied"], 5 * n + l)
                last = per_head(bank(3), sq_h(xx), sq_h(pp))
                if l < LEVELS - 1:
                    last = per_head(bank(2), sq_h(pp), sq_h(xx))
                last.then_inc(S["z_ps"], 1)
                fill((3, 4, 6, 7, 8)[l - 1], kind, i)
            if isinstance(n, int) and n == NP1:
                pe_wait(S["s_init"], 16)
            if first:
                pe_wait(S["pads_set"], 4)
            pe_wait(S["kd_done"], n + 1)
            per_head(wide(0), k_h, lambda h: state[:, h, :]).then_inc(S["ks_ps"], 1)
            fill(9, kind, i)
            pe_wait(S["r_done"], n + 1)
            pe_wait(S["y_upd"], 5 * n + 5)
            per_head(wide(2), sq_h(yy), lambda h: rr[:, h, :]).then_inc(S["vn_ps"], 1)
            fill(10, kind, i)
            pe_wait(S["vn_done"], n + 1)
            pe_wait(S["qg_done"], n + 1)
            for h in range(H):
                pe.matmul(bank(0, 128)(h), state[:, h, :], qg[:, h * C:(h + 1) * C], start=True, stop=False)
                last = pe.matmul(bank(0, 128)(h), vb[:, h, :], att[:, h * C:(h + 1) * C], start=False, stop=True)
            last.then_inc(S["o_ps"], 1)
            per_head(wide(2, 128), lambda h: kd[:, h, :], lambda h: vb[:, h, :]).then_inc(S["sup_ps"], 1)
            fill(11, kind, i)

        chunks(pe, delta)
        for m in range(FILL // 2, NZ):
            product(HPZ + m, 0, m % 2, EV_Z[m % 2] + m // 2, xh, xl, 2)

        pe.wait_ge(S["s_done"], NCH)
        pe.wait_ge(S["o_copied"], NCH)

        def gated(i):
            for u in range(2):
                h = 2 * i + u
                pe.wait_ge(S["go_sq"], h + 1)
                if not isinstance(i, int):
                    pe.wait_ge(S["go_ss"], h - 1)
                for half in range(2):
                    last = pe.matmul(aux[:, 2 * u + half, 0:HT], const("ones"),
                                     gq[u][:, half * HT:(half + 1) * HT], start=True, stop=True)
                last.then_inc(S["go_sum"], 1)
            for m in range(4):
                product(HPD + 4 * i + m, 0, m % 2, EV_D[m % 2] + 2 * i + m // 2, xh, xl, 2)

        peel(pe, H // 2, gated)
        pe.wait_ge(S["go_lo"], H)
        with pe.Fori(0, KD // 2) as i:
            for u in range(2):
                product(HPD2 + i, u, u, EV_D2[u] + i, yh, yl, 1)
        pe.wait_ge(S["mg_lo"], KD)

        def e(i):
            first = isinstance(i, int)
            product(HPE + 2 * i, 0, 0, EV_E[0] + i, xh, xl, 2)
            if not first:
                norm_sum(1, 2 * i - 1, 1)
            product(HPE + 2 * i + 1, 0, 1, EV_E[1] + i, xh, xl, 2)
            norm_sum(1, 2 * i, 0, start=first)

        peel(pe, KD // 2, e)
        norm_sum(1, KD - 1, 1, stop=True)

        def queries(h):
            for u in range(2):
                product(HPF + 2 * h + u, 0, u, EV_F[u] + h, xh, xl, 2,
                        chunk_ready(1) if isinstance(h, int) and u == 0 else None)
            for u in range(2):
                pe.wait_ge(S[f"evacuated{u}"], EV_F[u] + h + 1)
            if not isinstance(h, int):
                pe.wait_ge(S["scores_read"], h)
            for b, t0 in enumerate(BLOCKS):
                for u in range(2):
                    c = (b % 2) * 256 + u * NK
                    last = pe.matmul(aux[:, b // 2, c:c + NK], qh[u][:, t0:t0 + 128], keys[:, 2 * h + u, :],
                                     start=True, stop=True)
            last.then_inc(S["score_ps"], 1)

        pe.wait_ge(S["keys_in"], 16)
        peel(pe, H, queries)

        def turn():
            pe.wait_ge(S["pick_done"], 1)
            flat = aux[:, :, :].rearrange("p a b -> p (a b)")
            for x, t in enumerate((pick[0], pick[1], gate)):
                for b in range(NBL):
                    c = 128 * (NBL * x + b)
                    last = pe.transpose(flat[:, c:c + 128], t[:, b, :, :].rearrange("p h k -> p (h k)"),
                                        const("ident"))
            last.then_inc(S["pickT_ps"], 1)

        def gmats(i):
            for b in range(2):
                hp = HPG + PLAIN + 2 * i + b

                def unit(r_):
                    un = UNITS * b + r_
                    u = un % 2
                    pe.wait_ge(S["onehots"], 2 * UNITS * i + un + 1)
                    if not (isinstance(i, int) and un < 2):
                        pe.wait_ge(S["gmat_out"], 2 * UNITS * i + un - 1)
                    for c in range(4):
                        last = pe.matmul(aux[:, u, c * NK:(c + 1) * NK], oa[u][:, c, :], ob[u][:, c, :],
                                         start=True, stop=True)
                    last.then_inc(S["gmat_ps"], 1)

                pe.wait_ge(S[f"evacuated{b}"], EV_G[b] + PLAIN // 2 + i)
                for c in range(2):
                    pe.wait_ge(S["lo_done"], 2 * hp + c + 1)
                    piece(hp, c, b, xh, xl, NPIECE * c, c == 0, c == 1,
                          between=lambda t: unit(6 * c + AFTER.index(t)) if t in AFTER else None)
                    unit(6 * c + 5)

        for k in range(PLAIN):
            product(HPG + k, 0, k % 2, EV_G[k % 2] + k // 2, xh, xl, 2)
        turn()
        pe.wait_ge(S["pickT_done"], 1)
        peel(pe, NTB // 2, gmats)

        def hidden(hp, ev0, ev1):
            for k in range(G2):
                product(hp + k, 0, k % 2, (ev0, ev1)[k % 2] + k // 2, xh, xl, 2)

        def values(hp, g, par, ev, after=lambda d: None):
            pe.wait_ge(S["m_lo"], G2 * g + G2)
            for d in range(KD // 2):
                pe.wait_ge(S["lo_done"], 2 * hp + d + 1)
                for x in range(2):
                    pe.wait_ge(S[f"evacuated{x}"], ev[x] + d)
                    piece(hp, d, x, yh, yl, G2 * par, True, True, range(G2 * x, G2 * x + G2),
                          ("group_done", "piece_used")[x:])
                after(d)

        hidden(HPU, EV_U[0], EV_U[1])
        for g in range(EARLY - 1):
            values(HPV + 4 * g, g, g % 2, [e + g * KD // 2 for e in EV_V])

        def step(g, hp, par):
            base = [e + PER_G * (g - EARLY + 1) for e in EV_S]
            hidden(hp, base[0], base[1])
            values(hp + G2, g, par, [e + G2 // 2 for e in base])

        with pe.Fori(0, (NG - EARLY) // 2) as i:
            for u in range(2):
                step(EARLY - 1 + 2 * i + u, HPS + 8 * (2 * i + u), 1 - u)

        def last_sums(d):
            for k in (2 * d - 2, 2 * d - 1):
                if k >= 0:
                    norm_sum(2, k, k % 2, k == 0, k == KD - 1)

        values(HPS + 8 * (NG - EARLY), NG - 1, 1, [e - KD // 2 for e in EV_END], last_sums)
        last_sums(KD // 2)

    block_context.__exit__(None, None, None)


def constants():
    t = np.zeros((128, N_CONST), np.float32)

    def put(name, value):
        a, n = CONST[name]
        t[0:value.shape[0], a:a + n] = value

    i, j = np.arange(C)[:, None], np.arange(C)[None, :]
    put("ones", np.ones((128, 128), np.float32))
    put("ident", np.eye(128, dtype=np.float32))
    put("iota", np.broadcast_to(np.arange(128, dtype=np.float32), (128, 128)))
    put("upper", (i <= j).astype(np.float32))
    put("negT", np.where(j >= i, 0.0, NEG).astype(np.float32))
    put("negL", np.where(j < i, 0.0, NEG).astype(np.float32))
    put("eye", np.eye(C, dtype=np.float32))
    put("levels", np.concatenate([((i >> (l + 1)) == (j >> (l + 1))) & ((i >> l) % 2 == 1) & ((j >> l) % 2 == 0)
                                  for l in range(LEVELS)], axis=1).astype(np.float32))
    put("iota16", np.broadcast_to(np.arange(TOPK, dtype=np.float32), (128, TOPK)))
    return t


def pieces(w):
    k, m = w.shape
    return w.reshape(k // 1024, NPIECE, 128, m // 128, 128).transpose(3, 0, 2, 1, 4).reshape(-1, 128, 1024)


def kernel(x_prompt, x_sample, state_dn, state_dn_conv, state_sc_conv, norm1_g, w_in, sc_conv_w, dn_conv_w,
           dn_a_log, dn_dt_bias, dn_norm_g, w_br_sc, w_br_dn, w_o, norm2_g, peer_wq, peer_keys, peer_u,
           peer_v, final_norm_g):
    import concourse.bacc as bacc
    from concourse.bass_utils import run_bass_kernel_spmd

    f = {n: np.asarray(a) for n, a in dict(
        x_prompt=x_prompt, x_sample=x_sample, state_dn=state_dn, state_dn_conv=state_dn_conv,
        state_sc_conv=state_sc_conv, norm1_g=norm1_g, w_in=w_in, sc_conv_w=sc_conv_w, dn_conv_w=dn_conv_w,
        dn_a_log=dn_a_log, dn_dt_bias=dn_dt_bias, dn_norm_g=dn_norm_g, w_br_sc=w_br_sc, w_br_dn=w_br_dn,
        w_o=w_o, norm2_g=norm2_g, peer_wq=peer_wq, peer_keys=peer_keys, peer_u=peer_u, peer_v=peer_v,
        final_norm_g=final_norm_g).items()}
    x = np.concatenate([f["x_prompt"][0], f["x_sample"][0]], axis=0)
    x = np.ascontiguousarray(x.T.reshape(KD, 128, T).transpose(1, 0, 2))

    w = f["w_in"][0]
    edges = np.cumsum((0, SCW, SCW, SCW, QKV, 1024, H, H, D, D))
    sc_b, sc_c, sc_h, qkv_w, z_w, beta_w, a_w, gsc_w, gdn_w = (w[:, a:b] for a, b in zip(edges, edges[1:]))
    ba = np.zeros((D, 128), np.float32)
    ba[:, 0:H] = beta_w
    ba[:, 32:32 + H] = a_w
    stream = [pieces(qkv_w), pieces(ba)]
    stream.append(np.stack([pieces(m).reshape(NSC, 2, 128, 1024) for m in (sc_c, sc_h, sc_b)], axis=1
                           ).reshape(-1, 128, 1024))
    stream.append(np.concatenate([pieces(gsc_w).reshape(KD, 2, 128, 1024),
                                  pieces(f["w_br_sc"][0]).reshape(KD, 1, 128, 1024)], axis=1
                                 ).reshape(-1, 128, 1024))
    stream += [pieces(z_w), pieces(gdn_w), pieces(f["w_br_dn"][0])]
    stream += [pieces(f["w_o"][0]), pieces(f["peer_wq"][0])]
    u = f["peer_u"][0].reshape(NK, NG, G2, 2, NPIECE, 128).transpose(1, 2, 3, 5, 4, 0).reshape(NG, 2 * G2, 128, 1024)
    v = f["peer_v"][0].reshape(NK, NG, G2, KD // 2, 2, 128).transpose(1, 3, 0, 4, 2, 5).reshape(
        NG, KD // 2, 128, 1024)
    stream += [u[g] for g in range(1, EARLY)] + [u[0]] + [v[g] for g in range(EARLY - 1)]
    for g in range(EARLY - 1, NG - 1):
        stream += [u[g + 1], v[g]]
    stream.append(v[NG - 1])
    stream = np.concatenate(stream, axis=0)
    assert stream.shape == (N_PIECES, 128, 1024)

    vec = np.zeros((128, N_VEC), np.float32)

    def put(name, value):
        a, n = VEC[name]
        vec[:, a:a + n] = value

    def columns(a, n):
        return a.reshape(a.shape[0], n, 128).transpose(2, 1, 0).reshape(128, -1)

    put("g1", columns(f["norm1_g"], KD))
    put("g2", columns(f["norm2_g"], KD))
    put("gf", columns(f["final_norm_g"][None], KD))
    put("dnw", columns(f["dn_conv_w"][0], NQKV))
    put("scw", columns(f["sc_conv_w"][0], NSC))
    put("dng", f["dn_norm_g"][0][:, None])
    put("alog", np.broadcast_to(f["dn_a_log"][0], (128, H)))
    put("dtb", np.broadcast_to(f["dn_dt_bias"][0], (128, H)))
    put("dnst", columns(f["state_dn_conv"][0, 0], NQKV))
    put("scst", columns(f["state_sc_conv"][0, 0], NSC))
    arrays = {
        "x": x, "w": stream, "vec": vec, "const": constants(),
        "s0": np.ascontiguousarray(f["state_dn"][0, 0].transpose(1, 0, 2)),
        "keys": np.ascontiguousarray(f["peer_keys"][0].reshape(KD, NK, 128).transpose(2, 0, 1)),
    }
    outs = {"y": (128, KD, T), "sp": (128, H, 128), "ss": (128, H, 128),
            "dnc": (128, NQKV, 2, DN_TAPS - 1), "scc": (128, NSC, 2, SC_TAPS - 1)}
    scratch = {"qkv_s": (NCH, 128, NQKV, C), "z_s": (NZ, 128, T), "o_s": (NCH, 128, HC),
               "half_s": (KD, 128, T), "sig_s": (KD, 128, T),
               "gates_s": (NG, 128, NTB, G2 * TB), "hid_s": (KEPT, 128, T)}

    nc = bacc.Bacc("TRN2", target_bir_lowering=False, num_devices=1)
    args = [nc.dram_tensor(f"in_{n}", a.shape, F32, kind="ExternalInput").ap() for n, a in arrays.items()]
    args += [nc.dram_tensor(f"out_{n}", s, F32, kind="ExternalOutput").ap() for n, s in outs.items()]
    args += [nc.dram_tensor(n, s, F32, kind="Internal").ap() for n, s in scratch.items()]
    trunk_program(nc, *args)
    r = run_bass_kernel_spmd(nc, [{f"in_{n}": a for n, a in arrays.items()}], core_ids=[0]).results[0]

    y = r["out_y"].transpose(2, 1, 0).reshape(T, D)
    dn = [r[f"out_{n}"].transpose(1, 0, 2)[None, None] for n in ("sp", "ss")]
    dnc = r["out_dnc"].transpose(2, 3, 1, 0).reshape(2, DN_TAPS - 1, QKV)
    scc = r["out_scc"].transpose(2, 3, 1, 0).reshape(2, SC_TAPS - 1, SCW)
    out = (y[None, 0:TP], y[None, TP:], dn[0], dnc[None, None, 0], scc[None, None, 0],
           dn[1], dnc[None, None, 1], scc[None, None, 1])
    return tuple(np.ascontiguousarray(a) for a in out)
```
